# Optimizing a Trainium2 kernel written in Bass

```python
import math
import jax, jax.numpy as jnp
from jax import lax
import numpy as np
import jax
import jax.numpy as jnp

D_MODEL = 1024
BATCH = 1
SEQ = 256
DEPTH = 1

HEAD_DIM = 64
MIX_WIDTH = D_MODEL
ATTN_HEADS = 6
ATTN_KV_HEADS = 2
ATTN_GROUP = ATTN_HEADS // ATTN_KV_HEADS
ATTN_WIDTH = ATTN_HEADS * HEAD_DIM
ATTN_KV_WIDTH = ATTN_KV_HEADS * HEAD_DIM
WINDOW = 128
BLOCK_Q = 128
N_BUCKETS = 32
MAX_EXACT = N_BUCKETS // 2
MAX_DISTANCE = WINDOW
RWKV_HEADS = 6
RWKV_HEAD_DIM = 64
RWKV_WIDTH = RWKV_HEADS * RWKV_HEAD_DIM
D_DECAY_LORA = 32
D_AAA_LORA = 32
D_MV_LORA = 16
D_GATE_LORA = 64
RWKV_SHIFT_COLS = 3 * RWKV_WIDTH + D_DECAY_LORA + D_AAA_LORA + D_GATE_LORA
MEM_TOKENS = 256
MEM_HEADS = 4
MEM_WIDTH = MIX_WIDTH - ATTN_WIDTH - RWKV_WIDTH
IN_BASE = ATTN_WIDTH + 2 * ATTN_KV_WIDTH + RWKV_SHIFT_COLS + MEM_WIDTH
D_FF = 2816
CONV_WIDTH = 3
EPS = 1e-6
GN_EPS = 64e-5
L2_EPS = 1e-12


def split_cols(t, sizes):
    return jnp.split(t, [int(c) for c in np.cumsum(sizes)[:-1]], axis=-1)

def rms_norm(x, g):
    xf = x.astype(jnp.float32)
    y = xf * lax.rsqrt(jnp.mean(xf * xf, axis=-1, keepdims=True) + EPS)
    return (y * g.astype(jnp.float32)).astype(x.dtype)

def token_shift(p, mu):
    prev = jnp.pad(p, ((0, 0), (1, 0), (0, 0)))[:, :-1]
    return p + mu * (prev - p)

def t5_causal_bucket(dist):
    is_small = dist < MAX_EXACT
    d = jnp.maximum(dist, 1).astype(jnp.float32)
    large = MAX_EXACT + (jnp.log(d / MAX_EXACT) / math.log(MAX_DISTANCE / MAX_EXACT)
                         * (N_BUCKETS - MAX_EXACT)).astype(jnp.int32)
    large = jnp.minimum(large, N_BUCKETS - 1)
    return jnp.where(is_small, dist, large)

def sliding_window_attention(q, k, v, sinks, rel_bias):
    b, s = q.shape[0], q.shape[1]
    nb = s // BLOCK_Q
    qb = q.reshape(b, nb, BLOCK_Q, ATTN_KV_HEADS, ATTN_GROUP, HEAD_DIM)

    def band(t):
        tb = t.reshape(b, nb, BLOCK_Q, ATTN_KV_HEADS, HEAD_DIM)
        prev = jnp.concatenate([jnp.zeros_like(tb[:, :1]), tb[:, :-1]], axis=1)
        return jnp.concatenate([prev, tb], axis=2)

    kw, vw = band(k), band(v)
    logits = jnp.einsum('bnqhgd,bnkhd->bnhgqk', qb, kw,
                        preferred_element_type=jnp.float32) * (HEAD_DIM ** -0.5)
    qi = jnp.arange(BLOCK_Q)[:, None]
    kj = jnp.arange(2 * BLOCK_Q)[None, :]
    dist = qi + BLOCK_Q - kj
    in_band = (dist >= 0) & (dist < WINDOW)
    key_pos = jnp.arange(nb)[:, None, None] * BLOCK_Q - BLOCK_Q + kj[None]
    valid = in_band[None] & (key_pos >= 0)
    bucket = t5_causal_bucket(jnp.maximum(dist, 0))
    bias = rel_bias.astype(jnp.float32)[bucket]
    bias = bias.transpose(2, 0, 1).reshape(ATTN_KV_HEADS, ATTN_GROUP, BLOCK_Q, 2 * BLOCK_Q)
    logits = jnp.where(valid[None, :, None, None], logits + bias, -jnp.inf)
    sink = sinks.astype(jnp.float32).reshape(ATTN_KV_HEADS, ATTN_GROUP)[None, None, :, :, None, None]
    m = jnp.maximum(jnp.max(logits, axis=-1, keepdims=True), sink)
    e = jnp.exp(logits - m)
    p = e / (jnp.sum(e, axis=-1, keepdims=True) + jnp.exp(sink - m))
    out = jnp.einsum('bnhgqk,bnkhd->bnqhgd', p.astype(v.dtype), vw)
    return out.reshape(b, s, ATTN_WIDTH)

def rwkv7_scan(r, w, k, v, a, bvec):
    bsz = r.shape[0]
    decay = jnp.exp(-jnp.exp(w))

    def step(state, inp):
        r_t, d_t, k_t, v_t, a_t, b_t = inp
        sa = jnp.einsum('bhvk,bhk->bhv', state, a_t)
        state = (state * d_t[:, :, None, :] + sa[..., None] * b_t[:, :, None, :]
                 + v_t[..., None] * k_t[:, :, None, :])
        return state, jnp.einsum('bhvk,bhk->bhv', state, r_t)

    xs = tuple(jnp.moveaxis(t, 1, 0) for t in (r, decay, k, v, a, bvec))
    s0 = jnp.zeros((bsz, RWKV_HEADS, RWKV_HEAD_DIM, RWKV_HEAD_DIM), jnp.float32)
    _, y = lax.scan(step, s0, xs)
    return jnp.moveaxis(y, 0, 1)

def rwkv7_mixer(pb, value_residual, w0, w2, a0, a2, g2, k_k, k_a, r_k, ln_w, ln_b):
    out_dtype = pb.dtype
    f32 = lambda t: t.astype(jnp.float32)
    r, k, v, wd, ad, gd = split_cols(f32(pb), [RWKV_WIDTH, RWKV_WIDTH, RWKV_WIDTH,
                                               D_DECAY_LORA, D_AAA_LORA, D_GATE_LORA])
    w = -jax.nn.softplus(-(f32(w0) + jnp.tanh(wd) @ f32(w2))) - 0.5
    a = jax.nn.sigmoid(f32(a0) + ad @ f32(a2))
    g = jax.nn.sigmoid(gd) @ f32(g2)
    if value_residual is not None:
        v_first, v_down, v0, v2 = value_residual
        v = v + (f32(v_first) - v) * jax.nn.sigmoid(f32(v0) + f32(v_down) @ f32(v2))
    v_out = v
    b, s = pb.shape[0], pb.shape[1]
    heads = lambda t: t.reshape(b, s, RWKV_HEADS, RWKV_HEAD_DIM)
    kk = heads(k * f32(k_k))
    kk = kk / jnp.maximum(jnp.sqrt(jnp.sum(kk * kk, axis=-1, keepdims=True)), L2_EPS)
    k = k * (1.0 + (a - 1.0) * f32(k_a))
    rh, kh, vh, ah = heads(r), heads(k), heads(v), heads(a)
    y = rwkv7_scan(rh, heads(w), kh, vh, -kk, kk * ah)
    mu = jnp.mean(y, axis=-1, keepdims=True)
    var = jnp.mean(jnp.square(y - mu), axis=-1, keepdims=True)
    y = ((y - mu) * lax.rsqrt(var + GN_EPS)).reshape(b, s, RWKV_WIDTH) * f32(ln_w) + f32(ln_b)
    bonus = jnp.sum(rh * kh * f32(r_k), axis=-1, keepdims=True) * vh
    y = (y + bonus.reshape(b, s, RWKV_WIDTH)) * g
    return y.astype(out_dtype), v_out

def memory_attention(q, mk, mv):
    logits = jnp.einsum('bshd,bmhd->bhsm', q, mk,
                        preferred_element_type=jnp.float32) * (HEAD_DIM ** -0.5)
    p = jax.nn.softmax(logits, axis=-1)
    out = jnp.einsum('bhsm,bmhd->bshd', p.astype(mv.dtype), mv)
    return out.reshape(q.shape[0], q.shape[1], MEM_WIDTH)

def conv_ffn(h, w_up, conv_w, conv_b, w_down):
    u = h @ w_up
    s = u.shape[1]
    up_pad = jnp.pad(u, ((0, 0), (CONV_WIDTH - 1, 0), (0, 0)))
    uc = conv_b + sum(conv_w[i] * up_pad[:, i:i + s] for i in range(CONV_WIDTH))
    gate, val = jnp.split(uc, 2, axis=-1)
    return (jax.nn.silu(gate) * val) @ w_down

def first_inputs(seed: int = 0) -> dict:
    key = jax.random.key(seed)
    ks = iter(jax.random.split(key, 40))
    n = lambda shape: jax.random.normal(next(ks), shape, jnp.float32)
    L, Lv = DEPTH, DEPTH - 1
    C = RWKV_WIDTH
    return {
        "x": n((BATCH, SEQ, D_MODEL)),
        "mem": n((BATCH, MEM_TOKENS, D_MODEL)),
        "rel_bias": 0.5 * n((N_BUCKETS, ATTN_HEADS)),
        "mix_norm_g": 1.0 + 0.1 * n((L, D_MODEL)),
        "w_in": n((L, D_MODEL, IN_BASE)) * D_MODEL ** -0.5,
        "w_in_vres": n((Lv, D_MODEL, D_MV_LORA)) * D_MODEL ** -0.5,
        "attn_q_norm": 1.0 + 0.1 * n((L, HEAD_DIM)),
        "attn_k_norm": 1.0 + 0.1 * n((L, HEAD_DIM)),
        "attn_sinks": n((L, ATTN_HEADS)),
        "rwkv_mu": jax.random.uniform(next(ks), (L, RWKV_SHIFT_COLS), jnp.float32),
        "rwkv_mu_vres": jax.random.uniform(next(ks), (Lv, D_MV_LORA), jnp.float32),
        "rwkv_w0": -2.0 + 0.5 * n((L, C)),
        "rwkv_w2": 0.5 * n((L, D_DECAY_LORA, C)) * D_DECAY_LORA ** -0.5,
        "rwkv_a0": 0.5 * n((L, C)),
        "rwkv_a2": 0.5 * n((L, D_AAA_LORA, C)) * D_AAA_LORA ** -0.5,
        "rwkv_v0": 0.5 * n((Lv, C)),
        "rwkv_v2": 0.5 * n((Lv, D_MV_LORA, C)) * D_MV_LORA ** -0.5,
        "rwkv_g2": n((L, D_GATE_LORA, C)) * D_GATE_LORA ** -0.5,
        "rwkv_k_k": 0.85 + 0.1 * n((L, C)),
        "rwkv_k_a": 1.0 + 0.1 * n((L, C)),
        "rwkv_r_k": 0.1 * n((L, RWKV_HEADS, RWKV_HEAD_DIM)),
        "rwkv_ln_w": 1.0 + 0.1 * n((L, C)),
        "rwkv_ln_b": 0.02 * n((L, C)),
        "mem_norm_g": 1.0 + 0.1 * n((L, D_MODEL)),
        "w_mem_kv": n((L, D_MODEL, 2 * MEM_WIDTH)) * D_MODEL ** -0.5,
        "mem_q_norm": 1.0 + 0.1 * n((L, HEAD_DIM)),
        "mem_k_norm": 1.0 + 0.1 * n((L, HEAD_DIM)),
        "w_out": n((L, MIX_WIDTH, D_MODEL)) * MIX_WIDTH ** -0.5,
        "ffn_norm_g": 1.0 + 0.1 * n((L, D_MODEL)),
        "w_up": n((L, D_MODEL, 2 * D_FF)) * D_MODEL ** -0.5,
        "conv_w": n((L, CONV_WIDTH, 2 * D_FF)) * CONV_WIDTH ** -0.5,
        "conv_b": 0.02 * n((L, 2 * D_FF)),
        "w_down": n((L, D_FF, D_MODEL)) * D_FF ** -0.5,
    }

def first_block(x, mem, rel_bias, mix_norm_g, w_in, w_in_vres, attn_q_norm, attn_k_norm, attn_sinks,
              rwkv_mu, rwkv_mu_vres, rwkv_w0, rwkv_w2, rwkv_a0, rwkv_a2, rwkv_v0, rwkv_v2, rwkv_g2,
              rwkv_k_k, rwkv_k_a, rwkv_r_k, rwkv_ln_w, rwkv_ln_b, mem_norm_g, w_mem_kv,
              mem_q_norm, mem_k_norm, w_out, ffn_norm_g, w_up, conv_w, conv_b, w_down):
    b, s = x.shape[0], x.shape[1]
    m_tok = mem.shape[1]
    v_first = None
    for l in range(DEPTH):
        h = rms_norm(x, mix_norm_g[l])
        w_l = w_in[l] if l == 0 else jnp.concatenate([w_in[l], w_in_vres[l - 1]], axis=1)
        proj = h @ w_l
        sizes = [ATTN_WIDTH, ATTN_KV_WIDTH, ATTN_KV_WIDTH, RWKV_SHIFT_COLS, MEM_WIDTH]
        if l > 0:
            sizes = sizes + [D_MV_LORA]
        parts = split_cols(proj, sizes)
        qa, ka, va, pb, qm = parts[:5]

        qa = rms_norm(qa.reshape(b, s, ATTN_HEADS, HEAD_DIM), attn_q_norm[l])
        ka = rms_norm(ka.reshape(b, s, ATTN_KV_HEADS, HEAD_DIM), attn_k_norm[l])
        va = va.reshape(b, s, ATTN_KV_HEADS, HEAD_DIM)
        out_a = sliding_window_attention(qa, ka, va, attn_sinks[l], rel_bias)

        pb = token_shift(pb, rwkv_mu[l])
        if l == 0:
            vres = None
        else:
            v_down = token_shift(parts[5], rwkv_mu_vres[l - 1])
            vres = (v_first, v_down, rwkv_v0[l - 1], rwkv_v2[l - 1])
        out_b, v_l = rwkv7_mixer(pb, vres, rwkv_w0[l], rwkv_w2[l], rwkv_a0[l], rwkv_a2[l],
                                 rwkv_g2[l], rwkv_k_k[l], rwkv_k_a[l], rwkv_r_k[l],
                                 rwkv_ln_w[l], rwkv_ln_b[l])
        if l == 0:
            v_first = v_l

        mkv = rms_norm(mem, mem_norm_g[l]) @ w_mem_kv[l]
        mk, mv = jnp.split(mkv, 2, axis=-1)
        mk = rms_norm(mk.reshape(b, m_tok, MEM_HEADS, HEAD_DIM), mem_k_norm[l])
        mv = mv.reshape(b, m_tok, MEM_HEADS, HEAD_DIM)
        qm = rms_norm(qm.reshape(b, s, MEM_HEADS, HEAD_DIM), mem_q_norm[l])
        out_m = memory_attention(qm, mk, mv)

        x = x + jnp.concatenate([out_a, out_b, out_m], axis=-1) @ w_out[l]

        x = x + conv_ffn(rms_norm(x, ffn_norm_g[l]), w_up[l], conv_w[l], conv_b[l], w_down[l])
    return x


MOBA_HEADS = 8
MOBA_HEAD_DIM = 64
MOBA_BLOCK = 256
MOBA_TOPK = 3
MOBA_Q_CHUNK = 64
DIFF_HEADS = 4
DIFF_HEAD_DIM = 64
ATTN_Q_BLOCK = 128
ROPE_THETA = 10000.0
N_GROUPS = 4
EXPERTS_PER_GROUP = 8
N_EXPERTS = N_GROUPS * EXPERTS_PER_GROUP
EXPERT_TOPK = 2
D_EXPERT = 512
NORM_EPS = 1e-6
NEG_INF = -1e30
MOBA_WIDTH = MOBA_HEADS * MOBA_HEAD_DIM
DIFF_QK_WIDTH = DIFF_HEADS * 2 * DIFF_HEAD_DIM
DIFF_V_WIDTH = DIFF_HEADS * 2 * DIFF_HEAD_DIM
_SEGMENTS = (MOBA_WIDTH, MOBA_WIDTH, MOBA_WIDTH, DIFF_QK_WIDTH, DIFF_QK_WIDTH, DIFF_V_WIDTH, D_MODEL, D_MODEL)
IN_WIDTH = sum(_SEGMENTS)
IN_SPLITS = tuple(int(s) for s in np.cumsum(_SEGMENTS)[:-1])


def rmsnorm(x, g):
    xf = x.astype(jnp.float32)
    y = xf * lax.rsqrt(jnp.mean(xf * xf, axis=-1, keepdims=True) + NORM_EPS)
    return (y * g.astype(jnp.float32)).astype(x.dtype)

def rope_tables(seq, dim):
    inv = 1.0 / (ROPE_THETA ** (jnp.arange(0, dim, 2, dtype=jnp.float32) / dim))
    ang = jnp.arange(seq, dtype=jnp.float32)[:, None] * inv[None, :]
    return jnp.cos(ang), jnp.sin(ang)

def apply_rope(x, cos, sin):
    xf = x.astype(jnp.float32)
    half = x.shape[-1] // 2
    x1, x2 = xf[..., :half], xf[..., half:]
    return jnp.concatenate([x1 * cos - x2 * sin, x2 * cos + x1 * sin], axis=-1).astype(x.dtype)

def to_heads(t, n, d):
    b, s = t.shape[:2]
    return t.reshape(b, s, n, d).transpose(0, 2, 1, 3)

def moba_attention(q, k, v):
    B, H, S, dh = q.shape
    nb = -(-S // MOBA_BLOCK)
    topk = min(MOBA_TOPK, nb)
    pad = nb * MOBA_BLOCK - S
    kp = jnp.pad(k, ((0, 0), (0, 0), (0, pad), (0, 0)))
    vp = jnp.pad(v, ((0, 0), (0, 0), (0, pad), (0, 0)))
    k_blocks = kp.reshape(B, H, nb, MOBA_BLOCK, dh)
    v_blocks = vp.reshape(B, H, nb, MOBA_BLOCK, dh)
    k_mean = jnp.mean(k_blocks.astype(jnp.float32), axis=3)
    scale = dh ** -0.5
    nc = S // MOBA_Q_CHUNK
    q_chunks = q.reshape(B, H, nc, MOBA_Q_CHUNK, dh).transpose(2, 0, 1, 3, 4)
    starts = jnp.arange(nc, dtype=jnp.int32) * MOBA_Q_CHUNK
    b_idx = jnp.arange(B)[:, None, None, None]
    h_idx = jnp.arange(H)[None, :, None, None]
    block_ids = jnp.arange(nb, dtype=jnp.int32)
    own_offsets = jnp.arange(MOBA_BLOCK, dtype=jnp.int32)

    def chunk(args):
        qb, start = args
        blk = start // MOBA_BLOCK
        qpos = start + jnp.arange(MOBA_Q_CHUNK, dtype=jnp.int32)
        gate = jnp.einsum('bhqd,bhnd->bhqn', qb.astype(jnp.float32), k_mean)
        gate = jnp.where(block_ids < blk, gate, NEG_INF)
        _, sel = lax.top_k(gate, topk)
        valid = sel < blk
        ks = k_blocks[b_idx, h_idx, sel]
        vs = v_blocks[b_idx, h_idx, sel]
        s_sel = jnp.einsum('bhqd,bhqjnd->bhqjn', qb, ks).astype(jnp.float32) * scale
        s_sel = jnp.where(valid[..., None], s_sel, NEG_INF)
        s_sel = s_sel.reshape(B, H, MOBA_Q_CHUNK, topk * MOBA_BLOCK)
        k_own = lax.dynamic_slice_in_dim(kp, blk * MOBA_BLOCK, MOBA_BLOCK, axis=2)
        v_own = lax.dynamic_slice_in_dim(vp, blk * MOBA_BLOCK, MOBA_BLOCK, axis=2)
        s_own = jnp.einsum('bhqd,bhnd->bhqn', qb, k_own).astype(jnp.float32) * scale
        kpos = blk * MOBA_BLOCK + own_offsets
        s_own = jnp.where(kpos[None, :] <= qpos[:, None], s_own, NEG_INF)
        p = jax.nn.softmax(jnp.concatenate([s_sel, s_own], axis=-1), axis=-1).astype(v.dtype)
        p_sel = p[..., :topk * MOBA_BLOCK].reshape(B, H, MOBA_Q_CHUNK, topk, MOBA_BLOCK)
        p_own = p[..., topk * MOBA_BLOCK:]
        return (jnp.einsum('bhqjn,bhqjnd->bhqd', p_sel, vs)
                + jnp.einsum('bhqn,bhnd->bhqd', p_own, v_own))

    out = lax.map(chunk, (q_chunks, starts))
    return out.transpose(1, 2, 0, 3, 4).reshape(B, H, S, dh)

def diff_attention(q, k, v, lam):
    B, H2, S, dk = q.shape
    H = H2 // 2
    scale = dk ** -0.5
    nq = S // ATTN_Q_BLOCK
    q_blocks = q.reshape(B, H2, nq, ATTN_Q_BLOCK, dk).transpose(2, 0, 1, 3, 4)
    starts = jnp.arange(nq, dtype=jnp.int32) * ATTN_Q_BLOCK
    kpos = jnp.arange(S, dtype=jnp.int32)

    def block(args):
        qb, start = args
        s = jnp.einsum('bhqd,bhkd->bhqk', qb, k).astype(jnp.float32) * scale
        qpos = start + jnp.arange(ATTN_Q_BLOCK, dtype=jnp.int32)
        s = jnp.where(kpos[None, :] <= qpos[:, None], s, NEG_INF)
        p = jax.nn.softmax(s, axis=-1).reshape(B, H, 2, ATTN_Q_BLOCK, S)
        a = (p[:, :, 0] - lam * p[:, :, 1]).astype(v.dtype)
        return jnp.einsum('bhqk,bhkd->bhqd', a, v)

    out = lax.map(block, (q_blocks, starts))
    return out.transpose(1, 2, 0, 3, 4).reshape(B, H, S, 2 * dk)

def hierarchical_moe(h, w_group, b_group, w_expert, b_expert, w_gate, w_up, w_down):
    B, S, D = h.shape
    t = h.reshape(B * S, D)
    T = t.shape[0]
    g_prob = jax.nn.softmax((t @ w_group).astype(jnp.float32) + b_group, axis=-1)
    g_w, g_idx = lax.top_k(g_prob, 1)
    e_logits = ((t @ w_expert).astype(jnp.float32) + b_expert).reshape(T, N_GROUPS, EXPERTS_PER_GROUP)
    e_in_group = jnp.take_along_axis(e_logits, g_idx[:, :, None], axis=1)[:, 0]
    e_prob = jax.nn.softmax(e_in_group, axis=-1)
    e_w, e_idx = lax.top_k(e_prob, EXPERT_TOPK)
    e_w = e_w / jnp.sum(e_w, axis=-1, keepdims=True)
    weights = (g_w * e_w).reshape(-1)
    expert = (g_idx * EXPERTS_PER_GROUP + e_idx).reshape(-1)
    order = jnp.argsort(expert)
    tok = order // EXPERT_TOPK
    xs = t[tok]
    sizes = jnp.bincount(expert, length=N_EXPERTS).astype(jnp.int32)
    hid = jax.nn.silu(lax.ragged_dot(xs, w_gate, sizes)) * lax.ragged_dot(xs, w_up, sizes)
    out = lax.ragged_dot(hid.astype(xs.dtype), w_down, sizes)
    out = out * weights[order][:, None].astype(out.dtype)
    y = jnp.zeros_like(t).at[tok].add(out.astype(t.dtype))
    return y.reshape(B, S, D)

def second_inputs(seed: int = 0) -> dict:
    key = jax.random.key(seed)
    ks = jax.random.split(key, 24)
    D = D_MODEL

    def nrm(k, shape, scale):
        return jax.random.normal(k, shape, jnp.float32) * scale

    return {
        'x': nrm(ks[0], (BATCH, SEQ, D), 1.0),
        'c': nrm(ks[1], (BATCH, D), 1.0),
        'w_ada': nrm(ks[2], (DEPTH, D, 6 * D), 0.5 * D ** -0.5),
        'b_ada': nrm(ks[3], (DEPTH, 6 * D), 0.02),
        'norm1_g': 1.0 + nrm(ks[4], (DEPTH, D), 0.02),
        'w_in': nrm(ks[5], (DEPTH, D, IN_WIDTH), D ** -0.5),
        'lambda_q1': nrm(ks[6], (DEPTH, DIFF_HEAD_DIM), 0.1),
        'lambda_k1': nrm(ks[7], (DEPTH, DIFF_HEAD_DIM), 0.1),
        'lambda_q2': nrm(ks[8], (DEPTH, DIFF_HEAD_DIM), 0.1),
        'lambda_k2': nrm(ks[9], (DEPTH, DIFF_HEAD_DIM), 0.1),
        'diff_subln_g': 1.0 + nrm(ks[10], (DEPTH, 2 * DIFF_HEAD_DIM), 0.02),
        'w_proj_moba': nrm(ks[11], (DEPTH, MOBA_WIDTH, D), MOBA_WIDTH ** -0.5),
        'w_proj_diff': nrm(ks[12], (DEPTH, DIFF_V_WIDTH, D), DIFF_V_WIDTH ** -0.5),
        'w_out': nrm(ks[13], (DEPTH, D, D), D ** -0.5),
        'norm2_g': 1.0 + nrm(ks[14], (DEPTH, D), 0.02),
        'w_group': nrm(ks[15], (DEPTH, D, N_GROUPS), D ** -0.5),
        'b_group': nrm(ks[16], (DEPTH, N_GROUPS), 0.01),
        'w_expert': nrm(ks[17], (DEPTH, D, N_EXPERTS), D ** -0.5),
        'b_expert': nrm(ks[18], (DEPTH, N_EXPERTS), 0.01),
        'w_gate': nrm(ks[19], (DEPTH, N_EXPERTS, D, D_EXPERT), D ** -0.5),
        'w_up': nrm(ks[20], (DEPTH, N_EXPERTS, D, D_EXPERT), D ** -0.5),
        'w_down': nrm(ks[21], (DEPTH, N_EXPERTS, D_EXPERT, D), D_EXPERT ** -0.5),
        'final_g': 1.0 + nrm(ks[22], (D,), 0.02),
    }

def second_block(x, c, w_ada, b_ada, norm1_g, w_in, lambda_q1, lambda_k1, lambda_q2, lambda_k2,
              diff_subln_g, w_proj_moba, w_proj_diff, w_out, norm2_g, w_group, b_group,
              w_expert, b_expert, w_gate, w_up, w_down, final_g):
    S = x.shape[1]
    cos_m, sin_m = rope_tables(S, MOBA_HEAD_DIM)
    cos_d, sin_d = rope_tables(S, DIFF_HEAD_DIM)
    c_act = jax.nn.silu(c)
    for l in range(DEPTH):
        mod = c_act @ w_ada[l] + b_ada[l]
        sh1, sc1, g1, sh2, sc2, g2 = jnp.split(mod, 6, axis=-1)

        h = rmsnorm(x, norm1_g[l]) * (1.0 + sc1[:, None, :]) + sh1[:, None, :]
        proj = h @ w_in[l]
        q_m, k_m, v_m, q_d, k_d, v_d, gate_m, gate_d = jnp.split(proj, IN_SPLITS, axis=-1)

        qm = apply_rope(to_heads(q_m, MOBA_HEADS, MOBA_HEAD_DIM), cos_m, sin_m)
        km = apply_rope(to_heads(k_m, MOBA_HEADS, MOBA_HEAD_DIM), cos_m, sin_m)
        vm = to_heads(v_m, MOBA_HEADS, MOBA_HEAD_DIM)
        o_m = moba_attention(qm, km, vm)
        y_m = o_m.transpose(0, 2, 1, 3).reshape(x.shape[0], S, MOBA_WIDTH) @ w_proj_moba[l]

        lam_init = 0.8 - 0.6 * math.exp(-0.3 * l)
        lam = (jnp.exp(jnp.sum(lambda_q1[l].astype(jnp.float32) * lambda_k1[l].astype(jnp.float32)))
               - jnp.exp(jnp.sum(lambda_q2[l].astype(jnp.float32) * lambda_k2[l].astype(jnp.float32)))
               + lam_init)
        qd = apply_rope(to_heads(q_d, 2 * DIFF_HEADS, DIFF_HEAD_DIM), cos_d, sin_d)
        kd = apply_rope(to_heads(k_d, 2 * DIFF_HEADS, DIFF_HEAD_DIM), cos_d, sin_d)
        vd = to_heads(v_d, DIFF_HEADS, 2 * DIFF_HEAD_DIM)
        o_d = diff_attention(qd, kd, vd, lam)
        o_d = rmsnorm(o_d, diff_subln_g[l]) * (1.0 - lam_init)
        y_d = o_d.transpose(0, 2, 1, 3).reshape(x.shape[0], S, DIFF_V_WIDTH) @ w_proj_diff[l]

        merged = jax.nn.sigmoid(gate_m) * y_m + jax.nn.sigmoid(gate_d) * y_d
        x = x + g1[:, None, :] * (merged @ w_out[l])

        h2 = rmsnorm(x, norm2_g[l]) * (1.0 + sc2[:, None, :]) + sh2[:, None, :]
        y_ffn = hierarchical_moe(h2, w_group[l], b_group[l], w_expert[l], b_expert[l],
                                 w_gate[l], w_up[l], w_down[l])
        x = x + g2[:, None, :] * y_ffn
    return rmsnorm(x, final_g)


def setup_inputs(seed=0):
    out = dict(first_inputs(seed))
    for name, value in second_inputs(seed + 1).items():
        if name != "x":
            out[name + "_2"] = value
    return out


def reference(
    x, mem, rel_bias, mix_norm_g, w_in, w_in_vres, attn_q_norm, attn_k_norm, attn_sinks,
    rwkv_mu, rwkv_mu_vres, rwkv_w0, rwkv_w2, rwkv_a0, rwkv_a2, rwkv_v0, rwkv_v2, rwkv_g2,
    rwkv_k_k, rwkv_k_a, rwkv_r_k, rwkv_ln_w, rwkv_ln_b, mem_norm_g, w_mem_kv, mem_q_norm,
    mem_k_norm, w_out, ffn_norm_g, w_up, conv_w, conv_b, w_down, c_2, w_ada_2, b_ada_2,
    norm1_g_2, w_in_2, lambda_q1_2, lambda_k1_2, lambda_q2_2, lambda_k2_2, diff_subln_g_2,
    w_proj_moba_2, w_proj_diff_2, w_out_2, norm2_g_2, w_group_2, b_group_2, w_expert_2,
    b_expert_2, w_gate_2, w_up_2, w_down_2, final_g_2,
):
    x = first_block(
        x, mem, rel_bias, mix_norm_g, w_in, w_in_vres, attn_q_norm, attn_k_norm, attn_sinks,
        rwkv_mu, rwkv_mu_vres, rwkv_w0, rwkv_w2, rwkv_a0, rwkv_a2, rwkv_v0, rwkv_v2, rwkv_g2,
        rwkv_k_k, rwkv_k_a, rwkv_r_k, rwkv_ln_w, rwkv_ln_b, mem_norm_g, w_mem_kv, mem_q_norm,
        mem_k_norm, w_out, ffn_norm_g, w_up, conv_w, conv_b, w_down,
    )
    return second_block(
        x, c_2, w_ada_2, b_ada_2, norm1_g_2, w_in_2, lambda_q1_2, lambda_k1_2, lambda_q2_2,
        lambda_k2_2, diff_subln_g_2, w_proj_moba_2, w_proj_diff_2, w_out_2, norm2_g_2,
        w_group_2, b_group_2, w_expert_2, b_expert_2, w_gate_2, w_up_2, w_down_2, final_g_2,
    )


_drawn_inputs = setup_inputs


def setup_inputs(seed=0):
    import zlib

    import numpy as np

    out = dict(_drawn_inputs(seed))
    spreads = {}
    factors = {'attn_q_norm': 3.748,
     'attn_k_norm': 3.945,
     'attn_sinks': 8.0,
     'rwkv_w2': 2.744,
     'rwkv_k_k': 3.917,
     'rwkv_ln_b': 7.286,
     'mem_norm_g': 5.857,
     'mem_q_norm': 8.0,
     'mem_k_norm': 8.0,
     'conv_b': 3.394,
     'b_ada_2': 3.362,
     'norm1_g_2': 8.0,
     'lambda_q1_2': 8.0,
     'lambda_k1_2': 8.0,
     'lambda_q2_2': 3.106,
     'lambda_k2_2': 7.409,
     'diff_subln_g_2': 8.0,
     'norm2_g_2': 7.447,
     'b_group_2': 8.0,
     'b_expert_2': 22.271,
     'final_g_2': 8.266}
    for name, (base, spread) in spreads.items():
        noise = np.random.default_rng([zlib.crc32(name.encode()), seed]).standard_normal(out[name].shape)
        drawn = base * np.exp(spread * noise) if base else spread * noise
        out[name] = jnp.asarray(drawn.astype(out[name].dtype))
    for name, factor in factors.items():
        out[name] = (out[name] * factor).astype(out[name].dtype)
    return out
```

```python
import math

import numpy as np

import concourse.bass as bass
from concourse import mybir

T = 256
D = 1024
KT = 8
NEG = -1.0e30
LAM0 = 0.8 - 0.6 * math.exp(-0.3 * 0)
NSLOT = 32
NE = 32


def const_layout():
    names = [("ident", 128), ("bo", 128), ("ones", 128), ("perm", 128), ("rev", 128), ("cos", 256), ("sin", 256),
             ("caus", 128), ("SU", 128), ("IU", 128), ("SL", 128), ("LM", 7 * 128), ("LM1T", 128),
             ("iota", 32), ("key4", 4), ("key32", 32), ("hs", 30), ("hs2", 30), ("OHB", 1024), ("MR", 384)]
    at, off = {}, 0
    for n, w in names:
        at[n] = (off, w)
        off += w
    return at, off


def const_table():
    at, width = const_layout()
    c = np.zeros((128, width), np.float32)

    def put(name, a, rows=128):
        o, w = at[name]
        c[:rows, o:o + w] = a

    p = np.arange(128)
    t, j = p[:, None], p[None, :]
    put("ident", np.eye(128))
    put("rev", np.eye(128)[::-1])
    put("bo", (t // 64 == j // 64))
    put("ones", 1.0)
    pm = np.zeros((128, 128), np.float32)
    for o in range(128):
        if o % 64 < 32:
            pm[o + 32, o] = -1.0
        else:
            pm[o - 32, o] = 1.0
    put("perm", pm)
    inv = (1.0 / (np.float32(10000.0) ** (np.arange(0, 64, 2, dtype=np.float32) / np.float32(64)))).astype(np.float32)
    ang = (np.arange(T, dtype=np.float32)[:, None] * inv[None, :]).astype(np.float32)
    put("cos", np.cos(ang).astype(np.float32).T[p % 32])
    put("sin", np.sin(ang).astype(np.float32).T[p % 32])
    put("caus", np.where(j > t, NEG, 0.0))
    put("SU", t < j)
    put("IU", t <= j)
    put("SL", j < t)
    lm = [((t // (2 * s) == j // (2 * s)) & (t % (2 * s) >= s) & (j % (2 * s) < s)) for s in (1, 2, 4, 8, 16, 32, 64)]
    put("LM", np.concatenate(lm, 1))
    put("LM1T", lm[0].T)
    put("iota", np.arange(32)[None, :])
    put("key4", 8 - np.arange(4)[None, :])
    put("key32", 64 - np.arange(32)[None, :])
    hs = np.zeros((128, 30), np.float32)
    hs[:64, 14] = 1
    hs[64:, 15] = 1
    put("hs", hs)
    h2 = np.zeros((128, 30), np.float32)
    h2[:, 14:16] = 1
    put("hs2", h2)
    m = np.arange(384)
    dist = 255 - m
    ok = (dist >= 0) & (dist < 128)
    d = np.maximum(dist, 1).astype(np.float32)
    large = 16 + (np.log(d / np.float32(16)) / np.float32(math.log(8)) * np.float32(16)).astype(np.int32)
    bucket = np.where(dist < 16, np.maximum(dist, 0), np.minimum(large, 31))
    ob = np.zeros((128, 1024), np.float32)
    ob[64:96, 0:384] = (np.arange(32)[:, None] == bucket[None, :]) & ok[None, :]
    ob[0:16] = np.arange(16)[:, None] == np.arange(1024)[None, :] // 64
    put("OHB", ob)
    put("MR", np.where(ok, 0.0, NEG)[None, :].repeat(6, 0), 6)
    return c


PARAMS = [("mix_norm_g", 8), ("mem_norm_g", 8), ("ffn_norm_g", 8), ("norm1_g_2", 8), ("norm2_g_2", 8), ("c_2", 8),
          ("rwkv_mu", 10), ("rwkv_w0", 3), ("rwkv_a0", 3), ("rwkv_k_k", 3), ("rwkv_k_a", 3), ("rwkv_r_k", 3),
          ("rwkv_ln_w", 3), ("rwkv_ln_b", 3), ("diff_subln_g_2", 1),
          ("attn_q_norm", 1), ("attn_k_norm", 1), ("mem_q_norm", 1), ("mem_k_norm", 1),
          ("", 44), ("b_ada_2", 48), ("conv_b", 44), ("conv_w", 132)]


class Lane:

    def __init__(self, sem):
        self.sem, self.n, self.items = sem, 0, []

    def op(self, fn, *waits):
        self.n += 1
        self.items.append((fn, waits))
        return (self.sem, self.n)

    def job(self, fn, *waits):
        self.items.append((fn, waits))

    def last(self):
        return (self.sem, self.n)

    def play(self, eng):
        seen = {}

        def wait(w):
            if w is None:
                return
            if isinstance(w, list):
                for x in w:
                    wait(x)
                return
            sem, v = w
            if v > 0 and seen.get(id(sem), 0) < v:
                eng.wait_ge(sem, v)
                seen[id(sem)] = v

        for fn, waits in self.items:
            for w in waits:
                wait(w)
            r = fn(eng)
            if r is not None:
                r.then_inc(self.sem, 1)


class Bank:
    def __init__(self, ap):
        self.ap, self.w = ap, []


class Banks:

    def __init__(self, banks):
        self.banks, self.i = banks, 0

    def take(self):
        b = self.banks[self.i % len(self.banks)]
        self.i += 1
        return b


class Chunk:
    def __init__(self, ap, parts, sem, value, before):
        self.ap, self.parts, self.sem, self.tok, self.before, self.free = ap, parts, sem, (sem, value), before, None


class Ring:

    def __init__(self, aps, sems):
        self.aps, self.sems, self.counts, self.chunks = aps, sems, [0] * len(aps), []

    def load(self, *parts):
        n = len(self.chunks)
        s = n % len(self.aps)
        before = self.chunks[n - len(self.aps)] if n >= len(self.aps) else None
        self.counts[s] += 16 * len(parts)
        c = Chunk(self.aps[s], parts, self.sems[s], self.counts[s], before)
        self.chunks.append(c)
        return c

    def play(self, eng):
        for c in self.chunks:
            if c.before is not None:
                if c.before.free is None:
                    break
                for w in c.before.free:
                    eng.wait_ge(*w)
            for dst, src in c.parts:
                eng.dma_start(dst(c.ap), src).then_inc(c.sem, 16)


class Arena:

    def __init__(self, ap, width):
        self.ap, self.regions, self.top = ap, [[0, width, []]], 0

    def get(self, n, high=False):
        if high:
            for r in reversed(self.regions):
                if r[1] >= n:
                    r[1] -= n
                    b = Buf(self.ap[:, r[0] + r[1]:r[0] + r[1] + n], r[0] + r[1], n, list(r[2]))
                    if r[1] == 0:
                        self.regions.remove(r)
                    return b
        best = None
        for r in self.regions:
            if r[1] >= n and (best is None or r[1] < best[1]):
                best = r
        if best is None:
            raise ValueError(f"arena full: {n} of {self.regions}")
        b = Buf(self.ap[:, best[0]:best[0] + n], best[0], n, list(best[2]))
        best[0] += n
        best[1] -= n
        self.top = max(self.top, b.off + n)
        if best[1] == 0:
            self.regions.remove(best)
        return b

    def free(self, tokens, *bufs):
        for b in bufs:
            self.regions.append([b.off, b.n, list(tokens)])
        self.regions.sort(key=lambda r: r[0])
        out = []
        for r in self.regions:
            if out and out[-1][0] + out[-1][1] == r[0]:
                out[-1][1] += r[1]
                top = {}
                for s, v in out[-1][2] + r[2]:
                    top[id(s)] = (s, max(v, top.get(id(s), (s, 0))[1]))
                out[-1][2] = list(top.values())
            else:
                out.append([r[0], r[1], list(r[2])])
        self.regions = out


class Buf:
    def __init__(self, ap, off, n, w):
        self.ap, self.off, self.n, self.w = ap, off, n, w

    def v(self, pat, **k):
        return self.ap.rearrange(pat, **k)


def block_kernel(nc, A, out):
    from contextlib import ExitStack
    F = mybir.dt.float32
    I32 = mybir.dt.int32
    ALU = mybir.AluOpType
    ACT = mybir.ActivationFunctionType
    AX = mybir.AxisListType
    MUL, ADD, SUB, MAX, EQ = ALU.mult, ALU.add, ALU.subtract, ALU.max, ALU.is_equal
    NS = 6
    CL, CW = const_layout()
    NSEG = 28300

    ctx = ExitStack()
    with ctx:
        def sb(name, shape, dt=F):
            return ctx.enter_context(nc.sbuf_tensor(name, shape, dt))

        def sem(name):
            return ctx.enter_context(nc.semaphore(name))

        ringt = sb("ringt", [128, NS, 4096])
        arena_t = sb("arena", [128, NSEG])
        psum = [ctx.enter_context(nc.psum_tensor(f"ps{i}", [128, 512], F)) for i in range(8)]
        scratch = nc.dram_tensor("bias_scratch", [6, 384], F, kind="Internal")

        ar = Arena(arena_t, NSEG)
        PE, VE, SC, GP = Lane(sem("s_pe")), Lane(sem("s_ve")), Lane(sem("s_sc")), Lane(sem("s_gp"))
        ring = Ring([ringt[:, i, :] for i in range(NS)], [sem(f"s_ring{i}") for i in range(NS)])
        s_par = sem("s_par")
        s_par2 = sem("s_par2")
        s_x = sem("s_x")
        s_cst = sem("s_cst")
        s_bias = sem("s_bias")
        s_out = sem("s_out")
        s_gb = sem("s_gb")
        s_rt = sem("s_rt")
        s_fg = sem("s_fg")
        s_x2 = sem("s_x2")
        s_done, s_done2 = sem("s_done"), sem("s_done2")
        s_go = [sem(f"s_go{i}") for i in range(4)]

        def later(waits, parts, sm):
            def run(e):
                for d, s_ in parts:
                    e.dma_start(d, s_).then_inc(sm, 16)
                return None
            GP.job(run, waits)
        ps = Banks([Bank(p[:, :]) for p in psum])
        cur = {"pe": PE, "ve": VE, "sc": SC, "gp": GP}

        def pe(fn, *w):
            return cur["pe"].op(fn, *w)

        def ve(fn, *w):
            return cur["ve"].op(fn, *w)

        def sc(fn, *w):
            return cur["sc"].op(fn, *w)

        def gp(fn, *w):
            return cur["gp"].op(fn, *w)

        def now():
            return [PE.last(), VE.last(), SC.last(), GP.last()]

        def tt(o, a, b, op, *w):
            return ve(lambda e: e.tensor_tensor(o, a, b, op), *w)

        def ts(o, a, s1, op0, s2, op1, *w):
            if s2 is None:
                return ve(lambda e: e.tensor_scalar(o, a, s1, None, op0), *w)
            return ve(lambda e: e.tensor_scalar(o, a, s1, s2, op0, op1), *w)

        def stt(o, a, s, b, op0, op1, *w):
            return ve(lambda e: e.scalar_tensor_tensor(out=o, in0=a, scalar=s, in1=b, op0=op0, op1=op1), *w)

        def vcp(o, a, *w):
            return ve(lambda e: e.tensor_copy(o, a), *w)

        def act(o, a, f, *w, bias=0.0, scale=1.0, accum=None):
            if accum is None:
                return sc(lambda e: e.activation(o, a, f, bias=bias, scale=scale), *w)
            return sc(lambda e: e.activation(o, a, f, bias=bias, scale=scale, accum_out=accum), *w)

        def acp(o, a, *w):
            return sc(lambda e: e.activation(o, a, ACT.Copy), *w)

        def mm(o, l, r, start, stop):
            return lambda e: e.matmul(o, l, r, start=start, stop=stop, skip_group_check=True)

        def tr(o, i, ident):
            return lambda e: e.transpose(o, i, ident)

        def pes(fns, *w):
            def run(e):
                for f in fns:
                    last = f(e)
                return last
            return pe(run, *w)

        def bc(ap, shape):
            return ap.to_broadcast(shape)

        cst = ar.get(CW)
        C = {n: cst.ap[:, o:o + w] for n, (o, w) in CL.items()}
        par = ar.get(384)
        X = ar.get(2048)
        x = X.v("p (b d) -> p b d", b=2)
        small = ar.get(160)
        sm_at = [0]

        def sml(n):
            o = sm_at[0]
            sm_at[0] += n
            if sm_at[0] > 160:
                raise ValueError("small")
            return small.ap[:, o:o + n]

        rows = ar.get(384)
        Xm = ar.get(2048)
        xm = Xm.v("p (b d) -> p b d", b=2)
        swb = ar.get(1536)
        L2 = ar.get(384)
        relb = ar.get(8)
        sink = ar.get(8)
        lamv = ar.get(256)
        gpos, n_par = {}, 0
        for name, cnt in PARAMS:
            gpos[name] = n_par
            n_par += cnt

        def col(name, i=0, n=1):
            return par.ap[:, gpos[name] + i:gpos[name] + i + n]

        x_in = x

        def load_first(eng):
            eng.dma_start(x_in, A["x"].rearrange("a (b p) d -> p (a b) d", p=128)).then_inc(s_x, 16)
            eng.dma_start(cst.ap, A["consts"]).then_inc(s_cst, 16)
            pdma(eng, plist, s_par)
            eng.dma_start(xm, A["mem"].rearrange("a (b p) d -> p (a b) d", p=128)).then_inc(s_x, 16)
        def pdma(eng, lst, sm):
            for d, s in lst:
                eng.dma_start(d, s).then_inc(sm, 16)

        plist, plist2 = [], []
        for name, cnt in PARAMS:
            if not name:
                continue
            r0 = gpos[name]
            if name in ("attn_q_norm", "attn_k_norm", "mem_q_norm", "mem_k_norm"):
                src = A[name]
                for h in range(2):
                    plist.append((rows.ap[r0 % 128:r0 % 128 + 1, 128 * (r0 // 128) + 64 * h:128 * (r0 // 128) + 64 * h + 64], src))
                continue
            flat = A[name]
            if name == "conv_w":
                flat = flat.rearrange("a i (t p) -> (a i t) p", p=128)
            elif name == "rwkv_r_k":
                flat = flat.rearrange("a (t h) d -> (a t) (h d)", h=2)
            else:
                flat = flat.rearrange("a (t p) -> (a t) p", p=128)
            i = 0
            while i < cnt:
                r = r0 + i
                m = min(cnt - i, 128 - r % 128)
                (plist2 if r >= 128 else plist).append((rows.ap[r % 128:r % 128 + m, 128 * (r // 128):128 * (r // 128) + 128], flat[i:i + m, :]))
                i += m
        plist2.append((L2.ap[0:32, :], A["rwkv_w2"][0, :, :]))
        plist2.append((L2.ap[32:64, :], A["rwkv_a2"][0, :, :]))
        plist2.append((L2.ap[64:128, :], A["rwkv_g2"][0, :, :]))
        plist2.append((relb.ap[64:96, 0:6], A["rel_bias"]))
        plist2.append((sink.ap[:, 0:6], bc(A["attn_sinks"], [128, 6])))
        for i, name in enumerate(("lambda_q1_2", "lambda_k1_2", "lambda_q2_2", "lambda_k2_2")):
            plist2.append((lamv.ap[:, 64 * i:64 * i + 64], bc(A[name], [128, 64])))
        par1_tok = (s_par, 16 * len(plist))
        par_tok = (s_par2, 16 * len(plist2))
        x_tok = (s_x, 32)
        cst_tok = (s_cst, 16)
        ident = C["ident"]
        ones = C["ones"]

        def wcols(ap, c0, n, at=0):
            k = ap.shape[0] // 128

            def dst(s, k=k, n=n, at=at):
                return s[:, at:at + k * n].rearrange("p (k n) -> p k n", k=k)
            return dst, ap[:, c0:c0 + n].rearrange("(k p) n -> p k n", p=128)

        w_in = A["w_in"][0, :, :]
        ch_in = [ring.load(wcols(w_in, 640, 512)), ring.load(wcols(w_in, 1152, 512)),
                 ring.load(wcols(w_in, 1664, 512)), ring.load(wcols(w_in, 0, 512)),
                 ring.load(wcols(w_in, 512, 128))]
        ch_mem = ring.load(wcols(A["w_mem_kv"][0, :, :], 0, 512))
        w_ada = A["w_ada_2"][0, :, :]
        ch_ada = [ring.load(wcols(w_ada, 512 * i, 512)) for i in range(12)]
        w_o = A["w_out"][0, :, :]
        ch_o = [ring.load(wcols(w_o, 512 * i, 512)) for i in range(2)]
        w_up = A["w_up"][0, :, :]
        ch_up = [ring.load(wcols(w_up, 256 * i, 256), wcols(w_up, 2816 + 256 * i, 256, 2048)) for i in range(11)]
        w_dn = A["w_down"][0, :, :]
        ch_dn = [ring.load(wcols(w_dn[512 * i:min(512 * i + 512, 2816), :], 0, 1024)) for i in range(6)]
        w_in2 = A["w_in_2"][0, :, :]
        ch_i2 = [ring.load(wcols(w_in2, 512 * i, 512)) for i in range(10)]
        ch_pm = ring.load(wcols(A["w_proj_moba_2"][0, :, :], 0, 1024))
        ch_pd = ring.load(wcols(A["w_proj_diff_2"][0, :, :], 0, 1024))
        ch_o2 = [ring.load(wcols(A["w_out_2"][0, :, :], 512 * i, 512)) for i in range(2)]

        def load_expert(rg, e):
            return [rg.load(wcols(A["w_gate_2"][0, e, :, :], 0, 512)), rg.load(wcols(A["w_up_2"][0, e, :, :], 0, 512)),
                    rg.load(wcols(A["w_down_2"][0, e, :, :], 0, 1024))]
        ch_e = [load_expert(ring, e) for e in range(NE)]

        n_first = gpos[""]

        def par_cols(i, n, tok):
            b = ps.take()
            t = pe(tr(b.ap[:, 0:n], rows.ap[0:n, 128 * i:128 * i + 128], ident[0:n, 0:n]), tok, cst_tok, b.w)
            t = vcp(par.ap[:, 128 * i:128 * i + n], b.ap[:, 0:n], t)
            b.w = [t]
            return t
        t_par = par_cols(0, n_first, par1_tok)
        junk = ar.get(1024)

        def rstd_rows(src, tok, eps=1e-6, n=1024.0):
            s, r = sml(2), sml(2)
            for i in range(2):
                t1 = act(junk.ap, src[:, i, :], ACT.Square, tok, SC.last(), VE.last(), accum=s[:, i:i + 1])
            t2 = ts(r, s, 1.0 / n, MUL, eps, ADD, t1)
            t3 = ve(lambda e: e.reciprocal(s, r), t2)
            return r, act(r, s, ACT.Sqrt, t3)

        def normed(src, tok, dst, eps=1e-6):
            r, t3 = rstd_rows(src, tok, eps)
            for i in range(2):
                t4 = ts(dst.v("p (b d) -> p b d", b=2)[:, i, :], src[:, i, :], r[:, i:i + 1], MUL, None, None, t3, dst.w, tok)
            return t4

        def to_features(src, tok, dst, gcol, shift=None, dtok=None):
            sv = src.v("p (b d) -> p b d", b=2)
            dv = dst.v("p (k t) -> p k t", k=8)
            for k in range(0, 8, 2):
                b = ps.take()
                t = pes([tr(b.ap[:, 256 * i + 128 * h:256 * i + 128 * h + 128], sv[:, h, 128 * (k + i):128 * (k + i) + 128], ident)
                         for i in range(2) for h in range(2)], tok, b.w, cst_tok)
                pv = b.ap.rearrange("p (k t) -> p k t", k=2)
                if shift is None:
                    t2 = tt(dv[:, k:k + 2, :], pv, bc(gcol[:, k:k + 2].unsqueeze(2), [128, 2, 256]), MUL, t, dst.w, t_par, dtok)
                else:
                    for i in range(2):
                        t2 = ts(dv[:, k + i, :], pv[:, i, :], gcol[:, k + i:k + i + 1], MUL, shift[:, k + i:k + i + 1], ADD, t, dst.w, dtok)
                b.w = [t2]
            return t2

        Xn = ar.get(2048)
        hT = ar.get(2048)
        t = normed(x, x_tok, Xn)
        t_h = to_features(Xn, t, hT, col("mix_norm_g", 0, 8))
        ar.free(now(), Xn)
        Mn = ar.get(2048)
        mT = ar.get(2048)
        t = normed(xm, x_tok, Mn)
        t_m = to_features(Mn, t, mT, col("mem_norm_g", 0, 8))
        ar.free(now(), Mn, Xm, X)
        hv = hT.v("p (k t) -> p k t", k=8)
        mv_ = mT.v("p (k t) -> p k t", k=8)

        def proj_fm(b, half, chunk, cols, c0, act_v, k_n=8, base=0):
            w = chunk.ap[:, base:base + k_n * cols].rearrange("p (k n) -> p k n", k=k_n)
            return [mm(b.ap[:, 256 * half:256 * half + 256], w[:, k, c0:c0 + 128], act_v[:, k, :], k == 0, k == k_n - 1)
                    for k in range(k_n)]

        pz = ar.get(10 * 257)
        pzv = pz.v("p (n t) -> p n t", n=10)
        t_z = gp(lambda e: e.memset(pzv[:, :, 0:1], 0.0), pz.w)
        evac = []
        for i in range(0, 10, 2):
            b = ps.take()
            for h in range(2):
                n = i + h
                ch = ch_in[n // 4]
                t = pes(proj_fm(b, h, ch, 512, 128 * (n % 4), hv), t_h, ch.tok, b.w)
            t2 = acp(pzv[:, i:i + 2, 1:257], b.ap.rearrange("p (n t) -> p n t", n=2), t, pz.w)
            b.w = [t2]
            if i == 2:
                ch_in[0].free = [t]
            if i == 6:
                ch_in[1].free = [t]
        t_pz = t2
        par_cols(1, 128, par_tok)
        t_par = par_cols(2, n_par - 256, par_tok)
        b = ps.take()
        t = pe(mm(b.ap[0:6, 0:384], relb.ap[64:96, 0:6], C["OHB"][64:96, 0:384], True, True), b.w)
        Eb = ar.get(384)
        t_eb = tt(Eb.ap[0:6, :], b.ap[0:6, 0:384], C["MR"][0:6, :], ADD, t, Eb.w)
        b.w = [t_eb]
        bias_v = swb.v("p (h k) -> p h k", h=6)
        toep = bass.AP(scratch, 0, [[1, 128], [384, 6], [1, 256]])
        swr = ar.get(1536)
        swr_v = swr.v("p (h k) -> p h k", h=6)
        bias_tok = (s_bias, 32)

        def bias_dma(e):
            e.dma_start(scratch.ap(), Eb.ap[0:6, :]).then_inc(s_bias, 16)
            e.wait_ge(s_bias, 16)
            e.dma_start(swr_v, toep).then_inc(s_bias, 16)
            return None
        GP.job(bias_dma, t_eb, swr.w)

        qk = ar.get(8 * 256)
        qkv = qk.v("p (n t) -> p n t", n=8)
        plan = [(ch_in[2], 256, hv, t_h), (ch_in[2], 384, hv, t_h), (ch_in[3], 0, hv, t_h), (ch_in[3], 128, hv, t_h),
                (ch_in[3], 256, hv, t_h), (ch_in[3], 384, hv, t_h), (ch_mem, 0, mv_, t_m), (ch_mem, 128, mv_, t_m)]
        va = ar.get(256)
        vm = ar.get(512)
        for i in range(0, 8, 2):
            b = ps.take()
            for h in range(2):
                ch, c0, av, tk = plan[i + h]
                t = pes(proj_fm(b, h, ch, 512, c0, av), tk, ch.tok, b.w)
            t_qk = acp(qkv[:, i:i + 2, :], b.ap.rearrange("p (n t) -> p n t", n=2), t, qk.w)
            b.w = [t_qk]
            if i == 0:
                ch_in[2].free = [t]
            if i == 4:
                ch_in[3].free = [t]
        b = ps.take()
        w = ch_in[4].ap[:, 0:1024].rearrange("p (k n) -> p k n", k=8)
        for h in range(2):
            t = pes([mm(b.ap[:, 128 * h:128 * h + 128], hv[:, k, 128 * h:128 * h + 128], w[:, k, :], k == 0, k == 7)
                     for k in range(8)], ch_in[4].tok, b.w)
        ch_in[4].free = [t]
        t_va = acp(va.ap, b.ap[:, 0:256], t, va.w)
        b.w = [t_va]
        b = ps.take()
        w = ch_mem.ap.rearrange("p (k n) -> p k n", k=8)
        for h in range(2):
            t = pes([mm(b.ap[:, 256 * h:256 * h + 256], mv_[:, k, 128 * h:128 * h + 128], w[:, k, 256:512], k == 0, k == 7)
                     for k in range(8)], b.w)
        ch_mem.free = [t]
        t_vm = acp(vm.ap, b.ap, t, vm.w)
        b.w = [t_vm]
        ar.free(now(), hT, mT, rows)

        def head_rstd(tiles, tok, n, eps, dst, nh, floor=None, sel="hs"):
            b = ps.take()
            fns = [mm(b.ap[0:16, 0:256], C[sel][:, 14 - 2 * i:30 - 2 * i], s, i == 0, i == len(tiles) - 1)
                   for i, s in enumerate(tiles)]
            t = pes(fns, tok, b.w)
            if floor is None:
                t = ts(dst[0:16, 0:256], b.ap[0:16, 0:256], 1.0 / n, MUL, eps, ADD, t)
            else:
                t = ts(dst[0:16, 0:256], b.ap[0:16, 0:256], floor, MAX, None, None, t)
            b.w = [t]
            t = ve(lambda e: e.reciprocal(dst[0:16, 256:512], dst[0:16, 0:256]), t)
            return act(dst[0:16, 0:256], dst[0:16, 256:512], ACT.Sqrt, t)

        def head_bcast(b, half, i, dst):
            return mm(b.ap[:, 256 * half:256 * half + 256], C["OHB"][0:16, 128 * i:128 * i + 128],
                      dst[0:16, 0:256], True, True)

        sq = ar.get(2048)
        rs = ar.get(512)
        t = tt(sq.ap, qk.ap, qk.ap, MUL, t_qk, sq.w)
        sqv = sq.v("p (n t) -> p n t", n=8)
        t_rs = head_rstd([sqv[:, i, :] for i in range(8)], [t, *rs.w], 64.0, 1e-6, rs.ap, 16)
        gains = ["mem_q_norm", "mem_q_norm", "attn_q_norm", "attn_q_norm", "attn_q_norm", "attn_k_norm", "mem_k_norm", "mem_k_norm"]
        for i in range(0, 8, 2):
            b = ps.take()
            t = pes([head_bcast(b, 0, i, rs.ap), head_bcast(b, 1, i + 1, rs.ap)], t_rs, b.w)
            for h in range(2):
                t_qn = stt(qkv[:, i + h, :], qkv[:, i + h, :], col(gains[i + h]), b.ap[:, 256 * h:256 * h + 256], MUL, MUL, t)
            b.w = [t_qn]
        ar.free(now(), sq, rs)
        kb = ar.get(256)
        t_kb = act(kb.ap[0:64, :], qkv[64:128, 5, :], ACT.Copy, t_qn, kb.w)
        t_kb = act(kb.ap[64:128, :], qkv[0:64, 5, :], ACT.Copy, t_qn)

        for i in range(3):
            b = ps.take()
            t = pe(mm(b.ap, C["rev"], swr.ap[:, 512 * i:512 * i + 512], True, True), bias_tok, b.w)
            t_sw = acp(swb.ap[:, 512 * i:512 * i + 512], b.ap, t, swb.w)
            b.w = [t_sw]
        ar.free(now(), swr)
        cat = ar.get(2048)
        catv = cat.v("p (k t) -> p k t", k=8)

        cpad = ar.get(256)
        cpv = cpad.v("p (k m) -> p k m", k=8)
        modc = ar.get(32, True)
        g1b, g2b = ar.get(1024, True), ar.get(1024, True)
        msb = [ar.get(512), ar.get(512)]
        ms_free = [[], []]
        t_cp = ve(lambda e: e.memset(cpad.ap, 0.0), cpad.w)
        t_cp = act(cpv[:, :, 0:1].rearrange("p k o -> p (k o)"), col("c_2", 0, 8), ACT.Silu, t_cp, t_par)
        ada_tok = []

        def ada_step(i):
            b, m = ps.take(), msb[i % 2]
            w = ch_ada[i].ap.rearrange("p (k n) -> p k n", k=8)
            t = pes([mm(b.ap[32 * j:32 * j + 32, :], cpv[:, 2 * j + q, :], w[:, 2 * j + q, :], q == 0, q == 1)
                     for q in range(2) for j in range(4)], ch_ada[i].tok, t_cp, b.w)
            ch_ada[i].free = [t]
            t2 = acp(m.ap, b.ap, t, ms_free[i % 2], m.w)
            b.w = [t2]
            b = ps.take()
            part = i // 2
            if part in (2, 5):
                t = pe(mm(b.ap, ones, m.ap, True, True), t2, b.w)
                gb = (g1b if part == 2 else g2b).ap[:, 512 * (i % 2):512 * (i % 2) + 512]
                t3 = tt(gb, b.ap, gb, ADD, t, (s_gb, 32))
            else:
                t = pes([mm(b.ap[:, q:q + 1], m.ap[:, 128 * q:128 * q + 128], ones[:, 0:1], True, True) for q in range(4)], t2, b.w)
                o = {0: 0, 1: 8, 3: 16, 4: 24}[part] + 4 * (i % 2)
                t3 = tt(modc.ap[:, o:o + 4], b.ap[:, 0:4], col("b_ada_2", 4 * i, 4), ADD, t, modc.w)
            b.w = [t3]
            ms_free[i % 2] = [t]
            ada_tok.append(t3)
        ada_n = [0]

        def ada_next(n=1):
            for _ in range(n):
                if ada_n[0] < 12:
                    ada_step(ada_n[0])
                    ada_n[0] += 1
        later(g1b.w, [(g1b.ap, bc(A["b_ada_2"][:, 2048:3072], [128, 1024]))], s_gb)
        later(g2b.w, [(g2b.ap, bc(A["b_ada_2"][:, 5120:6144], [128, 1024]))], s_gb)

        NB_A = 2
        S_ = [ar.get(512) for _ in range(NB_A)]
        P_ = [ar.get(512) for _ in range(NB_A)]
        PT_ = [ar.get(512) for _ in range(NB_A)]
        st_ = [sml(12) for _ in range(NB_A)]
        a_free = [[[], []] for _ in range(NB_A)]
        a_n = [0]

        def attn_scores(q2, k2, blk, nk, masks, tok, sink_c=None, combine=None):
            i = a_n[0] % NB_A
            a_n[0] += 1
            S, P, PT, st = S_[i], P_[i], PT_[i], st_[i]
            bb = [ps.take(), ps.take()]
            w = nk * 128
            t = pes([mm(bb[h].ap[:, 0:w], q2[h][:, 128 * blk:128 * blk + 128], k2[h][:, 0:w], True, True)
                     for h in range(2)], tok, bb[0].w, bb[1].w)
            sv = S.ap[:, 0:2 * w].rearrange("p (h k) -> p h k", h=2)
            prev = a_free[i][0]
            for h in range(2):
                t1 = masks(h, sv[:, h, :], bb[h].ap[:, 0:w], [t, *prev, *S.w])
                bb[h].w = [t1]
            mx, nm, ssum, rc = st[:, 0:2], st[:, 2:4], st[:, 4:6], st[:, 6:8]
            t2 = ve(lambda e: e.tensor_reduce(mx, sv, AX.X, MAX), t1, prev)
            if sink_c is not None:
                t2 = tt(mx, mx, sink_c, MAX, t2)
            t3 = ts(nm, mx, -1.0, MUL, None, None, t2)
            pv = P.ap[:, 0:2 * w].rearrange("p (h k) -> p h k", h=2)
            for h in range(2):
                t4 = act(pv[:, h, :], sv[:, h, :], ACT.Exp, t3, prev, P.w, bias=nm[:, h:h + 1], accum=ssum[:, h:h + 1])
            if sink_c is not None:
                t5 = tt(st[:, 8:10], sink_c, nm, ADD, t3)
                t5 = act(st[:, 10:12], st[:, 8:10], ACT.Exp, t5)
                t4 = tt(ssum, ssum, st[:, 10:12], ADD, t4, t5)
            t5 = ve(lambda e: e.reciprocal(rc, ssum), t4)
            return i, pv, rc, t5, w

        def attn_out(i, pv, rc, t5, w, nk, v2, dst, vtok, dtok):
            P, PT = P_[i], PT_[i]
            t6 = tt(pv, pv, bc(rc.unsqueeze(2), [128, 2, w]), MUL, t5)
            b = ps.take()
            t7 = pes([tr(b.ap[:, 128 * (nk * h + j):128 * (nk * h + j) + 128], pv[:, h, 128 * j:128 * j + 128], ident)
                      for h in range(2) for j in range(nk)], t6, b.w)
            t8 = acp(PT.ap[:, 0:2 * w], b.ap[:, 0:2 * w], t7, a_free[i][1], PT.w)
            b.w = [t8]
            b = ps.take()
            t9 = pes([mm(b.ap[64 * h:64 * h + 64, 0:128], v2[h](j), PT.ap[:, 128 * (nk * h + j):128 * (nk * h + j) + 128], j == 0, j == nk - 1)
                      for h in range(2) for j in range(nk)], t8, vtok, b.w)
            t10 = acp(dst, b.ap[:, 0:128], t9, dtok)
            b.w = [t10]
            a_free[i] = [[t7, t6], [t9]]
            return t10

        def plain(h, sv, bv, w):
            return ts(sv, bv, 0.125, MUL, None, None, *w)

        def causal(nk):
            def f(h, sv, bv, w):
                if nk == 2:
                    ts(sv[:, 0:128], bv[:, 0:128], 0.125, MUL, None, None, *w)
                l = 128 * (nk - 1)
                return stt(sv[:, l:l + 128], bv[:, l:l + 128], 0.125, C["caus"], MUL, ADD, *w)
            return f

        def windowed(pair, nk):
            def f(h, sv, bv, w):
                return stt(sv, bv, 0.125, bias_v[:, 2 * pair + h, 256 - 128 * nk:256], MUL, ADD, t_sw, *w)
            return f

        def hrow(ap, h):
            return ap[64 * (h % 2):64 * (h % 2) + 64, :]

        vmv = vm.v("p (b d) -> p b d", b=2)
        for pr in range(2):
            for blk in range(2):
                r = attn_scores([hrow(qkv[:, pr, :], h) for h in range(2)], [hrow(qkv[:, 6 + pr, :], h) for h in range(2)],
                                blk, 2, plain, t_qn)
                t_cat = attn_out(*r, 2, [(lambda j, h=2 * pr + h: vmv[:, j, 64 * h:64 * h + 64]) for h in range(2)],
                                 catv[:, 6 + pr, 128 * blk:128 * blk + 128], t_vm, cat.w)
                ada_next()
        vav = va.v("p (b d) -> p b d", b=2)
        for pr in range(3):
            for blk in range(2):
                nk = 1 + blk
                ks = []
                for h in range(2):
                    kvh = (2 * pr + h) // 3
                    ks.append(hrow(qkv[:, 5, :] if kvh == h else kb.ap, h))
                r = attn_scores([hrow(qkv[:, 2 + pr, :], h) for h in range(2)], ks, blk, nk, windowed(pr, nk), [t_qn, t_kb],
                                sink_c=sink.ap[:, 2 * pr:2 * pr + 2])
                t_cat = attn_out(*r, nk, [(lambda j, n=(2 * pr + h) // 3: vav[:, j, 64 * n:64 * n + 64]) for h in range(2)],
                                 catv[:, pr, 128 * blk:128 * blk + 128], t_va, cat.w)
                ada_next()
        ada_next(12)
        t_att = now()
        ar.free(now(), *S_, *P_, *PT_, qk, kb, va, vm, Eb, swb, junk, *msb, cpad)

        dl = ar.get(2560)
        sh = ar.get(2560)
        dv = dl.v("p (n t) -> p n t", n=10)
        shv = sh.v("p (n t) -> p n t", n=10)
        t = tt(dv, pzv[:, :, 0:256], pzv[:, :, 1:257], SUB, t_pz, t_z, dl.w)
        t = tt(dv, dv, bc(col("rwkv_mu", 0, 10).unsqueeze(2), [128, 10, 256]), MUL, t)
        t_sh = tt(shv, dv, pzv[:, :, 1:257], ADD, t, sh.w)
        ar.free(now(), dl, pz)

        def v3(b):
            return b.v("p (n t) -> p n t", n=3)

        def c3(name):
            return bc(col(name, 0, 3).unsqueeze(2), [128, 3, 256])
        rT, kT_, vT = shv[:, 0:3, :], shv[:, 3:6, :], shv[:, 6:9, :]
        lt = ar.get(256)
        t1 = act(lt.ap[0:32, :], shv[0:32, 9, :], ACT.Tanh, t_sh, lt.w)
        t1 = act(lt.ap[32:64, :], shv[32:64, 9, :], ACT.Copy, t_sh, lt.w)
        t_lt = act(lt.ap[64:128, :], shv[64:128, 9, :], ACT.Sigmoid, t_sh, lt.w)
        sg, av, gg = ar.get(768), ar.get(768), ar.get(768)
        for p0, k_, dstb, f, bn in ((0, 32, sg, ACT.Sigmoid, "rwkv_w0"), (32, 32, av, ACT.Sigmoid, "rwkv_a0"), (64, 64, gg, ACT.Copy, None)):
            for i in range(3):
                b = ps.take()
                t = pe(mm(b.ap[:, 0:256], L2.ap[p0:p0 + k_, 128 * i:128 * i + 128], lt.ap[p0:p0 + k_, :], True, True), t_lt, par_tok, b.w)
                if bn:
                    t_w = act(v3(dstb)[:, i, :], b.ap[:, 0:256], f, t, dstb.w, bias=col(bn, i))
                else:
                    t_w = acp(v3(dstb)[:, i, :], b.ap[:, 0:256], t, dstb.w)
                b.w = [t_w]
        kk, tmp, rs = ar.get(768), ar.get(768), ar.get(512)
        t = tt(v3(kk), kT_, c3("rwkv_k_k"), MUL, t_sh, t_par, kk.w)
        t = tt(v3(tmp), v3(kk), v3(kk), MUL, t, tmp.w)
        t_rs = head_rstd([v3(tmp)[:, i, :] for i in range(3)], [t, *rs.w], 1.0, 0.0, rs.ap, 16, floor=1e-24)
        for i in range(3):
            b = ps.take()
            t = pe(head_bcast(b, 0, i, rs.ap), t_rs, b.w)
            t_kk = tt(v3(kk)[:, i, :], v3(kk)[:, i, :], b.ap[:, 0:256], MUL, t)
            b.w = [t_kk]
        t = ts(v3(tmp), v3(av), -1.0, ADD, None, None, t_w, VE.last(), PE.last())
        t = tt(v3(tmp), v3(tmp), c3("rwkv_k_a"), MUL, t)
        kp = ar.get(768)
        t_kp = stt(kp.ap, tmp.ap, 1.0, sh.ap[:, 768:1536], ADD, MUL, t, kp.w)
        t_b = tt(av.ap, kk.ap, av.ap, MUL, t_kk, t_kp)
        Lz = ar.get(6 * 129)
        Lv = Lz.v("p (n c t) -> p n c t", n=3, c=2)
        t_l0 = gp(lambda e: e.memset(Lv[:, :, :, 0:1], 0.0), Lz.w)
        t = ts(sg.ap, sg.ap, -math.exp(-0.5), MUL, None, None, t_w)
        for i in range(3):
            for c in range(2):
                t_L = ve(lambda e, i=i, c=c: e.tensor_tensor_scan(out=Lv[:, i, c, 1:129], data0=ones, data1=v3(sg)[:, i, 128 * c:128 * c + 128],
                                                                 initial=0.0, op0=MUL, op1=ADD), t, Lz.w)
        Lm = sml(12)
        t_lm = vcp(Lm[:, 0:6], Lv[:, :, :, 64:65].rearrange("p n c o -> p (n c o)"), t_L)
        t_nl = ts(Lm[:, 6:12], Lm[:, 0:6], -1.0, MUL, None, None, t_lm)
        E1, E2 = ar.get(6 * 129), ar.get(768)
        E1v, E2v = E1.v("p (n c t) -> p n c t", n=3, c=2), E2.v("p (n c t) -> p n c t", n=3, c=2)
        for i in range(3):
            for c in range(2):
                q = 2 * i + c
                act(E1v[:, i, c, :], Lv[:, i, c, :], ACT.Exp, t_L, t_nl, t_l0, E1.w, bias=Lm[:, 6 + q:7 + q])
                t_E = act(E2v[:, i, c, :], Lv[:, i, c, 1:129], ACT.Exp, E2.w, bias=Lm[:, q:q + 1], scale=-1.0)
        eM = sml(6)
        t_eM = act(eM, Lm[:, 0:6], ACT.Exp, t_lm)
        AR = ar.get(1536)
        ARv = AR.v("p (n c z t) -> p n c z t", n=3, c=2, z=2)

        def v4(ap):
            return ap.rearrange("p (n c t) -> p n c t", n=3, c=2)
        BK = [ar.get(768), ar.get(768)]
        for i in range(3):
            stt(ARv[:, i, :, 0, :], v4(kk.ap)[:, i, :, :], -1.0, E1v[:, i, :, 0:128], MUL, MUL, t_E, t_kk, AR.w)
            t_AR = tt(ARv[:, i, :, 1, :], v4(sh.ap[:, 0:768])[:, i, :, :], E1v[:, i, :, 1:129], MUL, AR.w)
        t_B = tt(BK[0].ap, av.ap, E2.ap, MUL, t_b, BK[0].w)
        t_K = tt(BK[1].ap, kp.ap, E2.ap, MUL, BK[1].w)
        bs = tmp
        t = tt(bs.ap, sh.ap[:, 0:768], kp.ap, MUL, t_kp, VE.last())
        t = tt(v3(bs), v3(bs), c3("rwkv_r_k"), MUL, t)
        for i in range(3):
            b = ps.take()
            t2 = pe(mm(b.ap[:, 0:256], C["bo"], v3(bs)[:, i, :], True, True), t, b.w)
            t_bon = tt(v3(bs)[:, i, :], b.ap[:, 0:256], vT[:, i, :], MUL, t2)
            b.w = [t_bon]
        VT, BT, KT_ = ar.get(768), ar.get(384), ar.get(384)
        VTv = VT.v("p (c n k) -> p c n k", c=2, n=3)
        for c in range(2):
            b = ps.take()
            t = pes([tr(b.ap[:, 128 * i:128 * i + 128], vT[:, i, 128 * c:128 * c + 128], ident) for i in range(3)], t_sh, b.w)
            t_VT = acp(VT.ap[:, 384 * c:384 * c + 384], b.ap[:, 0:384], t, VT.w)
            b.w = [t_VT]
        for src, dst, tk in ((BK[0], BT, t_B), (BK[1], KT_, t_K)):
            b = ps.take()
            t = pes([tr(b.ap[:, 128 * i:128 * i + 128], v4(src.ap)[:, i, 0, :], ident) for i in range(3)], tk, b.w)
            t_BT = acp(dst.ap, b.ap[:, 0:384], t, dst.w)
            b.w = [t_BT]
        ar.free(now(), kk, E2, Lz, sg, kp, av, lt)

        yT = ar.get(768)
        rhs_b, sa_b = ar.get(384), ar.get(384)
        st_b = ar.get(192)
        MB, MK, Xi, Zi, T1 = ar.get(1536), ar.get(1536), ar.get(768), ar.get(768), ar.get(768)
        Mt = Xi
        t_z1 = gp(lambda e: e.memset(MB.ap, 0.0), MB.w)
        t_z2 = gp(lambda e: e.memset(MK.ap, 0.0), MK.w)
        SUm, SLm = C["SU"], C["SL"]
        i32 = lambda a: a.bitcast(I32)
        su_iu = cst.ap[:, CL["SU"][0]:CL["SU"][0] + 256]
        done_prev = []
        for c in range(2):
            def h6(buf, w):
                return buf.ap.rearrange("p (h x) -> p h x", h=6)
            t_unit = []
            for h in range(6):
                i, o = h // 2, 64 * (h % 2)
                b, b2 = ps.take(), ps.take()
                ARh = ARv[o:o + 64, i, c, :, :].rearrange("p z t -> p (z t)")
                Bh, Kh = v4(BK[0].ap)[o:o + 64, i, c, :], v4(BK[1].ap)[o:o + 64, i, c, :]
                t = pes([mm(b.ap[:, 0:256], Bh, ARh, True, True), mm(b.ap[:, 256:512], Kh, ARh, True, True)], t_AR, t_B, t_K, b.w)
                ve(lambda e, h=h, b=b: e.copy_predicated(MB.ap[:, 256 * h:256 * h + 256], i32(su_iu), b.ap[:, 0:256]), t, t_z1, done_prev)
                t2 = ve(lambda e, h=h, b=b: e.copy_predicated(MK.ap[:, 256 * h:256 * h + 256], i32(su_iu), b.ap[:, 256:512]), t_z2)
                b.w = [t2]
                t = pe(mm(b2.ap[:, 0:128], ARv[o:o + 64, i, c, 0, :], Bh, True, True), b2.w)
                t3 = tt(h6(Xi, 128)[:, h, :], b2.ap[:, 0:128], C["LM"][:, 0:128], MUL, t, Xi.w, done_prev)
                b2.w = [t3]
                t4 = tt(h6(Xi, 128)[:, h, :], h6(Xi, 128)[:, h, :], ident, ADD, t3)
                t5 = tt(h6(Zi, 128)[:, h, :], h6(MB, 256)[:, h, 0:128], C["LM1T"], MUL, t2, Zi.w)
                t5 = tt(h6(Zi, 128)[:, h, :], h6(Zi, 128)[:, h, :], ident, ADD, t5)
                t_unit.append([t4, t5])
            for lv in range(1, 7):
                lm = C["LM"][:, 128 * lv:128 * lv + 128]
                for h in range(6):
                    Xh, Zh, Th = h6(Xi, 128)[:, h, :], h6(Zi, 128)[:, h, :], h6(T1, 128)[:, h, :]
                    b = ps.take()
                    t = pe(mm(b.ap[:, 0:128], h6(MB, 256)[:, h, 0:128], Xh, True, True), t_unit[h], b.w)
                    t = tt(Th, b.ap[:, 0:128], lm, MUL, t, T1.w)
                    b.w = [t]
                    b = ps.take()
                    fns = [mm(b.ap[:, 128:256], Th, Zh, True, True)]
                    if lv < 6:
                        fns.append(mm(b.ap[:, 0:128], Zh, Th, True, True))
                    t = pes(fns, t, b.w)
                    if lv < 6:
                        tt(Xh, Xh, b.ap[:, 0:128], ADD, t)
                    t2 = tt(Zh, Zh, b.ap[:, 128:256], ADD, t)
                    b.w = [t2]
                    t_unit[h] = [t2]
            rbs = [ps.take(), ps.take()]
            fns = []
            for h in range(6):
                i, o = h // 2, 64 * (h % 2)
                oc = rbs[h % 2].ap[:, 64 * i:64 * i + 64]
                if c == 1:
                    fns.append(mm(oc, ARv[o:o + 64, i, c, 0, :], st_b.ap[o:o + 64, 64 * i:64 * i + 64], True, False))
                fns.append(mm(oc, MK.ap[:, 256 * h:256 * h + 128], VTv[:, c, i, o:o + 64], c == 0, True))
            t0 = pes(fns, [x for u in t_unit for x in u], rbs[0].w, rbs[1].w, t_VT, done_prev)
            for o in range(2):
                t = acp(rhs_b.ap.rearrange("p (n o k) -> p n o k", n=3, o=2)[:, :, o, :],
                        rbs[o].ap[:, 0:192].rearrange("p (n k) -> p n k", n=3), t0, rhs_b.w, done_prev)
                rbs[o].w = [t]
            rb = ps.take()
            t = pes([mm(rb.ap[:, 64 * h:64 * h + 64], h6(Zi, 128)[:, h, :], rhs_b.ap[:, 64 * h:64 * h + 64], True, True) for h in range(6)], t, rb.w)
            t_sa = acp(sa_b.ap, rb.ap[:, 0:384], t, sa_b.w, done_prev)
            rb.w = [t_sa]
            yb = ps.take()
            fns = []
            for h in range(6):
                i, o = h // 2, 64 * (h % 2)
                oc = yb.ap[o:o + 64, 128 * i:128 * i + 128]
                if c == 1:
                    fns.append(mm(oc, st_b.ap[o:o + 64, 64 * i:64 * i + 64], ARv[o:o + 64, i, c, 1, :], True, False))
                fns.append(mm(oc, sa_b.ap[:, 64 * h:64 * h + 64], MB.ap[:, 256 * h + 128:256 * h + 256], c == 0, False))
                fns.append(mm(oc, VTv[:, c, i, o:o + 64], MK.ap[:, 256 * h + 128:256 * h + 256], False, True))
            t_y = pes(fns, t_sa, yb.w)
            t_yT = vcp(v4(yT.ap)[:, :, c, :], yb.ap[:, 0:384].rearrange("p (n t) -> p n t", n=3), t_y, yT.w)
            yb.w = [t_yT]
            if c == 0:
                sbk = ps.take()
                fns = []
                for h in range(6):
                    i, o = h // 2, 64 * (h % 2)
                    oc = sbk.ap[o:o + 64, 64 * i:64 * i + 64]
                    fns.append(mm(oc, BT.ap[:, 128 * i + o:128 * i + o + 64], sa_b.ap[:, 64 * h:64 * h + 64], True, False))
                    fns.append(mm(oc, KT_.ap[:, 128 * i + o:128 * i + o + 64], VTv[:, 0, i, o:o + 64], False, True))
                t = pes(fns, t_sa, t_BT, sbk.w)
                for i in range(3):
                    t = ts(st_b.ap[:, 64 * i:64 * i + 64], sbk.ap[:, 64 * i:64 * i + 64], E1v[:, i, 0, 128:129], MUL,
                           eM[:, 2 * i + 1:2 * i + 2], MUL, t, t_eM, st_b.w)
                sbk.w = [t]
                t_st = t
                done_prev = [t_st, t_y, t_yT]
        ar.free(now(), MB, MK, Xi, Zi, T1, rhs_b, sa_b, st_b, E1, AR, *BK, BT, KT_, VT)
        ysq = ar.get(768)
        for i in range(3):
            b = ps.take()
            t = pe(mm(b.ap[:, 0:256], C["bo"], v3(yT)[:, i, :], True, True), t_yT, b.w)
            t_c = stt(v3(yT)[:, i, :], b.ap[:, 0:256], -1.0 / 64, v3(yT)[:, i, :], MUL, ADD, t)
            b.w = [t_c]
        t = tt(ysq.ap, yT.ap, yT.ap, MUL, t_c, ysq.w)
        t_rs = head_rstd([v3(ysq)[:, i, :] for i in range(3)], [t, VE.last(), PE.last()], 64.0, 64e-5, rs.ap, 16)
        for i in range(3):
            b = ps.take()
            t = pe(head_bcast(b, 0, i, rs.ap), t_rs, b.w)
            t = tt(v3(yT)[:, i, :], v3(yT)[:, i, :], b.ap[:, 0:256], MUL, t)
            b.w = [t]
            t = ts(v3(yT)[:, i, :], v3(yT)[:, i, :], col("rwkv_ln_w", i), MUL, col("rwkv_ln_b", i), ADD, t)
        t = tt(yT.ap, yT.ap, bs.ap, ADD, t)
        t_cat2 = tt(cat.ap[:, 768:1536], yT.ap, gg.ap, MUL, t, cat.w)
        ar.free(now(), ysq, yT, rs, tmp, gg, sh, L2)

        X = ar.get(2048, True)
        x = X.v("p (b d) -> p b d", b=2)
        later(X.w, [(x, A["x"].rearrange("a (b p) d -> p (a b) d", p=128))], s_x2)
        x2_tok = (s_x2, 16)

        def token_out(chunks, act_v, use, tok, k_n=8):
            for c, ch in enumerate(chunks):
                w = ch.ap.rearrange("p (k n) -> p k n", k=8)
                for h in range(2):
                    b = ps.take()
                    t = pes([mm(b.ap, act_v[:, k, 128 * h:128 * h + 128], w[:, k, :], k == 0, k == k_n - 1)
                             for k in range(k_n)], tok, ch.tok, b.w)
                    t2 = use(c, h, b.ap, t)
                    b.w = [t2]
                ch.free = [t]
            return t2

        def add_x(c, h, bank, t):
            v = x[:, h, 512 * c:512 * c + 512]
            return tt(v, bank, v, ADD, t, x2_tok)

        t_x = token_out(ch_o, catv, add_x, [t_cat, t_cat2])
        ar.free(now(), cat)

        junk = ar.get(1024)
        Xn, hT = ar.get(2048), ar.get(2048)
        t = normed(x, t_x, Xn)
        t_h = to_features(Xn, t, hT, col("ffn_norm_g", 0, 8))
        ar.free(now(), Xn)
        hv = hT.v("p (k t) -> p k t", k=8)
        aT = ar.get(22 * 256)
        aTv = aT.v("p (k t) -> p k t", k=22)
        Uz = [ar.get(4 * 258) for _ in range(2)]
        Ub = [ar.get(1024) for _ in range(2)]
        u_free = [[], []]
        tz = []
        for u in Uz:
            tz.append(gp(lambda e, u=u: e.memset(u.v("p (n t) -> p n t", n=4)[:, :, 0:2], 0.0), u.w))
        for i in range(11):
            U, Uc = Uz[i % 2].v("p (n t) -> p n t", n=4), Ub[i % 2].v("p (n t) -> p n t", n=4)
            te = []
            for z in range(2):
                b = ps.take()
                for h in range(2):
                    t = pes(proj_fm(b, h, ch_up[i], 256, 128 * h, hv, base=2048 * z), t_h, ch_up[i].tok, b.w)
                t2 = acp(U[:, 2 * z:2 * z + 2, 2:258], b.ap.rearrange("p (n t) -> p n t", n=2), t, u_free[i % 2], Uz[i % 2].w, tz)
                b.w = [t2]
                te.append(t2)
            ch_up[i].free = [t]
            tiles = [2 * i, 2 * i + 1, 22 + 2 * i, 23 + 2 * i]
            for n, g_ in enumerate(tiles):
                t2 = act(Uc[:, n, :], U[:, n, 2:258], ACT.Identity, te[n // 2], u_free[i % 2], Ub[i % 2].w,
                         scale=col("conv_w", 88 + g_), bias=col("conv_b", g_))
                t2 = stt(Uc[:, n, :], U[:, n, 1:257], col("conv_w", 44 + g_), Uc[:, n, :], MUL, ADD, t2)
                t2 = stt(Uc[:, n, :], U[:, n, 0:256], col("conv_w", g_), Uc[:, n, :], MUL, ADD, t2)
                if n == 1:
                    tg = t2
            t3 = act(Uc[:, 0:2, :], Uc[:, 0:2, :], ACT.Silu, tg)
            t_a = tt(aTv[:, 2 * i:2 * i + 2, :], Uc[:, 0:2, :], Uc[:, 2:4, :], MUL, t3, t2, aT.w)
            u_free[i % 2] = [t_a]
        bb = [ps.take() for _ in range(4)]
        for c in range(6):
            w = ch_dn[c].ap.rearrange("p (k n) -> p k n", k=4)
            fns = []
            for k in range(4 if c < 5 else 2):
                f = 4 * c + k
                for h in range(2):
                    for q in range(2):
                        fns.append(mm(bb[2 * h + q].ap, aTv[:, f, 128 * h:128 * h + 128], w[:, k, 512 * q:512 * q + 512], f == 0, f == 21))
            t = pes(fns, t_a, ch_dn[c].tok, [b.w for b in bb])
            ch_dn[c].free = [t]
        for h in range(2):
            for q in range(2):
                t_x = add_x(q, h, bb[2 * h + q].ap, t)
                bb[2 * h + q].w = [t_x]
        ar.free(now(), aT, hT, *Uz, *Ub)
        mods = ar.get(32, True)
        t_md = stt(mods.ap[:, 0:8], modc.ap[:, 8:16], 1.0, col("norm1_g_2", 0, 8), ADD, MUL, ada_tok, mods.w)
        t_md = stt(mods.ap[:, 8:16], modc.ap[:, 24:32], 1.0, col("norm2_g_2", 0, 8), ADD, MUL)
        Xn, hT = ar.get(2048), ar.get(2048)
        t = normed(x, t_x, Xn)
        t_h = to_features(Xn, t, hT, mods.ap[:, 0:8], shift=modc.ap[:, 0:8], dtok=t_md)
        ar.free(now(), Xn)
        hv = hT.v("p (k t) -> p k t", k=8)
        Q = [ar.get(1024) for _ in range(6)]
        rt = ar.get(512)
        rt_free = []
        t_q = [None] * 6
        cosb = bc(C["cos"].unsqueeze(1), [128, 2, 256])
        sinb = bc(C["sin"].unsqueeze(1), [128, 2, 256])
        GM = ar.get(4096)
        GMv = GM.v("p (k t) -> p k t", k=16)
        rtv = rt.v("p (n t) -> p n t", n=2)
        for c in range(10):
            ch = ch_i2[c]
            if c in (2, 5):
                w = ch.ap.rearrange("p (k n) -> p k n", k=8)
                for h in range(2):
                    b = ps.take()
                    t = pes([mm(b.ap, hv[:, k, 128 * h:128 * h + 128], w[:, k, :], k == 0, k == 7) for k in range(8)], t_h, ch.tok, b.w)
                    t_q[c] = acp(Q[c].ap[:, 512 * h:512 * h + 512], b.ap, t, Q[c].w)
                    b.w = [t_q[c]]
                ch.free = [t]
                continue
            for z in range(2):
                b = ps.take()
                for h in range(2):
                    t = pes(proj_fm(b, h, ch, 512, 256 * z + 128 * h, hv), t_h, ch.tok, b.w)
                bv = b.ap.rearrange("p (n t) -> p n t", n=2)
                if c >= 6:
                    t_g = act(GMv[:, 4 * (c - 6) + 2 * z:4 * (c - 6) + 2 * z + 2, :], bv, ACT.Sigmoid, t, GM.w)
                    b.w = [t_g]
                    continue
                qv = Q[c].v("p (n t) -> p n t", n=4)[:, 2 * z:2 * z + 2, :]
                t1 = acp(qv, bv, t, Q[c].w)
                b.w = [t1]
                b = ps.take()
                t2 = pe(mm(b.ap, C["perm"], Q[c].ap[:, 512 * z:512 * z + 512], True, True), t1, b.w)
                t3 = tt(rtv, b.ap.rearrange("p (n t) -> p n t", n=2), sinb, MUL, t2, rt.w, VE.last())
                b.w = [t3]
                t4 = tt(qv, qv, cosb, MUL, t3)
                t_q[c] = tt(qv, qv, rtv, ADD, t4)
            ch.free = [t]
        ar.free(now(), hT, rt, junk)
        S_[:] = [ar.get(512) for _ in range(NB_A)]
        P_[:] = [ar.get(512) for _ in range(NB_A)]
        PT_[:] = [ar.get(512) for _ in range(NB_A)]
        a_free[:] = [[[], []] for _ in range(NB_A)]
        OM, OD = ar.get(1024), ar.get(1024)
        OMv, ODv = OM.v("p (n t) -> p n t", n=4), OD.v("p (n t) -> p n t", n=4)
        lam = sml(6)
        lv_ = lamv.v("p (a k) -> p a k", a=4)
        lt2 = ar.get(128)
        t = tt(lt2.v("p (a k) -> p a k", a=2), lamv.v("p (a z k) -> p a z k", a=2, z=2)[:, :, 0, :],
               lamv.v("p (a z k) -> p a z k", a=2, z=2)[:, :, 1, :], MUL, par_tok, lt2.w)
        t = ve(lambda e: e.tensor_reduce(lam[:, 0:2], lt2.v("p (a k) -> p a k", a=2), AX.X, ADD), t)
        t = act(lam[:, 2:4], lam[:, 0:2], ACT.Exp, t)
        t = tt(lam[:, 4:5], lam[:, 3:4], lam[:, 2:3], SUB, t)
        t_lam = ts(lam[:, 4:5], lam[:, 4:5], -LAM0, ADD, None, None, t)
        Qv = [q.v("p (n t) -> p n t", n=4) for q in Q]
        VMv, VDv = Q[2].v("p (b d) -> p b d", b=2), Q[5].v("p (b d) -> p b d", b=2)
        for pr in range(4):
            for blk in range(2):
                nk = 1 + blk
                r = attn_scores([hrow(Qv[0][:, pr, :], h) for h in range(2)], [hrow(Qv[1][:, pr, :], h) for h in range(2)],
                                blk, nk, causal(nk), [t_q[0], t_q[1]])
                t_om = attn_out(*r, nk, [(lambda j, h=2 * pr + h: VMv[:, j, 64 * h:64 * h + 64]) for h in range(2)],
                                OMv[:, pr, 128 * blk:128 * blk + 128], t_q[2], OM.w)
                i, pv, rc, t5, w = attn_scores([hrow(Qv[3][:, pr, :], h) for h in range(2)], [hrow(Qv[4][:, pr, :], h) for h in range(2)],
                                               blk, nk, causal(nk), [t_q[3], t_q[4]])
                P, PT = P_[i], PT_[i]
                t6 = ts(pv[:, 1, :], pv[:, 1, :], rc[:, 1:2], MUL, lam[:, 4:5], MUL, t5, t_lam)
                t6 = stt(pv[:, 0, :], pv[:, 0, :], rc[:, 0:1], pv[:, 1, :], MUL, ADD, t6)
                b = ps.take()
                t7 = pes([tr(b.ap[:, 128 * j:128 * j + 128], pv[:, 0, 128 * j:128 * j + 128], ident) for j in range(nk)], t6, b.w)
                t8 = acp(PT.ap[:, 0:w], b.ap[:, 0:w], t7, a_free[i][1], PT.w)
                b.w = [t8]
                b = ps.take()
                t9 = pes([mm(b.ap[:, 0:128], VDv[:, j, 128 * pr:128 * pr + 128], PT.ap[:, 128 * j:128 * j + 128], j == 0, j == nk - 1)
                          for j in range(nk)], t8, t_q[5], b.w)
                t_od = acp(ODv[:, pr, 128 * blk:128 * blk + 128], b.ap[:, 0:128], t9, OD.w)
                b.w = [t_od]
                a_free[i] = [[t7, t6], [t9]]
        ar.free(now(), *S_, *P_, *PT_, *Q, lt2, lamv)
        sq, rs = ar.get(1024), ar.get(512)
        g8 = sml(1)
        t8 = ts(g8, col("diff_subln_g_2"), 1.0 - LAM0, MUL, None, None, t_par)
        t = tt(sq.ap, OD.ap, OD.ap, MUL, t_od, sq.w)
        t_rs = head_rstd([sq.ap[:, 256 * i:256 * i + 256] for i in range(4)], [t, *rs.w], 128.0, 1e-6, rs.ap, 16, sel="hs2")
        for i in range(4):
            b = ps.take()
            t = pe(head_bcast(b, 0, i, rs.ap), t_rs, b.w)
            t_od = stt(ODv[:, i, :], ODv[:, i, :], g8, b.ap[:, 0:256], MUL, MUL, t, t8)
            b.w = [t_od]
        ar.free(now(), sq, rs)
        mg = ar.get(2048)
        mgv = mg.v("p (k t) -> p k t", k=8)
        for ch, src, z, tk in ((ch_pm, OMv, 0, t_om), (ch_pd, ODv, 8, t_od)):
            for n in range(0, 8, 2):
                b = ps.take()
                for h in range(2):
                    t = pes(proj_fm(b, h, ch, 1024, 128 * (n + h), src, k_n=4), tk, ch.tok, b.w)
                bv = b.ap.rearrange("p (n t) -> p n t", n=2)
                gv = GMv[:, z + n:z + n + 2, :]
                if z == 0:
                    t_mg = tt(mgv[:, n:n + 2, :], bv, gv, MUL, t, t_g, mg.w)
                    b.w = [t_mg]
                else:
                    t2 = tt(gv, bv, gv, MUL, t, t_g)
                    b.w = [t2]
                    t_mg = tt(mgv[:, n:n + 2, :], mgv[:, n:n + 2, :], gv, ADD, t2)
            ch.free = [t]

        ar.free(now(), GM, OM, OD)
        gt = ar.get(512, True)

        def add_gated(gb):
            def f(c, h, bank, t):
                v = x[:, h, 512 * c:512 * c + 512]
                t = tt(gt.ap, bank, gb.ap[:, 512 * c:512 * c + 512], MUL, t, gt.w, VE.last() if cur["ve"] is VE else None)
                tt(v, v, gt.ap, ADD, t)
                return cur["ve"].last()
            return f
        t_x = token_out(ch_o2, mgv, add_gated(g1b), [t_mg, ada_tok])
        ar.free(now(), mg, g1b)
        junk = ar.get(1024)
        w36, b36 = ar.get(288), ar.get(36)
        w36v = w36.v("p (k n) -> p k n", k=8)
        later([*w36.w, *b36.w], [
            (w36v[:, :, 0:4], A["w_group_2"][0, :, :].rearrange("(k p) n -> p k n", p=128)),
            (w36v[:, :, 4:36], A["w_expert_2"][0, :, :].rearrange("(k p) n -> p k n", p=128)),
            (b36.ap[:, 0:4], bc(A["b_group_2"], [128, 4])), (b36.ap[:, 4:36], bc(A["b_expert_2"], [128, 32]))], s_rt)
        X2, hT = ar.get(2048, True), ar.get(2048)
        t = normed(x, t_x, X2)
        t_x2 = t
        t_h = to_features(X2, t, hT, mods.ap[:, 8:16], shift=modc.ap[:, 16:24], dtok=t_md)
        hv = hT.v("p (k t) -> p k t", k=8)
        b = ps.take()
        t = pes([mm(b.ap[:, 36 * h:36 * h + 36], hv[:, k, 128 * h:128 * h + 128], w36v[:, k, :], k == 0, k == 7)
                 for h in range(2) for k in range(8)], t_h, (s_rt, 64), b.w)
        lg = ar.get(72)
        lgv = lg.v("p (b n) -> p b n", b=2)
        t_lg = tt(lgv, b.ap[:, 0:72].rearrange("p (b n) -> p b n", b=2), bc(b36.ap[:, 0:36].unsqueeze(1), [128, 2, 36]), ADD, t, lg.w)
        b.w = [t_lg]
        R = ar.get(640)
        ro = [0]

        def rget(n, pat="p (b n) -> p b n"):
            o = ro[0]
            ro[0] += 2 * n
            return R.ap[:, o:o + 2 * n].rearrange(pat, b=2)

        def chain(f, *w):
            return ve(f, VE.last(), *w)

        def first_max(src, n, key, dst, mx):
            kt_ = rget(n)
            chain(lambda e: e.tensor_reduce(mx, src, AX.X, MAX), t_lg, R.w)
            chain(lambda e: e.tensor_tensor(kt_, src, bc(mx, [128, 2, n]), EQ))
            chain(lambda e: e.tensor_tensor(kt_, kt_, bc(key.unsqueeze(1), [128, 2, n]), MUL))
            km = rget(1)
            chain(lambda e: e.tensor_reduce(km, kt_, AX.X, MAX))
            return chain(lambda e: e.tensor_tensor(dst, kt_, bc(km, [128, 2, n]), EQ))

        def softmax_parts(src, mx, n):
            nm, ee, zz = rget(1), rget(n), rget(1)
            t = chain(lambda e: e.tensor_scalar(nm, mx, -1.0, None, MUL))
            for i in range(2):
                t = act(ee[:, i, :], src[:, i, :], ACT.Exp, t, SC.last(), bias=nm[:, i, :], accum=zz[:, i, :])
            chain(lambda e: e.reciprocal(zz, zz), t)
            return ee, zz
        mxg, ohg = rget(1), rget(4)
        first_max(lgv[:, :, 0:4], 4, C["key4"], ohg, mxg)
        _, gw = softmax_parts(lgv[:, :, 0:4], mxg, 4)
        em = rget(32)
        of = rget(4)
        chain(lambda e: e.tensor_scalar(of, ohg, -1.0, -NEG, ADD, MUL))
        for i in range(2):
            v8 = em[:, i, :].rearrange("p (g n) -> p g n", g=4)
            chain(lambda e, i=i, v8=v8: e.tensor_tensor(v8, lgv[:, i, 4:36].rearrange("p (g n) -> p g n", g=4), bc(ohg[:, i, :].unsqueeze(2), [128, 4, 8]), MUL))
            chain(lambda e, i=i, v8=v8: e.tensor_tensor(v8, v8, bc(of[:, i, :].unsqueeze(2), [128, 4, 8]), ADD))
        mx1, oh1 = rget(1), rget(32)
        first_max(em, 32, C["key32"], oh1, mx1)
        ee, zz = softmax_parts(em, mx1, 32)
        chain(lambda e: e.tensor_tensor(ee, ee, bc(zz, [128, 2, 32]), MUL))
        chain(lambda e: e.scalar_tensor_tensor(out=em, in0=oh1, scalar=NEG, in1=em, op0=MUL, op1=ADD))
        mx2, oh2 = rget(1), rget(32)
        first_max(em, 32, C["key32"], oh2, mx2)
        RK = ar.get(192, True)
        Aa, Ww, rk = (RK.ap[:, 64 * i:64 * i + 64].rearrange("p (b n) -> p b n", b=2) for i in range(3))
        chain(lambda e: e.tensor_tensor(Aa, oh1, oh2, ADD), RK.w)
        chain(lambda e: e.tensor_tensor(Ww, Aa, ee, MUL))
        tot = rget(1)
        chain(lambda e: e.tensor_reduce(tot, Ww, AX.X, ADD))
        chain(lambda e: e.reciprocal(tot, tot))
        chain(lambda e: e.tensor_tensor(tot, tot, gw, MUL))
        t_ww = chain(lambda e: e.tensor_tensor(Ww, Ww, bc(tot, [128, 2, 32]), MUL))
        b = ps.take()
        t = pes([mm(b.ap[:, 0:32], C["SU"], Aa[:, 0, :], True, True), mm(b.ap[:, 32:64], ones, Aa[:, 0, :], True, False),
                 mm(b.ap[:, 32:64], C["SU"], Aa[:, 1, :], False, True), mm(b.ap[:, 64:96], ones, Aa[:, 0, :], True, False),
                 mm(b.ap[:, 64:96], ones, Aa[:, 1, :], False, True)], t_ww, b.w)
        cntf, cnti = sml(1), sml(1)
        chain(lambda e, b=b: e.tensor_reduce(cntf, b.ap[:, 64:96], AX.X, MAX), t)
        t_cnt = chain(lambda e: e.tensor_copy(cnti.bitcast(I32), cntf))
        chain(lambda e, b=b: e.scalar_tensor_tensor(out=rk, in0=b.ap[:, 0:64].rearrange("p (b n) -> p b n", b=2), scalar=1.0, in1=Aa, op0=ADD, op1=MUL))
        t_rk = chain(lambda e: e.tensor_scalar(rk, rk, -1.0, None, ADD))
        b.w = [t_rk]
        ar.free(now(), hT, w36, b36, lg, R, junk)
        xg = [ar.get(4096), ar.get(4096)]
        Pb, PwT = ar.get(2048), ar.get(2048)
        sgl, hh, hts, ost = ([ar.get(n) for _ in range(2)] for n in (256, 256, 128, 1024))
        g_ps = psum

        def moe_round(chs, start, first):
            Pv = Pb.v("p (b e s) -> p b e s", b=2, e=32)
            xgv = [g.v("p (k s) -> p k s", k=8) for g in xg]
            X2v = X2.v("p (b d) -> p b d", b=2)
            bw = {i: [] for i in range(8)}
            tk = start
            if not first:
                tk = ts(rk, rk, -float(NSLOT), ADD, None, None, tk)
            for i in range(2):
                tP = tt(Pv[:, i, :, :], bc(rk[:, i, :].unsqueeze(2), [128, 32, 32]), bc(C["iota"].unsqueeze(1), [128, 32, 32]), EQ,
                        tk, start, Pb.w)
            bi = [0]

            def nb():
                r = 4 + bi[0] % 4
                bi[0] += 1
                return r
            t_xg = [None, None]

            def gather(half):
                for k in range(8):
                    q = nb()
                    t = pes([mm(g_ps[q][:, :], X2v[:, i, 128 * k:128 * k + 128], Pv[:, i, 16 * half:16 * half + 16, :].rearrange("p e s -> p (e s)"),
                                i == 0, i == 1) for i in range(2)], tP, start, bw[q])
                    o = xgv[half][:, k, :]
                    if k % 2:
                        t = ts(o, g_ps[q][:, :], mods.ap[:, 8 + k:9 + k], MUL, modc.ap[:, 16 + k:17 + k], ADD, t, start, xg[half].w)
                    else:
                        t = act(o, g_ps[q][:, :], ACT.Identity, t, start, xg[half].w, scale=mods.ap[:, 8 + k:9 + k], bias=modc.ap[:, 16 + k:17 + k])
                    bw[q] = [t]
                    t_xg[half] = (t_xg[half] or []) + [t]
            gather(0)
            gather(1)
            t_pw = []
            for i in range(2):
                tw = tt(Pv[:, i, :, :], Pv[:, i, :, :], bc(Ww[:, i, :].unsqueeze(2), [128, 32, 32]), MUL, tP, cur["pe"].last())
                for g4 in range(0, 8, 4):
                    q = nb()
                    t = pes([tr(g_ps[q][:, 128 * z:128 * z + 128], Pb.ap[:, 1024 * i + 128 * (g4 + z):1024 * i + 128 * (g4 + z) + 128], ident) for z in range(4)], tw, bw[q])
                    t = acp(PwT.v("p (g t) -> p g t", g=8)[:, g4:g4 + 4, 128 * i:128 * i + 128],
                            g_ps[q][:, :].rearrange("p (g t) -> p g t", g=4), t, PwT.w, start)
                    bw[q] = [t]
                    t_pw.append(t)
            PwTv = PwT.v("p (g t) -> p g t", g=8)
            fre = {"sg": [[], []], "hh": [[], []], "ht": [[], []], "os": [[], []]}
            t_gu, t_hh, t_ost = {}, {}, {}

            def gate_up(e):
                q = 4 + e % 2
                cg, cu = chs[e][0], chs[e][1]
                wg = cg.ap.rearrange("p (k n) -> p k n", k=8)
                wu = cu.ap.rearrange("p (k n) -> p k n", k=8)
                fns = []
                for k in range(8):
                    for j in range(4):
                        w = (wg if j < 2 else wu)[:, k, 256 * (j % 2):256 * (j % 2) + 256]
                        fns.append(mm(g_ps[q][32 * j:32 * j + 32, 0:256], xgv[e // 16][:, k, 32 * (e % 16):32 * (e % 16) + 32], w, k == 0, k == 7))
                t = pes(fns, t_xg[e // 16], cg.tok, cu.tok, bw[q])
                cg.free = cu.free = [t]
                i = e % 2
                t1 = act(sgl[i].ap[0:64, :], g_ps[q][0:64, 0:256], ACT.Silu, t, sgl[i].w, fre["sg"][i])
                t2 = tt(hh[i].ap[0:64, :], g_ps[q][64:128, 0:256], sgl[i].ap[0:64, :], MUL, t1, hh[i].w, fre["hh"][i])
                bw[q] = [t2]
                fre["sg"][i] = [t2]
                t_hh[e] = t2

            def down(e):
                i = e % 2
                t = pes([tr(g_ps[6][:, 64 * c:64 * c + 64], hh[i].ap[0:64, 128 * c:128 * c + 128], ident[0:64, 0:64]) for c in range(2)],
                        t_hh[e], bw[6])
                fre["hh"][i] = [t]
                t = acp(hts[i].ap, g_ps[6][:, 0:128], t, hts[i].w, fre["ht"][i])
                bw[6] = [t]
                cd = chs[e][2]
                wd = cd.ap.rearrange("p (k n) -> p k n", k=4)
                fns = []
                for f in range(4):
                    o = 64 * (f % 2) + 32 * (f // 2)
                    for j in range(4):
                        fns.append(mm(g_ps[7][32 * j:32 * j + 32, 0:256], hts[i].ap[:, o:o + 32], wd[:, f, 256 * j:256 * j + 256], f == 0, f == 3))
                t = pes(fns, t, cd.tok, bw[7])
                cd.free = [t]
                fre["ht"][i] = [t]
                g, r = e // 4, 32 * (e % 4)
                o = ost[g % 2]
                tw = []
                for j in range(4):
                    d, s_ = o.ap[r:r + 32, 256 * j:256 * j + 256], g_ps[7][32 * j:32 * j + 32, 0:256]
                    tw.append((acp if j % 2 else vcp)(d, s_, t, o.w, fre["os"][g % 2]))
                bw[7] = tw
                t_ost.setdefault(g, []).extend(tw)

            def combine(g):
                t = pes([mm(g_ps[2 * b_ + h_][:, :], PwTv[:, g, 128 * b_:128 * b_ + 128], ost[g % 2].ap[:, 512 * h_:512 * h_ + 512], g == 0, g == 7)
                         for b_ in range(2) for h_ in range(2)], t_ost[g], t_pw, start)
                fre["os"][g % 2] = [t]
                return t
            gate_up(0)
            for e in range(NE):
                if e + 1 < NE:
                    gate_up(e + 1)
                if e % 4 == 1 and e > 4:
                    combine(e // 4 - 1)
                down(e)
            t = combine(7)
            for h_ in range(2):
                for b_ in range(2):
                    v = x[:, b_, 512 * h_:512 * h_ + 512]
                    t1 = tt(gt.ap, g_ps[2 * b_ + h_][:, :], g2b.ap[:, 512 * h_:512 * h_ + 512], MUL, t, gt.w, cur["ve"].last())
                    t1 = tt(v, v, gt.ap, ADD, t1)
            return t1
        t_x = moe_round(ch_e, [*now(), t_rk], True)
        main_end = now()
        LP = {"pe": Lane(sem("l_pe")), "ve": Lane(sem("l_ve")), "sc": Lane(sem("l_sc")), "gp": Lane(sem("l_gp"))}
        ring2 = Ring([ringt[:, i, :] for i in range(NS)], [sem(f"l_ring{i}") for i in range(NS)])
        cur.update(LP)
        for bf in (Pb, PwT, *xg, *sgl, *hh, *hts, *ost, gt):
            bf.w = []
        ch_e2 = [load_expert(ring2, e) for e in range(NE)]
        moe_round(ch_e2, [], False)
        FN = {"pe": Lane(sem("f_pe")), "ve": Lane(sem("f_ve")), "sc": Lane(sem("f_sc")), "gp": Lane(sem("f_gp"))}
        cur.update(FN)
        s, r = sml(2), sml(2)
        for i in range(2):
            t1 = act(xg[0].ap[:, 1024 * i:1024 * i + 1024], x[:, i, :], ACT.Square, accum=s[:, i:i + 1])
        t2 = ts(r, s, 1.0 / 1024, MUL, 1e-6, ADD, t1)
        t3 = ve(lambda e: e.reciprocal(s, r), t2)
        t3 = act(r, s, ACT.Sqrt, t3)
        for i in range(2):
            t_fin = stt(x[:, i, :], x[:, i, :], r[:, i:i + 1], Pb.ap[:, 0:1024], MUL, MUL, t3, (s_fg, 16))
        block = ctx.enter_context(nc.Block())


        def rounds(eng, body, me):
            n = eng.value_load(cnti[0:1, 0:1].bitcast(mybir.dt.int32), min_val=0, max_val=256)
            with eng.If(n > NSLOT):
                with eng.Fori(NSLOT, n, NSLOT):
                    body(eng)
                    if me is None:
                        for k in ("pe", "ve", "sc"):
                            eng.wait_ge(*LP[k].last())
                        eng.wait_ge(s_done2, 3)
                        for k in ("pe", "ve", "sc"):
                            eng.sem_clear(LP[k].sem)
                        for q in ring2.sems:
                            eng.sem_clear(q)
                        eng.sem_clear(s_done2)
                        for q in s_go[0:3]:
                            eng.sem_inc(q, 1)
                    else:
                        eng.sem_inc(s_done2, 1)
                        eng.wait_ge(s_go[me], 1)
                        eng.sem_clear(s_go[me])

        @block.sync
        def _(e):
            ring.play(e)
            for w in main_end:
                e.wait_ge(*w)
            rounds(e, ring2.play, None)
            e.dma_start(Pb.ap[:, 0:1024], A["final_g_2"].rearrange("(a d) -> a d", a=1).to_broadcast([128, 1024])).then_inc(s_fg, 16)
            e.wait_ge(*t_fin)
            e.dma_start(out.rearrange("a (b p) d -> p (a b) d", p=128), x).then_inc(s_out, 16)
            e.wait_ge(s_out, 16)

        def compute(e, lane, k, me):
            lane.play(e)
            for w in main_end:
                e.wait_ge(*w)
            rounds(e, LP[k].play, me)
            FN[k].play(e)

        @block.scalar
        def _(e):
            load_first(e)
            compute(e, SC, "sc", 0)

        @block.vector
        def _(e):
            compute(e, VE, "ve", 1)

        @block.gpsimd
        def _(e):
            pdma(e, plist2, s_par2)
            GP.play(e)

        @block.tensor
        def _(e):
            compute(e, PE, "pe", 2)


_INS = ["x", "mem", "rel_bias", "mix_norm_g", "w_in", "attn_q_norm", "attn_k_norm", "attn_sinks", "rwkv_mu", "rwkv_w0",
        "rwkv_w2", "rwkv_a0", "rwkv_a2", "rwkv_g2", "rwkv_k_k", "rwkv_k_a", "rwkv_r_k", "rwkv_ln_w", "rwkv_ln_b",
        "mem_norm_g", "w_mem_kv", "mem_q_norm", "mem_k_norm", "w_out", "ffn_norm_g", "w_up", "conv_w", "conv_b", "w_down",
        "c_2", "w_ada_2", "b_ada_2", "norm1_g_2", "w_in_2", "lambda_q1_2", "lambda_k1_2", "lambda_q2_2", "lambda_k2_2",
        "diff_subln_g_2", "w_proj_moba_2", "w_proj_diff_2", "w_out_2", "norm2_g_2", "w_group_2", "b_group_2", "w_expert_2",
        "b_expert_2", "w_gate_2", "w_up_2", "w_down_2", "final_g_2"]


def kernel(**inputs):
    import concourse.bacc as bacc
    from concourse.bass_utils import run_bass_kernel_spmd

    nc = bacc.Bacc("TRN2", target_bir_lowering=False, num_devices=1)
    arrays, aps = {}, {}
    named = [(n, np.ascontiguousarray(inputs[n])) for n in _INS] + [("consts", const_table())]
    for name, a in named:
        arrays[f"in_{name}"] = a
        aps[name] = nc.dram_tensor(f"in_{name}", a.shape, mybir.dt.from_np(a.dtype), kind="ExternalInput").ap()
    out = nc.dram_tensor("out_0", (1, T, D), mybir.dt.float32, kind="ExternalOutput").ap()
    block_kernel(nc, aps, out)
    r = run_bass_kernel_spmd(nc, [arrays], core_ids=[0])
    return r.results[0]["out_0"]
```

```python
import math

import numpy as np

import concourse.bass as bass
from concourse import mybir

T = 256
D = 1024
KT = 8
NEG = -1.0e30
LAM0 = 0.8 - 0.6 * math.exp(-0.3 * 0)
NSLOT = 32
NE = 32


def const_layout():
    names = [("ident", 128), ("bo", 128), ("ones", 128), ("perm", 128), ("rev", 128), ("cos", 256), ("sin", 256),
             ("caus", 128), ("SU", 128), ("IU", 128), ("SL", 128), ("LM", 7 * 128), ("LM1T", 128),
             ("iota", 32), ("key4", 4), ("key32", 32), ("hs", 30), ("hs2", 30), ("OHB", 1024), ("MR", 384)]
    at, off = {}, 0
    for n, w in names:
        at[n] = (off, w)
        off += w
    return at, off


def const_table():
    at, width = const_layout()
    c = np.zeros((128, width), np.float32)

    def put(name, a, rows=128):
        o, w = at[name]
        c[:rows, o:o + w] = a

    p = np.arange(128)
    t, j = p[:, None], p[None, :]
    put("ident", np.eye(128))
    put("rev", np.eye(128)[::-1])
    put("bo", (t // 64 == j // 64))
    put("ones", 1.0)
    pm = np.zeros((128, 128), np.float32)
    for o in range(128):
        if o % 64 < 32:
            pm[o + 32, o] = -1.0
        else:
            pm[o - 32, o] = 1.0
    put("perm", pm)
    inv = (1.0 / (np.float32(10000.0) ** (np.arange(0, 64, 2, dtype=np.float32) / np.float32(64)))).astype(np.float32)
    ang = (np.arange(T, dtype=np.float32)[:, None] * inv[None, :]).astype(np.float32)
    put("cos", np.cos(ang).astype(np.float32).T[p % 32])
    put("sin", np.sin(ang).astype(np.float32).T[p % 32])
    put("caus", np.where(j > t, NEG, 0.0))
    put("SU", t < j)
    put("IU", t <= j)
    put("SL", j < t)
    lm = [((t // (2 * s) == j // (2 * s)) & (t % (2 * s) >= s) & (j % (2 * s) < s)) for s in (1, 2, 4, 8, 16, 32, 64)]
    put("LM", np.concatenate(lm, 1))
    put("LM1T", lm[0].T)
    put("iota", np.arange(32)[None, :])
    put("key4", 8 - np.arange(4)[None, :])
    put("key32", 64 - np.arange(32)[None, :])
    hs = np.zeros((128, 30), np.float32)
    hs[:64, 14] = 1
    hs[64:, 15] = 1
    put("hs", hs)
    h2 = np.zeros((128, 30), np.float32)
    h2[:, 14:16] = 1
    put("hs2", h2)
    m = np.arange(384)
    dist = 255 - m
    ok = (dist >= 0) & (dist < 128)
    d = np.maximum(dist, 1).astype(np.float32)
    large = 16 + (np.log(d / np.float32(16)) / np.float32(math.log(8)) * np.float32(16)).astype(np.int32)
    bucket = np.where(dist < 16, np.maximum(dist, 0), np.minimum(large, 31))
    ob = np.zeros((128, 1024), np.float32)
    ob[64:96, 0:384] = (np.arange(32)[:, None] == bucket[None, :]) & ok[None, :]
    ob[0:16] = np.arange(16)[:, None] == np.arange(1024)[None, :] // 64
    put("OHB", ob)
    put("MR", np.where(ok, 0.0, NEG)[None, :].repeat(6, 0), 6)
    return c


PARAMS = [("mix_norm_g", 8), ("mem_norm_g", 8), ("ffn_norm_g", 8), ("norm1_g_2", 8), ("norm2_g_2", 8), ("c_2", 8),
          ("rwkv_mu", 10), ("rwkv_w0", 3), ("rwkv_a0", 3), ("rwkv_k_k", 3), ("rwkv_k_a", 3), ("rwkv_r_k", 3),
          ("rwkv_ln_w", 3), ("rwkv_ln_b", 3), ("diff_subln_g_2", 1),
          ("attn_q_norm", 1), ("attn_k_norm", 1), ("mem_q_norm", 1), ("mem_k_norm", 1),
          ("", 44), ("b_ada_2", 48), ("conv_b", 44), ("conv_w", 132)]


class Lane:

    def __init__(self, sem):
        self.sem, self.n, self.items = sem, 0, []

    def op(self, fn, *waits):
        self.n += 1
        self.items.append((fn, waits))
        return (self.sem, self.n)

    def job(self, fn, *waits):
        self.items.append((fn, waits))

    def last(self):
        return (self.sem, self.n)

    def play(self, eng):
        seen = {}

        def wait(w):
            if w is None:
                return
            if isinstance(w, list):
                for x in w:
                    wait(x)
                return
            sem, v = w
            if v > 0 and seen.get(id(sem), 0) < v:
                eng.wait_ge(sem, v)
                seen[id(sem)] = v

        for fn, waits in self.items:
            for w in waits:
                wait(w)
            r = fn(eng)
            if r is not None:
                r.then_inc(self.sem, 1)


class Bank:
    def __init__(self, ap):
        self.ap, self.w = ap, []


class Banks:

    def __init__(self, banks):
        self.all = banks
        self.pool = Pool(banks)

    def take(self):
        return self.pool.take()


class Pool:
    def __init__(self, banks):
        self.banks, self.i = list(banks), 0

    def take(self):
        self.i += 1
        return self.banks[(self.i - 1) % len(self.banks)]


def interleave(ps, lead, others):
    lead_gen, lead_banks = lead
    pools = [(g, Pool([ps.all[i] for i in b]), n) for g, b, n in others]
    lead_pool = Pool([ps.all[i] for i in lead_banks])

    def step(g, pool):
        ps.pool = pool
        try:
            next(g)
            return True
        except StopIteration:
            return False
    alive = True
    credit = [0.0] * len(pools)
    while alive or pools:
        if alive:
            alive = step(lead_gen, lead_pool)
        for q, (_, _, n) in enumerate(pools):
            credit[q] += n if alive else 1.0
        keep, kc = [], []
        for q, (g, pool, n) in enumerate(pools):
            ok = True
            while ok and credit[q] >= 1.0:
                credit[q] -= 1.0
                ok = step(g, pool)
            if ok:
                keep.append((g, pool, n))
                kc.append(credit[q])
            else:
                lead_pool.banks += pool.banks
        pools, credit = keep, kc
    ps.pool = Pool(ps.all)


class Chunk:
    def __init__(self, ring, slot, parts, sem, value, before):
        self.ring, self.slot, self.parts, self.sem, self.tok, self.before, self.free = ring, slot, parts, sem, (sem, value), before, None

    @property
    def ap(self):
        return self.ring.aps[self.slot]


class Ring:

    def __init__(self, aps, sems):
        self.aps, self.sems, self.counts, self.chunks = aps, sems, [0] * len(aps), []
        self.order, self.at, self.lent = list(range(len(aps))), 0, {}
        self.holder = [None] * len(aps)

    def use(self, slots):
        self.order, self.at = slots, 0

    def load(self, *parts):
        s = self.order[self.at % len(self.order)]
        self.at += 1
        before = self.holder[s]
        self.counts[s] += 16 * len(parts)
        c = Chunk(self, s, parts, self.sems[s], self.counts[s], before)
        self.chunks.append(c)
        self.holder[s] = c
        return c

    def play(self, eng):
        for c in self.chunks:
            if c.before is not None:
                if c.before.free is None:
                    break
                for w in c.before.free:
                    eng.wait_ge(*w)
            else:
                for w in self.lent.get(c.slot, []):
                    eng.wait_ge(*w)
            for dst, src in c.parts:
                eng.dma_start(dst(c.ap), src).then_inc(c.sem, 16)


class Arena:

    def __init__(self, ap, width):
        self.ap, self.regions, self.top = ap, [[0, width, []]], 0

    def get(self, n, high=False):
        if high:
            for r in reversed(self.regions):
                if r[1] >= n:
                    r[1] -= n
                    b = Buf(self.ap[:, r[0] + r[1]:r[0] + r[1] + n], r[0] + r[1], n, list(r[2]))
                    if r[1] == 0:
                        self.regions.remove(r)
                    return b
        best = None
        for r in self.regions:
            if r[1] >= n and (best is None or r[1] < best[1]):
                best = r
        if best is None:
            raise ValueError(f"arena full: {n} of {self.regions}")
        b = Buf(self.ap[:, best[0]:best[0] + n], best[0], n, list(best[2]))
        best[0] += n
        best[1] -= n
        self.top = max(self.top, b.off + n)
        if best[1] == 0:
            self.regions.remove(best)
        return b

    def free(self, tokens, *bufs):
        for b in bufs:
            self.regions.append([b.off, b.n, list(tokens)])
        self.regions.sort(key=lambda r: r[0])
        out = []
        for r in self.regions:
            if out and out[-1][0] + out[-1][1] == r[0]:
                out[-1][1] += r[1]
                top = {}
                for s, v in out[-1][2] + r[2]:
                    top[id(s)] = (s, max(v, top.get(id(s), (s, 0))[1]))
                out[-1][2] = list(top.values())
            else:
                out.append([r[0], r[1], list(r[2])])
        self.regions = out


class Buf:
    def __init__(self, ap, off, n, w):
        self.ap, self.off, self.n, self.w, self.home = ap, off, n, w, None

    def v(self, pat, **k):
        return self.ap.rearrange(pat, **k)


def block_kernel(nc, A, out):
    from contextlib import ExitStack
    F = mybir.dt.float32
    I32 = mybir.dt.int32
    ALU = mybir.AluOpType
    ACT = mybir.ActivationFunctionType
    AX = mybir.AxisListType
    MUL, ADD, SUB, MAX, EQ = ALU.mult, ALU.add, ALU.subtract, ALU.max, ALU.is_equal
    NS = 6
    CL, CW = const_layout()
    NSEG = 28632

    ctx = ExitStack()
    with ctx:
        def sb(name, shape, dt=F):
            return ctx.enter_context(nc.sbuf_tensor(name, shape, dt))

        def sem(name):
            return ctx.enter_context(nc.semaphore(name))

        ringt = sb("ringt", [128, NS, 4096])
        arena_t = sb("arena", [128, NSEG])
        psum = [ctx.enter_context(nc.psum_tensor(f"ps{i}", [128, 512], F)) for i in range(8)]
        scratch = nc.dram_tensor("bias_scratch", [6, 384], F, kind="Internal")

        ar = Arena(arena_t, NSEG)
        ar2 = Arena(ringt[:, 3:6, :].rearrange("p a n -> p (a n)"), 3 * 4096)

        def rbuf(n):
            for a in (ar2, ar):
                if any(r[1] >= n for r in a.regions):
                    b = a.get(n)
                    b.home = a
                    return b
            return ar.get(n)

        def rfree(*bufs):
            for b in bufs:
                b.home.free(now(), b)
        PE, VE, SC, GP = Lane(sem("s_pe")), Lane(sem("s_ve")), Lane(sem("s_sc")), Lane(sem("s_gp"))
        ring = Ring([ringt[:, i, :] for i in range(NS)] + [None], [sem(f"s_ring{i}") for i in range(NS + 1)])
        s_par = sem("s_par")
        s_par2 = sem("s_par2")
        s_x = sem("s_x")
        s_cst = sem("s_cst")
        s_bias = sem("s_bias")
        s_out = sem("s_out")
        s_gb = sem("s_gb")
        s_rt = sem("s_rt")
        s_fg = sem("s_fg")
        s_x2 = sem("s_x2")
        s_done, s_done2 = sem("s_done"), sem("s_done2")
        s_go = [sem(f"s_go{i}") for i in range(4)]

        def later(waits, parts, sm):
            def run(e):
                for d, s_ in parts:
                    e.dma_start(d, s_).then_inc(sm, 16)
                return None
            GP.job(run, waits)
        ps = Banks([Bank(p[:, :]) for p in psum])
        cur = {"pe": PE, "ve": VE, "sc": SC, "gp": GP}

        def pe(fn, *w):
            return cur["pe"].op(fn, *w)

        def ve(fn, *w):
            return cur["ve"].op(fn, *w)

        def sc(fn, *w):
            return cur["sc"].op(fn, *w)

        def gp(fn, *w):
            return cur["gp"].op(fn, *w)

        def now():
            return [PE.last(), VE.last(), SC.last(), GP.last()]

        def tt(o, a, b, op, *w):
            return ve(lambda e: e.tensor_tensor(o, a, b, op), *w)

        def ts(o, a, s1, op0, s2, op1, *w):
            if s2 is None:
                return ve(lambda e: e.tensor_scalar(o, a, s1, None, op0), *w)
            return ve(lambda e: e.tensor_scalar(o, a, s1, s2, op0, op1), *w)

        def stt(o, a, s, b, op0, op1, *w):
            return ve(lambda e: e.scalar_tensor_tensor(out=o, in0=a, scalar=s, in1=b, op0=op0, op1=op1), *w)

        def vcp(o, a, *w):
            return ve(lambda e: e.tensor_copy(o, a), *w)

        def act(o, a, f, *w, bias=0.0, scale=1.0, accum=None):
            if accum is None:
                return sc(lambda e: e.activation(o, a, f, bias=bias, scale=scale), *w)
            return sc(lambda e: e.activation(o, a, f, bias=bias, scale=scale, accum_out=accum), *w)

        def acp(o, a, *w):
            return sc(lambda e: e.activation(o, a, ACT.Copy), *w)

        def mm(o, l, r, start, stop):
            return lambda e: e.matmul(o, l, r, start=start, stop=stop, skip_group_check=True)

        def tr(o, i, ident):
            return lambda e: e.transpose(o, i, ident)

        def pes(fns, *w):
            def run(e):
                for f in fns:
                    last = f(e)
                return last
            return pe(run, *w)

        def bc(ap, shape):
            return ap.to_broadcast(shape)

        cst = ar.get(CW)
        C = {n: cst.ap[:, o:o + w] for n, (o, w) in CL.items()}
        par = ar.get(384)
        X = ar.get(2048)
        x = X.v("p (b d) -> p b d", b=2)
        small = ar.get(160)
        sm_at = [0]

        def sml(n):
            o = sm_at[0]
            sm_at[0] += n
            if sm_at[0] > 160:
                raise ValueError("small")
            return small.ap[:, o:o + n]

        rows = ar.get(384)
        Xm = ar.get(2048)
        xm = Xm.v("p (b d) -> p b d", b=2)
        swb = ar.get(1536)
        L2 = ar.get(384)
        relb = ar.get(8)
        sink = ar.get(8)
        lamv = ar.get(256)
        gpos, n_par = {}, 0
        for name, cnt in PARAMS:
            gpos[name] = n_par
            n_par += cnt

        def col(name, i=0, n=1):
            return par.ap[:, gpos[name] + i:gpos[name] + i + n]

        x_in = x

        def load_first(eng):
            eng.dma_start(x_in, A["x"].rearrange("a (b p) d -> p (a b) d", p=128)).then_inc(s_x, 16)
            eng.dma_start(cst.ap, A["consts"]).then_inc(s_cst, 16)
            pdma(eng, plist, s_par)
            eng.dma_start(xm, A["mem"].rearrange("a (b p) d -> p (a b) d", p=128)).then_inc(s_x, 16)
        def pdma(eng, lst, sm):
            for d, s in lst:
                eng.dma_start(d, s).then_inc(sm, 16)

        plist, plist2 = [], []
        for name, cnt in PARAMS:
            if not name:
                continue
            r0 = gpos[name]
            if name in ("attn_q_norm", "attn_k_norm", "mem_q_norm", "mem_k_norm"):
                src = A[name]
                for h in range(2):
                    plist.append((rows.ap[r0 % 128:r0 % 128 + 1, 128 * (r0 // 128) + 64 * h:128 * (r0 // 128) + 64 * h + 64], src))
                continue
            flat = A[name]
            if name == "conv_w":
                flat = flat.rearrange("a i (t p) -> (a i t) p", p=128)
            elif name == "rwkv_r_k":
                flat = flat.rearrange("a (t h) d -> (a t) (h d)", h=2)
            else:
                flat = flat.rearrange("a (t p) -> (a t) p", p=128)
            i = 0
            while i < cnt:
                r = r0 + i
                m = min(cnt - i, 128 - r % 128)
                (plist2 if r >= 128 else plist).append((rows.ap[r % 128:r % 128 + m, 128 * (r // 128):128 * (r // 128) + 128], flat[i:i + m, :]))
                i += m
        plist2.append((L2.ap[0:32, :], A["rwkv_w2"][0, :, :]))
        plist2.append((L2.ap[32:64, :], A["rwkv_a2"][0, :, :]))
        plist2.append((L2.ap[64:128, :], A["rwkv_g2"][0, :, :]))
        plist2.append((relb.ap[64:96, 0:6], A["rel_bias"]))
        plist2.append((sink.ap[:, 0:6], bc(A["attn_sinks"], [128, 6])))
        for i, name in enumerate(("lambda_q1_2", "lambda_k1_2", "lambda_q2_2", "lambda_k2_2")):
            plist2.append((lamv.ap[:, 64 * i:64 * i + 64], bc(A[name], [128, 64])))
        par1_tok = (s_par, 16 * len(plist))
        par_tok = (s_par2, 16 * len(plist2))
        x_tok = (s_x, 32)
        cst_tok = (s_cst, 16)
        ident = C["ident"]
        ones = C["ones"]

        def wcols(ap, c0, n, at=0):
            k = ap.shape[0] // 128

            def dst(s, k=k, n=n, at=at):
                return s[:, at:at + k * n].rearrange("p (k n) -> p k n", k=k)
            return dst, ap[:, c0:c0 + n].rearrange("(k p) n -> p k n", p=128)

        w_in = A["w_in"][0, :, :]
        ring.use([0, 1, 2])
        ch_in = [ring.load(wcols(w_in, 640, 512)), ring.load(wcols(w_in, 1152, 512)),
                 ring.load(wcols(w_in, 1664, 512)), ring.load(wcols(w_in, 0, 512)),
                 ring.load(wcols(w_in, 512, 128))]
        ch_mem = ring.load(wcols(A["w_mem_kv"][0, :, :], 0, 512))
        w_ada = A["w_ada_2"][0, :, :]
        ch_ada = [ring.load(wcols(w_ada, 512 * i, 512)) for i in range(12)]
        w_o = A["w_out"][0, :, :]
        ch_o = [ring.load(wcols(w_o, 512 * i, 512)) for i in range(2)]
        ring.use([3, 4, 5, 0, 1, 2])
        w_up = A["w_up"][0, :, :]
        ch_up = [ring.load(wcols(w_up, 256 * i, 256), wcols(w_up, 2816 + 256 * i, 256, 2048)) for i in range(11)]
        w_dn = A["w_down"][0, :, :]
        ch_dn = [ring.load(wcols(w_dn[512 * i:min(512 * i + 512, 2816), :], 0, 1024)) for i in range(6)]
        w_in2 = A["w_in_2"][0, :, :]
        ch_i2 = [ring.load(wcols(w_in2, 512 * i, 512)) for i in range(10)]
        ch_pm = ring.load(wcols(A["w_proj_moba_2"][0, :, :], 0, 1024))
        ch_pd = ring.load(wcols(A["w_proj_diff_2"][0, :, :], 0, 1024))
        ch_o2 = [ring.load(wcols(A["w_out_2"][0, :, :], 512 * i, 512)) for i in range(2)]

        def load_expert(rg, e):
            return [rg.load(wcols(A["w_gate_2"][0, e, :, :], 0, 512)), rg.load(wcols(A["w_up_2"][0, e, :, :], 0, 512)),
                    rg.load(wcols(A["w_down_2"][0, e, :, :], 0, 1024))]
        ring.use([4, 5, 0, 1, 2, 3, 6])
        ch_e = [load_expert(ring, e) for e in range(NE)]

        n_first = gpos[""]

        def par_cols(i, n, tok):
            b = ps.take()
            t = pe(tr(b.ap[:, 0:n], rows.ap[0:n, 128 * i:128 * i + 128], ident[0:n, 0:n]), tok, cst_tok, b.w)
            t = vcp(par.ap[:, 128 * i:128 * i + n], b.ap[:, 0:n], t)
            b.w = [t]
            return t
        t_par = par_cols(0, n_first, par1_tok)
        junk = ar.get(1024)

        def rstd_rows(src, tok, eps=1e-6, n=1024.0):
            s, r = sml(2), sml(2)
            for i in range(2):
                t1 = act(junk.ap, src[:, i, :], ACT.Square, tok, SC.last(), VE.last(), accum=s[:, i:i + 1])
            t2 = ts(r, s, 1.0 / n, MUL, eps, ADD, t1)
            t3 = ve(lambda e: e.reciprocal(s, r), t2)
            return r, act(r, s, ACT.Sqrt, t3)

        def normed(src, tok, dst, eps=1e-6):
            r, t3 = rstd_rows(src, tok, eps)
            for i in range(2):
                t4 = ts(dst.v("p (b d) -> p b d", b=2)[:, i, :], src[:, i, :], r[:, i:i + 1], MUL, None, None, t3, dst.w, tok)
            return t4

        def to_features(src, tok, dst, gcol, shift=None, dtok=None):
            sv = src.v("p (b d) -> p b d", b=2)
            dv = dst.v("p (k t) -> p k t", k=8)
            for k in range(0, 8, 2):
                b = ps.take()
                t = pes([tr(b.ap[:, 256 * i + 128 * h:256 * i + 128 * h + 128], sv[:, h, 128 * (k + i):128 * (k + i) + 128], ident)
                         for i in range(2) for h in range(2)], tok, b.w, cst_tok)
                pv = b.ap.rearrange("p (k t) -> p k t", k=2)
                if shift is None:
                    t2 = tt(dv[:, k:k + 2, :], pv, bc(gcol[:, k:k + 2].unsqueeze(2), [128, 2, 256]), MUL, t, dst.w, t_par, dtok)
                else:
                    for i in range(2):
                        t2 = ts(dv[:, k + i, :], pv[:, i, :], gcol[:, k + i:k + i + 1], MUL, shift[:, k + i:k + i + 1], ADD, t, dst.w, dtok)
                b.w = [t2]
            return t2

        Xn = ar.get(2048)
        hT = ar.get(2048)
        t = normed(x, x_tok, Xn)
        t_h = to_features(Xn, t, hT, col("mix_norm_g", 0, 8))
        ar.free(now(), Xn)
        Mn = ar.get(2048)
        mT = ar.get(2048)
        t = normed(xm, x_tok, Mn)
        t_m = to_features(Mn, t, mT, col("mem_norm_g", 0, 8))
        ar.free(now(), Mn, Xm, X)
        hv = hT.v("p (k t) -> p k t", k=8)
        mv_ = mT.v("p (k t) -> p k t", k=8)

        def proj_fm(b, half, chunk, cols, c0, act_v, k_n=8, base=0):
            w = chunk.ap[:, base:base + k_n * cols].rearrange("p (k n) -> p k n", k=k_n)
            return [mm(b.ap[:, 256 * half:256 * half + 256], w[:, k, c0:c0 + 128], act_v[:, k, :], k == 0, k == k_n - 1)
                    for k in range(k_n)]

        pz = rbuf(10 * 257)
        sh = rbuf(2560)
        shv = sh.v("p (n t) -> p n t", n=10)
        pzv = pz.v("p (n t) -> p n t", n=10)
        t_z = gp(lambda e: e.memset(pzv[:, :, 0:1], 0.0), pz.w)
        evac = []
        for i in range(0, 10, 2):
            b = ps.take()
            for h in range(2):
                n = i + h
                ch = ch_in[n // 4]
                t = pes(proj_fm(b, h, ch, 512, 128 * (n % 4), hv), t_h, ch.tok, b.w)
            t2 = acp(pzv[:, i:i + 2, 1:257], b.ap.rearrange("p (n t) -> p n t", n=2), t, pz.w)
            b.w = [t2]
            if i == 2:
                ch_in[0].free = [t]
            if i == 6:
                ch_in[1].free = [t]
        t_pz = t2
        par_cols(1, 128, par_tok)
        t_par = par_cols(2, n_par - 256, par_tok)
        t = tt(shv, pzv[:, :, 0:256], pzv[:, :, 1:257], SUB, t_pz, t_z, sh.w)
        t = tt(shv, shv, bc(col("rwkv_mu", 0, 10).unsqueeze(2), [128, 10, 256]), MUL, t)
        t_sh = tt(shv, shv, pzv[:, :, 1:257], ADD, t)
        rfree(pz)
        b = ps.take()
        t = pe(mm(b.ap[0:6, 0:384], relb.ap[64:96, 0:6], C["OHB"][64:96, 0:384], True, True), b.w)
        Eb = ar.get(384)
        t_eb = tt(Eb.ap[0:6, :], b.ap[0:6, 0:384], C["MR"][0:6, :], ADD, t, Eb.w)
        b.w = [t_eb]
        bias_v = swb.v("p (h k) -> p h k", h=6)
        toep = bass.AP(scratch, 0, [[1, 128], [384, 6], [1, 256]])
        swr = ar.get(1536)
        swr_v = swr.v("p (h k) -> p h k", h=6)
        bias_tok = (s_bias, 32)

        def bias_dma(e):
            e.dma_start(scratch.ap(), Eb.ap[0:6, :]).then_inc(s_bias, 16)
            e.wait_ge(s_bias, 16)
            e.dma_start(swr_v, toep).then_inc(s_bias, 16)
            return None
        GP.job(bias_dma, t_eb, swr.w)

        qk = ar.get(8 * 256)
        qkv = qk.v("p (n t) -> p n t", n=8)
        plan = [(ch_in[2], 256, hv, t_h), (ch_in[2], 384, hv, t_h), (ch_in[3], 0, hv, t_h), (ch_in[3], 128, hv, t_h),
                (ch_in[3], 256, hv, t_h), (ch_in[3], 384, hv, t_h), (ch_mem, 0, mv_, t_m), (ch_mem, 128, mv_, t_m)]
        va = ar.get(256)
        vm = ar.get(512)
        for i in range(0, 8, 2):
            b = ps.take()
            for h in range(2):
                ch, c0, av, tk = plan[i + h]
                t = pes(proj_fm(b, h, ch, 512, c0, av), tk, ch.tok, b.w)
            t_qk = acp(qkv[:, i:i + 2, :], b.ap.rearrange("p (n t) -> p n t", n=2), t, qk.w)
            b.w = [t_qk]
            if i == 0:
                ch_in[2].free = [t]
            if i == 4:
                ch_in[3].free = [t]
        b = ps.take()
        w = ch_in[4].ap[:, 0:1024].rearrange("p (k n) -> p k n", k=8)
        for h in range(2):
            t = pes([mm(b.ap[:, 128 * h:128 * h + 128], hv[:, k, 128 * h:128 * h + 128], w[:, k, :], k == 0, k == 7)
                     for k in range(8)], ch_in[4].tok, b.w)
        ch_in[4].free = [t]
        t_va = acp(va.ap, b.ap[:, 0:256], t, va.w)
        b.w = [t_va]
        b = ps.take()
        w = ch_mem.ap.rearrange("p (k n) -> p k n", k=8)
        for h in range(2):
            t = pes([mm(b.ap[:, 256 * h:256 * h + 256], mv_[:, k, 128 * h:128 * h + 128], w[:, k, 256:512], k == 0, k == 7)
                     for k in range(8)], b.w)
        ch_mem.free = [t]
        t_vm = acp(vm.ap, b.ap, t, vm.w)
        b.w = [t_vm]
        ar.free(now(), hT, mT, rows, junk)

        def head_rstd(tiles, tok, n, eps, dst, nh, floor=None, sel="hs"):
            b = ps.take()
            fns = [mm(b.ap[0:16, 0:256], C[sel][:, 14 - 2 * i:30 - 2 * i], s, i == 0, i == len(tiles) - 1)
                   for i, s in enumerate(tiles)]
            t = pes(fns, tok, b.w)
            if floor is None:
                t = ts(dst[0:16, 0:256], b.ap[0:16, 0:256], 1.0 / n, MUL, eps, ADD, t)
            else:
                t = ts(dst[0:16, 0:256], b.ap[0:16, 0:256], floor, MAX, None, None, t)
            b.w = [t]
            t = ve(lambda e: e.reciprocal(dst[0:16, 256:512], dst[0:16, 0:256]), t)
            return act(dst[0:16, 0:256], dst[0:16, 256:512], ACT.Sqrt, t)

        def head_bcast(b, half, i, dst):
            return mm(b.ap[:, 256 * half:256 * half + 256], C["OHB"][0:16, 128 * i:128 * i + 128],
                      dst[0:16, 0:256], True, True)

        sq = ar.get(2048)
        rs = ar.get(512)
        t = tt(sq.ap, qk.ap, qk.ap, MUL, t_qk, sq.w)
        sqv = sq.v("p (n t) -> p n t", n=8)
        t_rs = head_rstd([sqv[:, i, :] for i in range(8)], [t, *rs.w], 64.0, 1e-6, rs.ap, 16)
        gains = ["mem_q_norm", "mem_q_norm", "attn_q_norm", "attn_q_norm", "attn_q_norm", "attn_k_norm", "mem_k_norm", "mem_k_norm"]
        for i in range(0, 8, 2):
            b = ps.take()
            t = pes([head_bcast(b, 0, i, rs.ap), head_bcast(b, 1, i + 1, rs.ap)], t_rs, b.w)
            for h in range(2):
                t_qn = stt(qkv[:, i + h, :], qkv[:, i + h, :], col(gains[i + h]), b.ap[:, 256 * h:256 * h + 256], MUL, MUL, t)
            b.w = [t_qn]
        ar.free(now(), sq, rs)
        kb = ar.get(256)
        t_kb = act(kb.ap[0:64, :], qkv[64:128, 5, :], ACT.Copy, t_qn, kb.w)
        t_kb = act(kb.ap[64:128, :], qkv[0:64, 5, :], ACT.Copy, t_qn)

        for i in range(3):
            b = ps.take()
            t = pe(mm(b.ap, C["rev"], swr.ap[:, 512 * i:512 * i + 512], True, True), bias_tok, b.w)
            t_sw = acp(swb.ap[:, 512 * i:512 * i + 512], b.ap, t, swb.w)
            b.w = [t_sw]
        ar.free(now(), swr)
        cat = ar.get(2048)
        catv = cat.v("p (k t) -> p k t", k=8)

        cpad = ar.get(256)
        cpv = cpad.v("p (k m) -> p k m", k=8)
        modc = ar.get(32, True)
        g1b, g2b = ar.get(1024, True), ar.get(1024, True)
        msb = [ar.get(512), ar.get(512)]
        ms_free = [[], []]
        t_cp = ve(lambda e: e.memset(cpad.ap, 0.0), cpad.w)
        t_cp = act(cpv[:, :, 0:1].rearrange("p k o -> p (k o)"), col("c_2", 0, 8), ACT.Silu, t_cp, t_par)
        ada_tok = []

        def ada_step(i):
            b, m = ps.take(), msb[i % 2]
            w = ch_ada[i].ap.rearrange("p (k n) -> p k n", k=8)
            t = pes([mm(b.ap[32 * j:32 * j + 32, :], cpv[:, 2 * j + q, :], w[:, 2 * j + q, :], q == 0, q == 1)
                     for q in range(2) for j in range(4)], ch_ada[i].tok, t_cp, b.w)
            ch_ada[i].free = [t]
            t2 = acp(m.ap, b.ap, t, ms_free[i % 2], m.w)
            b.w = [t2]
            yield
            b = ps.take()
            part = i // 2
            if part in (2, 5):
                t = pe(mm(b.ap, ones, m.ap, True, True), t2, b.w)
                gb = (g1b if part == 2 else g2b).ap[:, 512 * (i % 2):512 * (i % 2) + 512]
                t3 = tt(gb, b.ap, gb, ADD, t, (s_gb, 32))
            else:
                t = pes([mm(b.ap[:, q:q + 1], m.ap[:, 128 * q:128 * q + 128], ones[:, 0:1], True, True) for q in range(4)], t2, b.w)
                o = {0: 0, 1: 8, 3: 16, 4: 24}[part] + 4 * (i % 2)
                t3 = tt(modc.ap[:, o:o + 4], b.ap[:, 0:4], col("b_ada_2", 4 * i, 4), ADD, t, modc.w)
            b.w = [t3]
            ms_free[i % 2] = [t]
            ada_tok.append(t3)

        def ada_chain():
            for i in range(12):
                yield from ada_step(i)
                yield
        later(g1b.w, [(g1b.ap, bc(A["b_ada_2"][:, 2048:3072], [128, 1024]))], s_gb)
        later(g2b.w, [(g2b.ap, bc(A["b_ada_2"][:, 5120:6144], [128, 1024]))], s_gb)

        NB_A = 2
        S_ = [ar.get(512) for _ in range(NB_A)]
        P_ = [ar.get(512) for _ in range(NB_A)]
        PT_ = [ar.get(512) for _ in range(NB_A)]
        st_ = [sml(12) for _ in range(NB_A)]
        a_free = [[[], []] for _ in range(NB_A)]

        def attn_scores(i, q2, k2, blk, nk, masks, tok, sink_c=None, combine=None):
            S, P, PT, st = S_[i], P_[i], PT_[i], st_[i]
            bb = [ps.take(), ps.take()]
            w = nk * 128
            t = pes([mm(bb[h].ap[:, 0:w], q2[h][:, 128 * blk:128 * blk + 128], k2[h][:, 0:w], True, True)
                     for h in range(2)], tok, bb[0].w, bb[1].w)
            sv = S.ap[:, 0:2 * w].rearrange("p (h k) -> p h k", h=2)
            prev = a_free[i][0]
            for h in range(2):
                t1 = masks(h, sv[:, h, :], bb[h].ap[:, 0:w], [t, *prev, *S.w])
                bb[h].w = [t1]
            mx, nm, ssum, rc = st[:, 0:2], st[:, 2:4], st[:, 4:6], st[:, 6:8]
            t2 = ve(lambda e: e.tensor_reduce(mx, sv, AX.X, MAX), t1, prev)
            if sink_c is not None:
                t2 = tt(mx, mx, sink_c, MAX, t2)
            t3 = ts(nm, mx, -1.0, MUL, None, None, t2)
            pv = P.ap[:, 0:2 * w].rearrange("p (h k) -> p h k", h=2)
            for h in range(2):
                t4 = act(pv[:, h, :], sv[:, h, :], ACT.Exp, t3, prev, P.w, bias=nm[:, h:h + 1], accum=ssum[:, h:h + 1])
            if sink_c is not None:
                t5 = tt(st[:, 8:10], sink_c, nm, ADD, t3)
                t5 = act(st[:, 10:12], st[:, 8:10], ACT.Exp, t5)
                t4 = tt(ssum, ssum, st[:, 10:12], ADD, t4, t5)
            t5 = ve(lambda e: e.reciprocal(rc, ssum), t4)
            return i, pv, rc, t5, w

        def attn_out(i, pv, rc, t5, w, nk, v2, dst, vtok, dtok, done):
            P, PT = P_[i], PT_[i]
            t6 = tt(pv, pv, bc(rc.unsqueeze(2), [128, 2, w]), MUL, t5)
            b = ps.take()
            t7 = pes([tr(b.ap[:, 128 * (nk * h + j):128 * (nk * h + j) + 128], pv[:, h, 128 * j:128 * j + 128], ident)
                      for h in range(2) for j in range(nk)], t6, b.w)
            t8 = acp(PT.ap[:, 0:2 * w], b.ap[:, 0:2 * w], t7, a_free[i][1], PT.w)
            b.w = [t8]
            yield
            b = ps.take()
            t9 = pes([mm(b.ap[64 * h:64 * h + 64, 0:128], v2[h](j), PT.ap[:, 128 * (nk * h + j):128 * (nk * h + j) + 128], j == 0, j == nk - 1)
                      for h in range(2) for j in range(nk)], t8, vtok, b.w)
            t10 = acp(dst, b.ap[:, 0:128], t9, dtok)
            b.w = [t10]
            a_free[i] = [[t7, t6], [t9]]
            done.append(t10)

        def plain(h, sv, bv, w):
            return ts(sv, bv, 0.125, MUL, None, None, *w)

        def causal(nk):
            def f(h, sv, bv, w):
                if nk == 2:
                    ts(sv[:, 0:128], bv[:, 0:128], 0.125, MUL, None, None, *w)
                l = 128 * (nk - 1)
                return stt(sv[:, l:l + 128], bv[:, l:l + 128], 0.125, C["caus"], MUL, ADD, *w)
            return f

        def windowed(pair, nk):
            def f(h, sv, bv, w):
                return stt(sv, bv, 0.125, bias_v[:, 2 * pair + h, 256 - 128 * nk:256], MUL, ADD, t_sw, *w)
            return f

        def hrow(ap, h):
            return ap[64 * (h % 2):64 * (h % 2) + 64, :]

        vmv = vm.v("p (b d) -> p b d", b=2)
        vav = va.v("p (b d) -> p b d", b=2)
        cat_done = []

        def mem_unit(i, pr, blk):
            r = attn_scores(i, [hrow(qkv[:, pr, :], h) for h in range(2)], [hrow(qkv[:, 6 + pr, :], h) for h in range(2)],
                            blk, 2, plain, t_qn)
            yield
            yield from attn_out(*r, 2, [(lambda j, h=2 * pr + h: vmv[:, j, 64 * h:64 * h + 64]) for h in range(2)],
                                catv[:, 6 + pr, 128 * blk:128 * blk + 128], t_vm, cat.w, cat_done)

        def win_unit(i, pr, blk):
            nk = 1 + blk
            ks = []
            for h in range(2):
                kvh = (2 * pr + h) // 3
                ks.append(hrow(qkv[:, 5, :] if kvh == h else kb.ap, h))
            r = attn_scores(i, [hrow(qkv[:, 2 + pr, :], h) for h in range(2)], ks, blk, nk, windowed(pr, nk), [t_qn, t_kb],
                            sink_c=sink.ap[:, 2 * pr:2 * pr + 2])
            yield
            yield from attn_out(*r, nk, [(lambda j, n=(2 * pr + h) // 3: vav[:, j, 64 * n:64 * n + 64]) for h in range(2)],
                                catv[:, pr, 128 * blk:128 * blk + 128], t_va, cat.w, cat_done)

        def unit_chain(i, units):
            for f, pr, blk in units:
                yield from f(i, pr, blk)
                yield
        units = [(mem_unit, pr, blk) for pr in range(2) for blk in range(2)] + [(win_unit, pr, blk) for pr in range(3) for blk in range(2)]

        def v3(b):
            return b.v("p (n t) -> p n t", n=3)

        def c3(name):
            return bc(col(name, 0, 3).unsqueeze(2), [128, 3, 256])
        rT, kT_, vT = shv[:, 0:3, :], shv[:, 3:6, :], shv[:, 6:9, :]
        cat2_done = []

        def rwkv_chain():
            lt = rbuf(256)
            t1 = act(lt.ap[0:32, :], shv[0:32, 9, :], ACT.Tanh, t_sh, lt.w)
            t1 = act(lt.ap[32:64, :], shv[32:64, 9, :], ACT.Copy, t_sh, lt.w)
            t_lt = act(lt.ap[64:128, :], shv[64:128, 9, :], ACT.Sigmoid, t_sh, lt.w)
            sg, av, gg = rbuf(768), rbuf(768), rbuf(768)
            for p0, k_, dstb, f, bn in ((0, 32, sg, ACT.Sigmoid, "rwkv_w0"), (32, 32, av, ACT.Sigmoid, "rwkv_a0"), (64, 64, gg, ACT.Copy, None)):
                for i in range(3):
                    b = ps.take()
                    t = pe(mm(b.ap[:, 0:256], L2.ap[p0:p0 + k_, 128 * i:128 * i + 128], lt.ap[p0:p0 + k_, :], True, True), t_lt, par_tok, b.w)
                    if bn:
                        t_w = act(v3(dstb)[:, i, :], b.ap[:, 0:256], f, t, dstb.w, bias=col(bn, i))
                    else:
                        t_w = acp(v3(dstb)[:, i, :], b.ap[:, 0:256], t, dstb.w)
                    b.w = [t_w]
            yield
            kk, tmp, rs = rbuf(768), rbuf(768), rbuf(512)
            t = tt(v3(kk), kT_, c3("rwkv_k_k"), MUL, t_sh, t_par, kk.w)
            t = tt(v3(tmp), v3(kk), v3(kk), MUL, t, tmp.w)
            t_rs = head_rstd([v3(tmp)[:, i, :] for i in range(3)], [t, *rs.w], 1.0, 0.0, rs.ap, 16, floor=1e-24)
            for i in range(3):
                b = ps.take()
                t = pe(head_bcast(b, 0, i, rs.ap), t_rs, b.w)
                t_kk = tt(v3(kk)[:, i, :], v3(kk)[:, i, :], b.ap[:, 0:256], MUL, t)
                b.w = [t_kk]
            yield
            t = ts(v3(tmp), v3(av), -1.0, ADD, None, None, t_w, VE.last(), PE.last())
            t = tt(v3(tmp), v3(tmp), c3("rwkv_k_a"), MUL, t)
            kp = rbuf(768)
            t_kp = stt(kp.ap, tmp.ap, 1.0, sh.ap[:, 768:1536], ADD, MUL, t, kp.w)
            t_b = tt(av.ap, kk.ap, av.ap, MUL, t_kk, t_kp)
            yield
            Lz = rbuf(6 * 129)
            Lv = Lz.v("p (n c t) -> p n c t", n=3, c=2)
            t_l0 = gp(lambda e: e.memset(Lv[:, :, :, 0:1], 0.0), Lz.w)
            t = ts(sg.ap, sg.ap, -math.exp(-0.5), MUL, None, None, t_w)
            for i in range(3):
                for c in range(2):
                    t_L = ve(lambda e, i=i, c=c: e.tensor_tensor_scan(out=Lv[:, i, c, 1:129], data0=ones, data1=v3(sg)[:, i, 128 * c:128 * c + 128],
                                                                     initial=0.0, op0=MUL, op1=ADD), t, Lz.w)
            yield
            Lm = sml(12)
            t_lm = vcp(Lm[:, 0:6], Lv[:, :, :, 64:65].rearrange("p n c o -> p (n c o)"), t_L)
            t_nl = ts(Lm[:, 6:12], Lm[:, 0:6], -1.0, MUL, None, None, t_lm)
            E1, E2 = rbuf(6 * 129), rbuf(768)
            E1v, E2v = E1.v("p (n c t) -> p n c t", n=3, c=2), E2.v("p (n c t) -> p n c t", n=3, c=2)
            for i in range(3):
                for c in range(2):
                    q = 2 * i + c
                    act(E1v[:, i, c, :], Lv[:, i, c, :], ACT.Exp, t_L, t_nl, t_l0, E1.w, bias=Lm[:, 6 + q:7 + q])
                    t_E = act(E2v[:, i, c, :], Lv[:, i, c, 1:129], ACT.Exp, E2.w, bias=Lm[:, q:q + 1], scale=-1.0)
            yield
            eM = sml(6)
            t_eM = act(eM, Lm[:, 0:6], ACT.Exp, t_lm)
            AR = rbuf(1536)
            ARv = AR.v("p (n c z t) -> p n c z t", n=3, c=2, z=2)

            def v4(ap):
                return ap.rearrange("p (n c t) -> p n c t", n=3, c=2)
            BK = [rbuf(768), rbuf(768)]
            for i in range(3):
                stt(ARv[:, i, :, 0, :], v4(kk.ap)[:, i, :, :], -1.0, E1v[:, i, :, 0:128], MUL, MUL, t_E, t_kk, AR.w)
                t_AR = tt(ARv[:, i, :, 1, :], v4(sh.ap[:, 0:768])[:, i, :, :], E1v[:, i, :, 1:129], MUL, AR.w)
            t_B = tt(BK[0].ap, av.ap, E2.ap, MUL, t_b, BK[0].w)
            t_K = tt(BK[1].ap, kp.ap, E2.ap, MUL, BK[1].w)
            yield
            bs = tmp
            t = tt(bs.ap, sh.ap[:, 0:768], kp.ap, MUL, t_kp, VE.last())
            t = tt(v3(bs), v3(bs), c3("rwkv_r_k"), MUL, t)
            for i in range(3):
                b = ps.take()
                t2 = pe(mm(b.ap[:, 0:256], C["bo"], v3(bs)[:, i, :], True, True), t, b.w)
                t_bon = tt(v3(bs)[:, i, :], b.ap[:, 0:256], vT[:, i, :], MUL, t2)
                b.w = [t_bon]
            yield
            VT, BT, KT_ = rbuf(768), rbuf(384), rbuf(384)
            VTv = VT.v("p (c n k) -> p c n k", c=2, n=3)
            for c in range(2):
                b = ps.take()
                t = pes([tr(b.ap[:, 128 * i:128 * i + 128], vT[:, i, 128 * c:128 * c + 128], ident) for i in range(3)], t_sh, b.w)
                t_VT = acp(VT.ap[:, 384 * c:384 * c + 384], b.ap[:, 0:384], t, VT.w)
                b.w = [t_VT]
            for src, dst, tk in ((BK[0], BT, t_B), (BK[1], KT_, t_K)):
                b = ps.take()
                t = pes([tr(b.ap[:, 128 * i:128 * i + 128], v4(src.ap)[:, i, 0, :], ident) for i in range(3)], tk, b.w)
                t_BT = acp(dst.ap, b.ap[:, 0:384], t, dst.w)
                b.w = [t_BT]
            rfree(kk, E2, Lz, sg, kp, av, lt)

            yield
            yT = rbuf(768)
            rhs_b, sa_b = rbuf(384), rbuf(384)
            st_b = rbuf(192)
            MB, MK, XZ, T1 = rbuf(1536), rbuf(1536), rbuf(1536), rbuf(768)
            t_z1 = gp(lambda e: e.memset(MB.ap, 0.0), MB.w)
            t_z2 = gp(lambda e: e.memset(MK.ap, 0.0), MK.w)
            SUm, SLm = C["SU"], C["SL"]
            i32 = lambda a: a.bitcast(I32)
            su_iu = cst.ap[:, CL["SU"][0]:CL["SU"][0] + 256]
            done_prev = []
            XZv = XZ.v("p (h z t) -> p h z t", h=6, z=2)
            T1v = T1.v("p (h t) -> p h t", h=6)

            def at(h):
                return 3 * (h % 2) + h // 2

            def Mab(k):
                h = 2 * (k % 3) + k // 3
                return MB.ap[:, 256 * h:256 * h + 128]
            for c in range(2):
                t_unit = [[] for _ in range(6)]
                for h in range(6):
                    i, o = h // 2, 64 * (h % 2)
                    b = ps.take()
                    ARh = ARv[o:o + 64, i, c, :, :].rearrange("p z t -> p (z t)")
                    Bh, Kh = v4(BK[0].ap)[o:o + 64, i, c, :], v4(BK[1].ap)[o:o + 64, i, c, :]
                    t = pes([mm(b.ap[:, 0:256], Bh, ARh, True, True), mm(b.ap[:, 256:512], Kh, ARh, True, True)], t_AR, t_B, t_K, b.w)
                    ve(lambda e, h=h, b=b: e.copy_predicated(MB.ap[:, 256 * h:256 * h + 256], i32(su_iu), b.ap[:, 0:256]), t, t_z1, done_prev)
                    t2 = ve(lambda e, h=h, b=b: e.copy_predicated(MK.ap[:, 256 * h:256 * h + 256], i32(su_iu), b.ap[:, 256:512]), t_z2)
                    b.w = [t2]
                    t_unit[at(h)].append(t2)
                    yield
                for z in range(2):
                    b = ps.take()
                    t = pes([mm(b.ap[:, 128 * i:128 * i + 128], ARv[64 * z:64 * z + 64, i, c, 0, :], v4(BK[0].ap)[64 * z:64 * z + 64, i, c, :], True, True)
                             for i in range(3)], b.w)
                    X3, Z3 = XZv[:, 3 * z:3 * z + 3, 0, :], XZv[:, 3 * z:3 * z + 3, 1, :]
                    t3 = tt(X3, b.ap[:, 0:384].rearrange("p (n t) -> p n t", n=3), bc(C["LM"][:, 0:128].unsqueeze(1), [128, 3, 128]), MUL, t, XZ.w, done_prev)
                    b.w = [t3]
                    M3 = MB.ap.rearrange("p (i o x) -> p i o x", i=3, o=2)[:, :, z, 0:128]
                    t5 = tt(Z3, M3, bc(C["LM1T"].unsqueeze(1), [128, 3, 128]), MUL, t_unit[3 * z:3 * z + 3], XZ.w)
                    for i in range(3):
                        t5 = tt(XZv[:, 3 * z + i, :, :], XZv[:, 3 * z + i, :, :], bc(ident.unsqueeze(1), [128, 2, 128]), ADD, t3, t5)
                        t_unit[3 * z + i] = [t5]
                    yield
                for lv in range(1, 7):
                    lm = bc(C["LM"][:, 128 * lv:128 * lv + 128].unsqueeze(1), [128, 2, 128])
                    t_T = []
                    for q in range(3):
                        b = ps.take()
                        t = pes([mm(b.ap[:, 128 * y:128 * y + 128], Mab(2 * q + y), XZv[:, 2 * q + y, 0, :], True, True) for y in range(2)],
                                t_unit[2 * q], t_unit[2 * q + 1], b.w)
                        t = tt(T1v[:, 2 * q:2 * q + 2, :], b.ap[:, 0:256].rearrange("p (y t) -> p y t", y=2), lm, MUL, t, T1.w)
                        b.w = [t]
                        t_T.append(t)
                    yield
                    for q in range(3):
                        b = ps.take()
                        fns = []
                        for y in range(2):
                            Th, Zh = T1v[:, 2 * q + y, :], XZv[:, 2 * q + y, 1, :]
                            if lv < 6:
                                fns.append(mm(b.ap[:, 256 * y:256 * y + 128], Zh, Th, True, True))
                            fns.append(mm(b.ap[:, 256 * y + 128:256 * y + 256], Th, Zh, True, True))
                        t = pes(fns, t_T[q], b.w)
                        b4 = b.ap.rearrange("p (y z t) -> p y z t", y=2, z=2)
                        if lv < 6:
                            t2 = tt(XZ.ap[:, 512 * q:512 * q + 512], XZ.ap[:, 512 * q:512 * q + 512], b.ap, ADD, t)
                        else:
                            t2 = tt(XZv[:, 2 * q:2 * q + 2, 1, :], XZv[:, 2 * q:2 * q + 2, 1, :], b4[:, :, 1, :], ADD, t)
                        b.w = [t2]
                        t_unit[2 * q] = t_unit[2 * q + 1] = [t2]
                    yield
                yield
                rbs = [ps.take(), ps.take()]
                fns = []
                for h in range(6):
                    i, o = h // 2, 64 * (h % 2)
                    oc = rbs[h % 2].ap[:, 64 * i:64 * i + 64]
                    if c == 1:
                        fns.append(mm(oc, ARv[o:o + 64, i, c, 0, :], st_b.ap[o:o + 64, 64 * i:64 * i + 64], True, False))
                    fns.append(mm(oc, MK.ap[:, 256 * h:256 * h + 128], VTv[:, c, i, o:o + 64], c == 0, True))
                t0 = pes(fns, [x for u in t_unit for x in u], rbs[0].w, rbs[1].w, t_VT, done_prev)
                for o in range(2):
                    t = acp(rhs_b.ap.rearrange("p (n o k) -> p n o k", n=3, o=2)[:, :, o, :],
                            rbs[o].ap[:, 0:192].rearrange("p (n k) -> p n k", n=3), t0, rhs_b.w, done_prev)
                    rbs[o].w = [t]
                yield
                rb = ps.take()
                t = pes([mm(rb.ap[:, 64 * h:64 * h + 64], XZv[:, at(h), 1, :], rhs_b.ap[:, 64 * h:64 * h + 64], True, True) for h in range(6)], t, rb.w)
                t_sa = acp(sa_b.ap, rb.ap[:, 0:384], t, sa_b.w, done_prev)
                rb.w = [t_sa]
                yield
                yb = ps.take()
                fns = []
                for h in range(6):
                    i, o = h // 2, 64 * (h % 2)
                    oc = yb.ap[o:o + 64, 128 * i:128 * i + 128]
                    if c == 1:
                        fns.append(mm(oc, st_b.ap[o:o + 64, 64 * i:64 * i + 64], ARv[o:o + 64, i, c, 1, :], True, False))
                    fns.append(mm(oc, sa_b.ap[:, 64 * h:64 * h + 64], MB.ap[:, 256 * h + 128:256 * h + 256], c == 0, False))
                    fns.append(mm(oc, VTv[:, c, i, o:o + 64], MK.ap[:, 256 * h + 128:256 * h + 256], False, True))
                t_y = pes(fns, t_sa, yb.w)
                t_yT = vcp(v4(yT.ap)[:, :, c, :], yb.ap[:, 0:384].rearrange("p (n t) -> p n t", n=3), t_y, yT.w)
                yb.w = [t_yT]
                yield
                if c == 0:
                    sbk = ps.take()
                    fns = []
                    for h in range(6):
                        i, o = h // 2, 64 * (h % 2)
                        oc = sbk.ap[o:o + 64, 64 * i:64 * i + 64]
                        fns.append(mm(oc, BT.ap[:, 128 * i + o:128 * i + o + 64], sa_b.ap[:, 64 * h:64 * h + 64], True, False))
                        fns.append(mm(oc, KT_.ap[:, 128 * i + o:128 * i + o + 64], VTv[:, 0, i, o:o + 64], False, True))
                    t = pes(fns, t_sa, t_BT, sbk.w)
                    for i in range(3):
                        t = ts(st_b.ap[:, 64 * i:64 * i + 64], sbk.ap[:, 64 * i:64 * i + 64], E1v[:, i, 0, 128:129], MUL,
                               eM[:, 2 * i + 1:2 * i + 2], MUL, t, t_eM, st_b.w)
                    sbk.w = [t]
                    t_st = t
                    done_prev = [t_st, t_y, t_yT]
            yield
            rfree(MB, MK, XZ, T1, rhs_b, sa_b, st_b, E1, AR, *BK, BT, KT_, VT)
            ysq = rbuf(768)
            for i in range(3):
                b = ps.take()
                t = pe(mm(b.ap[:, 0:256], C["bo"], v3(yT)[:, i, :], True, True), t_yT, b.w)
                t_c = stt(v3(yT)[:, i, :], b.ap[:, 0:256], -1.0 / 64, v3(yT)[:, i, :], MUL, ADD, t)
                b.w = [t_c]
            yield
            t = tt(ysq.ap, yT.ap, yT.ap, MUL, t_c, ysq.w)
            t_rs = head_rstd([v3(ysq)[:, i, :] for i in range(3)], [t, VE.last(), PE.last()], 64.0, 64e-5, rs.ap, 16)
            for i in range(3):
                b = ps.take()
                t = pe(head_bcast(b, 0, i, rs.ap), t_rs, b.w)
                t = tt(v3(yT)[:, i, :], v3(yT)[:, i, :], b.ap[:, 0:256], MUL, t)
                b.w = [t]
                t = ts(v3(yT)[:, i, :], v3(yT)[:, i, :], col("rwkv_ln_w", i), MUL, col("rwkv_ln_b", i), ADD, t)
            t = tt(yT.ap, yT.ap, bs.ap, ADD, t)
            t_cat2 = tt(cat.ap[:, 768:1536], yT.ap, gg.ap, MUL, t, cat.w)
            rfree(ysq, yT, rs, tmp, gg, sh)
            for i in (3, 4, 5):
                ring.lent[i] = now()
            cat2_done.append(t_cat2)

        interleave(ps, (rwkv_chain(), [4, 5, 6]), [(unit_chain(0, units[0::2]), [0, 1], 0.4), (unit_chain(1, units[1::2]), [2, 3], 0.4),
                                                   (ada_chain(), [7], 0.5)])
        t_cat, t_cat2 = cat_done, cat2_done
        ar.free(now(), *S_, *P_, *PT_, qk, kb, va, vm, Eb, swb, *msb, cpad, L2)

        X = ar.get(2048, True)
        x = X.v("p (b d) -> p b d", b=2)
        later(X.w, [(x, A["x"].rearrange("a (b p) d -> p (a b) d", p=128))], s_x2)
        x2_tok = (s_x2, 16)

        def token_out(chunks, act_v, use, tok, k_n=8):
            for c, ch in enumerate(chunks):
                w = ch.ap.rearrange("p (k n) -> p k n", k=8)
                for h in range(2):
                    b = ps.take()
                    t = pes([mm(b.ap, act_v[:, k, 128 * h:128 * h + 128], w[:, k, :], k == 0, k == k_n - 1)
                             for k in range(k_n)], tok, ch.tok, b.w)
                    t2 = use(c, h, b.ap, t)
                    b.w = [t2]
                ch.free = [t]
            return t2

        def add_x(c, h, bank, t):
            v = x[:, h, 512 * c:512 * c + 512]
            return tt(v, bank, v, ADD, t, x2_tok)

        t_x = token_out(ch_o, catv, add_x, [t_cat, t_cat2])
        ar.free(now(), cat)

        junk = ar.get(1024)
        Xn, hT = ar.get(2048), ar.get(2048)
        t = normed(x, t_x, Xn)
        t_h = to_features(Xn, t, hT, col("ffn_norm_g", 0, 8))
        ar.free(now(), Xn)
        hv = hT.v("p (k t) -> p k t", k=8)
        aT = ar.get(22 * 256)
        aTv = aT.v("p (k t) -> p k t", k=22)
        Uz = [ar.get(4 * 258) for _ in range(2)]
        Ub = [ar.get(1024) for _ in range(2)]
        u_free = [[], []]
        tz = []
        for u in Uz:
            tz.append(gp(lambda e, u=u: e.memset(u.v("p (n t) -> p n t", n=4)[:, :, 0:2], 0.0), u.w))
        for i in range(11):
            U, Uc = Uz[i % 2].v("p (n t) -> p n t", n=4), Ub[i % 2].v("p (n t) -> p n t", n=4)
            te = []
            for z in range(2):
                b = ps.take()
                for h in range(2):
                    t = pes(proj_fm(b, h, ch_up[i], 256, 128 * h, hv, base=2048 * z), t_h, ch_up[i].tok, b.w)
                t2 = acp(U[:, 2 * z:2 * z + 2, 2:258], b.ap.rearrange("p (n t) -> p n t", n=2), t, u_free[i % 2], Uz[i % 2].w, tz)
                b.w = [t2]
                te.append(t2)
            ch_up[i].free = [t]
            tiles = [2 * i, 2 * i + 1, 22 + 2 * i, 23 + 2 * i]
            for n, g_ in enumerate(tiles):
                t2 = act(Uc[:, n, :], U[:, n, 2:258], ACT.Identity, te[n // 2], u_free[i % 2], Ub[i % 2].w,
                         scale=col("conv_w", 88 + g_), bias=col("conv_b", g_))
                t2 = stt(Uc[:, n, :], U[:, n, 1:257], col("conv_w", 44 + g_), Uc[:, n, :], MUL, ADD, t2)
                t2 = stt(Uc[:, n, :], U[:, n, 0:256], col("conv_w", g_), Uc[:, n, :], MUL, ADD, t2)
                if n == 1:
                    tg = t2
            t3 = act(Uc[:, 0:2, :], Uc[:, 0:2, :], ACT.Silu, tg)
            t_a = tt(aTv[:, 2 * i:2 * i + 2, :], Uc[:, 0:2, :], Uc[:, 2:4, :], MUL, t3, t2, aT.w)
            u_free[i % 2] = [t_a]
        bb = [ps.take() for _ in range(4)]
        for c in range(6):
            w = ch_dn[c].ap.rearrange("p (k n) -> p k n", k=4)
            fns = []
            for k in range(4 if c < 5 else 2):
                f = 4 * c + k
                for h in range(2):
                    for q in range(2):
                        fns.append(mm(bb[2 * h + q].ap, aTv[:, f, 128 * h:128 * h + 128], w[:, k, 512 * q:512 * q + 512], f == 0, f == 21))
            t = pes(fns, t_a, ch_dn[c].tok, [b.w for b in bb])
            ch_dn[c].free = [t]
        for h in range(2):
            for q in range(2):
                t_x = add_x(q, h, bb[2 * h + q].ap, t)
                bb[2 * h + q].w = [t_x]
        ar.free(now(), aT, hT, *Uz, *Ub)
        mods = ar.get(32, True)
        t_md = stt(mods.ap[:, 0:8], modc.ap[:, 8:16], 1.0, col("norm1_g_2", 0, 8), ADD, MUL, ada_tok, mods.w)
        t_md = stt(mods.ap[:, 8:16], modc.ap[:, 24:32], 1.0, col("norm2_g_2", 0, 8), ADD, MUL)
        Xn, hT = ar.get(2048), ar.get(2048)
        t = normed(x, t_x, Xn)
        t_h = to_features(Xn, t, hT, mods.ap[:, 0:8], shift=modc.ap[:, 0:8], dtok=t_md)
        ar.free(now(), Xn)
        hv = hT.v("p (k t) -> p k t", k=8)
        Q = [ar.get(1024) for _ in range(6)]
        rt = ar.get(512)
        rt_free = []
        t_q = [None] * 6
        cosb = bc(C["cos"].unsqueeze(1), [128, 2, 256])
        sinb = bc(C["sin"].unsqueeze(1), [128, 2, 256])
        GM = ar.get(4096)
        GMv = GM.v("p (k t) -> p k t", k=16)
        rtv = rt.v("p (n t) -> p n t", n=2)
        for c in range(6):
            ch = ch_i2[c]
            if c in (2, 5):
                w = ch.ap.rearrange("p (k n) -> p k n", k=8)
                for h in range(2):
                    b = ps.take()
                    t = pes([mm(b.ap, hv[:, k, 128 * h:128 * h + 128], w[:, k, :], k == 0, k == 7) for k in range(8)], t_h, ch.tok, b.w)
                    t_q[c] = acp(Q[c].ap[:, 512 * h:512 * h + 512], b.ap, t, Q[c].w)
                    b.w = [t_q[c]]
                ch.free = [t]
                continue
            for z in range(2):
                b = ps.take()
                for h in range(2):
                    t = pes(proj_fm(b, h, ch, 512, 256 * z + 128 * h, hv), t_h, ch.tok, b.w)
                bv = b.ap.rearrange("p (n t) -> p n t", n=2)
                qv = Q[c].v("p (n t) -> p n t", n=4)[:, 2 * z:2 * z + 2, :]
                t1 = acp(qv, bv, t, Q[c].w)
                b.w = [t1]
                b = ps.take()
                t2 = pe(mm(b.ap, C["perm"], Q[c].ap[:, 512 * z:512 * z + 512], True, True), t1, b.w)
                t3 = tt(rtv, b.ap.rearrange("p (n t) -> p n t", n=2), sinb, MUL, t2, rt.w, VE.last())
                b.w = [t3]
                t4 = tt(qv, qv, cosb, MUL, t3)
                t_q[c] = tt(qv, qv, rtv, ADD, t4)
            ch.free = [t]
        ar.free(now(), rt, junk)
        gate_done = []

        def gate_chain():
            for c in range(6, 10):
                ch = ch_i2[c]
                for z in range(2):
                    b = ps.take()
                    for h in range(2):
                        t = pes(proj_fm(b, h, ch, 512, 256 * z + 128 * h, hv), t_h, ch.tok, b.w)
                        if h == 0:
                            yield
                    if z:
                        ch.free = [t]
                    t_g = act(GMv[:, 4 * (c - 6) + 2 * z:4 * (c - 6) + 2 * z + 2, :], b.ap.rearrange("p (n t) -> p n t", n=2), ACT.Sigmoid, t, GM.w)
                    b.w = [t_g]
                    yield
            gate_done.append(t_g)
        S_[:] = [ar.get(512) for _ in range(3)]
        P_[:] = [ar.get(512) for _ in range(3)]
        PT_[:] = [ar.get(512) for _ in range(3)]
        a_free[:] = [[[], []] for _ in range(3)]
        st_.append(sml(12))
        OM, OD = ar.get(1024), ar.get(1024)
        OMv, ODv = OM.v("p (n t) -> p n t", n=4), OD.v("p (n t) -> p n t", n=4)
        lam = sml(6)
        lv_ = lamv.v("p (a k) -> p a k", a=4)
        lt2 = ar.get(128)
        t = tt(lt2.v("p (a k) -> p a k", a=2), lamv.v("p (a z k) -> p a z k", a=2, z=2)[:, :, 0, :],
               lamv.v("p (a z k) -> p a z k", a=2, z=2)[:, :, 1, :], MUL, par_tok, lt2.w)
        t = ve(lambda e: e.tensor_reduce(lam[:, 0:2], lt2.v("p (a k) -> p a k", a=2), AX.X, ADD), t)
        t = act(lam[:, 2:4], lam[:, 0:2], ACT.Exp, t)
        t = tt(lam[:, 4:5], lam[:, 3:4], lam[:, 2:3], SUB, t)
        t_lam = ts(lam[:, 4:5], lam[:, 4:5], -LAM0, ADD, None, None, t)
        Qv = [q.v("p (n t) -> p n t", n=4) for q in Q]
        VMv, VDv = Q[2].v("p (b d) -> p b d", b=2), Q[5].v("p (b d) -> p b d", b=2)
        om_done, od_done = [], []

        def moba_unit(i, pr, blk):
            nk = 1 + blk
            r = attn_scores(i, [hrow(Qv[0][:, pr, :], h) for h in range(2)], [hrow(Qv[1][:, pr, :], h) for h in range(2)],
                            blk, nk, causal(nk), [t_q[0], t_q[1]])
            yield
            yield from attn_out(*r, nk, [(lambda j, h=2 * pr + h: VMv[:, j, 64 * h:64 * h + 64]) for h in range(2)],
                                OMv[:, pr, 128 * blk:128 * blk + 128], t_q[2], OM.w, om_done)

        def diff_unit(i, pr, blk):
            nk = 1 + blk
            _, pv, rc, t5, w = attn_scores(i, [hrow(Qv[3][:, pr, :], h) for h in range(2)], [hrow(Qv[4][:, pr, :], h) for h in range(2)],
                                           blk, nk, causal(nk), [t_q[3], t_q[4]])
            yield
            PT = PT_[i]
            t6 = ts(pv[:, 1, :], pv[:, 1, :], rc[:, 1:2], MUL, lam[:, 4:5], MUL, t5, t_lam)
            t6 = stt(pv[:, 0, :], pv[:, 0, :], rc[:, 0:1], pv[:, 1, :], MUL, ADD, t6)
            b = ps.take()
            t7 = pes([tr(b.ap[:, 128 * j:128 * j + 128], pv[:, 0, 128 * j:128 * j + 128], ident) for j in range(nk)], t6, b.w)
            t8 = acp(PT.ap[:, 0:w], b.ap[:, 0:w], t7, a_free[i][1], PT.w)
            b.w = [t8]
            yield
            b = ps.take()
            t9 = pes([mm(b.ap[:, 0:128], VDv[:, j, 128 * pr:128 * pr + 128], PT.ap[:, 128 * j:128 * j + 128], j == 0, j == nk - 1)
                      for j in range(nk)], t8, t_q[5], b.w)
            t10 = acp(ODv[:, pr, 128 * blk:128 * blk + 128], b.ap[:, 0:128], t9, OD.w)
            b.w = [t10]
            a_free[i] = [[t7, t6], [t9]]
            od_done.append(t10)
        units = [(f, pr, blk) for pr in range(4) for blk in range(2) for f in (moba_unit, diff_unit)]
        interleave(ps, (gate_chain(), [6, 7]), [(unit_chain(i, units[i::3]), [2 * i, 2 * i + 1], 1.3) for i in range(3)])
        t_g, t_od = gate_done, od_done
        ar.free(now(), hT)
        ar.free(now(), *S_, *P_, *PT_, *Q, lt2, lamv)
        sq, rs = ar.get(1024), ar.get(512)
        g8 = sml(1)
        t8 = ts(g8, col("diff_subln_g_2"), 1.0 - LAM0, MUL, None, None, t_par)
        t = tt(sq.ap, OD.ap, OD.ap, MUL, t_od, sq.w)
        t_rs = head_rstd([sq.ap[:, 256 * i:256 * i + 256] for i in range(4)], [t, *rs.w], 128.0, 1e-6, rs.ap, 16, sel="hs2")
        for i in range(4):
            b = ps.take()
            t = pe(head_bcast(b, 0, i, rs.ap), t_rs, b.w)
            t_od = stt(ODv[:, i, :], ODv[:, i, :], g8, b.ap[:, 0:256], MUL, MUL, t, t8)
            b.w = [t_od]
        ar.free(now(), sq, rs)
        mg = ar.get(2048)
        mgv = mg.v("p (k t) -> p k t", k=8)
        for ch, src, z, tk in ((ch_pm, OMv, 0, om_done), (ch_pd, ODv, 8, t_od)):
            for n in range(0, 8, 2):
                b = ps.take()
                for h in range(2):
                    t = pes(proj_fm(b, h, ch, 1024, 128 * (n + h), src, k_n=4), tk, ch.tok, b.w)
                bv = b.ap.rearrange("p (n t) -> p n t", n=2)
                gv = GMv[:, z + n:z + n + 2, :]
                if z == 0:
                    t_mg = tt(mgv[:, n:n + 2, :], bv, gv, MUL, t, t_g, mg.w)
                    b.w = [t_mg]
                else:
                    t2 = tt(gv, bv, gv, MUL, t, t_g)
                    b.w = [t2]
                    t_mg = tt(mgv[:, n:n + 2, :], mgv[:, n:n + 2, :], gv, ADD, t2)
            ch.free = [t]

        ar.free(now(), GM, OM, OD)
        slot7 = ar.get(4096)
        ring.aps[6], ring.lent[6] = slot7.ap, slot7.w
        gt = ar.get(512, True)

        def add_gated(gb):
            def f(c, h, bank, t):
                v = x[:, h, 512 * c:512 * c + 512]
                t = tt(gt.ap, bank, gb.ap[:, 512 * c:512 * c + 512], MUL, t, gt.w, VE.last() if cur["ve"] is VE else None)
                tt(v, v, gt.ap, ADD, t)
                return cur["ve"].last()
            return f
        t_x = token_out(ch_o2, mgv, add_gated(g1b), [t_mg, ada_tok])
        ar.free(now(), mg, g1b)
        junk = ar.get(1024)
        w36, b36 = ar.get(288), ar.get(36)
        w36v = w36.v("p (k n) -> p k n", k=8)
        later([*w36.w, *b36.w], [
            (w36v[:, :, 0:4], A["w_group_2"][0, :, :].rearrange("(k p) n -> p k n", p=128)),
            (w36v[:, :, 4:36], A["w_expert_2"][0, :, :].rearrange("(k p) n -> p k n", p=128)),
            (b36.ap[:, 0:4], bc(A["b_group_2"], [128, 4])), (b36.ap[:, 4:36], bc(A["b_expert_2"], [128, 32]))], s_rt)
        X2, hT = ar.get(2048, True), ar.get(2048)
        t = normed(x, t_x, X2)
        t_x2 = t
        t_h = to_features(X2, t, hT, mods.ap[:, 8:16], shift=modc.ap[:, 16:24], dtok=t_md)
        hv = hT.v("p (k t) -> p k t", k=8)
        b = ps.take()
        t = pes([mm(b.ap[:, 36 * h:36 * h + 36], hv[:, k, 128 * h:128 * h + 128], w36v[:, k, :], k == 0, k == 7)
                 for h in range(2) for k in range(8)], t_h, (s_rt, 64), b.w)
        lg = ar.get(72)
        lgv = lg.v("p (b n) -> p b n", b=2)
        t_lg = tt(lgv, b.ap[:, 0:72].rearrange("p (b n) -> p b n", b=2), bc(b36.ap[:, 0:36].unsqueeze(1), [128, 2, 36]), ADD, t, lg.w)
        b.w = [t_lg]
        R = ar.get(640)
        ro = [0]

        def rget(n, pat="p (b n) -> p b n"):
            o = ro[0]
            ro[0] += 2 * n
            return R.ap[:, o:o + 2 * n].rearrange(pat, b=2)

        def chain(f, *w):
            return ve(f, VE.last(), *w)

        def first_max(src, n, key, dst, mx):
            kt_ = rget(n)
            chain(lambda e: e.tensor_reduce(mx, src, AX.X, MAX), t_lg, R.w)
            chain(lambda e: e.tensor_tensor(kt_, src, bc(mx, [128, 2, n]), EQ))
            chain(lambda e: e.tensor_tensor(kt_, kt_, bc(key.unsqueeze(1), [128, 2, n]), MUL))
            km = rget(1)
            chain(lambda e: e.tensor_reduce(km, kt_, AX.X, MAX))
            return chain(lambda e: e.tensor_tensor(dst, kt_, bc(km, [128, 2, n]), EQ))

        def softmax_parts(src, mx, n):
            nm, ee, zz = rget(1), rget(n), rget(1)
            t = chain(lambda e: e.tensor_scalar(nm, mx, -1.0, None, MUL))
            for i in range(2):
                t = act(ee[:, i, :], src[:, i, :], ACT.Exp, t, SC.last(), bias=nm[:, i, :], accum=zz[:, i, :])
            chain(lambda e: e.reciprocal(zz, zz), t)
            return ee, zz
        mxg, ohg = rget(1), rget(4)
        first_max(lgv[:, :, 0:4], 4, C["key4"], ohg, mxg)
        _, gw = softmax_parts(lgv[:, :, 0:4], mxg, 4)
        em = rget(32)
        of = rget(4)
        chain(lambda e: e.tensor_scalar(of, ohg, -1.0, -NEG, ADD, MUL))
        for i in range(2):
            v8 = em[:, i, :].rearrange("p (g n) -> p g n", g=4)
            chain(lambda e, i=i, v8=v8: e.tensor_tensor(v8, lgv[:, i, 4:36].rearrange("p (g n) -> p g n", g=4), bc(ohg[:, i, :].unsqueeze(2), [128, 4, 8]), MUL))
            chain(lambda e, i=i, v8=v8: e.tensor_tensor(v8, v8, bc(of[:, i, :].unsqueeze(2), [128, 4, 8]), ADD))
        mx1, oh1 = rget(1), rget(32)
        first_max(em, 32, C["key32"], oh1, mx1)
        ee, zz = softmax_parts(em, mx1, 32)
        chain(lambda e: e.tensor_tensor(ee, ee, bc(zz, [128, 2, 32]), MUL))
        chain(lambda e: e.scalar_tensor_tensor(out=em, in0=oh1, scalar=NEG, in1=em, op0=MUL, op1=ADD))
        mx2, oh2 = rget(1), rget(32)
        first_max(em, 32, C["key32"], oh2, mx2)
        RK = ar.get(192, True)
        Aa, Ww, rk = (RK.ap[:, 64 * i:64 * i + 64].rearrange("p (b n) -> p b n", b=2) for i in range(3))
        chain(lambda e: e.tensor_tensor(Aa, oh1, oh2, ADD), RK.w)
        chain(lambda e: e.tensor_tensor(Ww, Aa, ee, MUL))
        tot = rget(1)
        chain(lambda e: e.tensor_reduce(tot, Ww, AX.X, ADD))
        chain(lambda e: e.reciprocal(tot, tot))
        chain(lambda e: e.tensor_tensor(tot, tot, gw, MUL))
        t_ww = chain(lambda e: e.tensor_tensor(Ww, Ww, bc(tot, [128, 2, 32]), MUL))
        b = ps.take()
        t = pes([mm(b.ap[:, 0:32], C["SU"], Aa[:, 0, :], True, True), mm(b.ap[:, 32:64], ones, Aa[:, 0, :], True, False),
                 mm(b.ap[:, 32:64], C["SU"], Aa[:, 1, :], False, True), mm(b.ap[:, 64:96], ones, Aa[:, 0, :], True, False),
                 mm(b.ap[:, 64:96], ones, Aa[:, 1, :], False, True)], t_ww, b.w)
        cntf, cnti = sml(1), sml(1)
        chain(lambda e, b=b: e.tensor_reduce(cntf, b.ap[:, 64:96], AX.X, MAX), t)
        t_cnt = chain(lambda e: e.tensor_copy(cnti.bitcast(I32), cntf))
        chain(lambda e, b=b: e.scalar_tensor_tensor(out=rk, in0=b.ap[:, 0:64].rearrange("p (b n) -> p b n", b=2), scalar=1.0, in1=Aa, op0=ADD, op1=MUL))
        t_rk = chain(lambda e: e.tensor_scalar(rk, rk, -1.0, None, ADD))
        b.w = [t_rk]
        ar.free(now(), hT, w36, b36, lg, R, junk)
        xg = [ar.get(2048), ar.get(2048)]
        Pb, PwT = ar.get(2048), ar.get(2048)
        sgl, hh, hts, ost = ([ar.get(n) for _ in range(2)] for n in (256, 256, 128, 1024))
        g_ps = psum

        def moe_round(chs, start, first):
            Pv = Pb.v("p (b e s) -> p b e s", b=2, e=32)
            xgv = [g.v("p (k s) -> p k s", k=8) for g in xg]
            X2v = X2.v("p (b d) -> p b d", b=2)
            bw = {i: [] for i in range(8)}
            tk = start
            if not first:
                tk = ts(rk, rk, -float(NSLOT), ADD, None, None, tk)
            for i in range(2):
                tP = tt(Pv[:, i, :, :], bc(rk[:, i, :].unsqueeze(2), [128, 32, 32]), bc(C["iota"].unsqueeze(1), [128, 32, 32]), EQ,
                        tk, start, Pb.w)
            bi = [0]

            def nb():
                r = 4 + bi[0] % 4
                bi[0] += 1
                return r
            t_xg = [[] for _ in range(4)]
            xg_free = [[], []]

            def gather(qu, ks):
                for k in ks:
                    q = nb()
                    t = pes([mm(g_ps[q][:, 0:256], X2v[:, i, 128 * k:128 * k + 128], Pv[:, i, 8 * qu:8 * qu + 8, :].rearrange("p e s -> p (e s)"),
                                i == 0, i == 1) for i in range(2)], tP, start, bw[q])
                    o = xgv[qu % 2][:, k, :]
                    if k % 2:
                        t = ts(o, g_ps[q][:, 0:256], mods.ap[:, 8 + k:9 + k], MUL, modc.ap[:, 16 + k:17 + k], ADD, t, start, xg[qu % 2].w, xg_free[qu % 2])
                    else:
                        t = act(o, g_ps[q][:, 0:256], ACT.Identity, t, start, xg[qu % 2].w, xg_free[qu % 2],
                                scale=mods.ap[:, 8 + k:9 + k], bias=modc.ap[:, 16 + k:17 + k])
                    bw[q] = [t]
                    t_xg[qu].append(t)
            t_pw = []
            fre = {"sg": [[], []], "hh": [[], []], "ht": [[], []], "os": [[], []]}

            def weights():
                for i in range(2):
                    tw = tt(ost[i].v("p (e s) -> p e s", e=32), Pv[:, i, :, :], bc(Ww[:, i, :].unsqueeze(2), [128, 32, 32]), MUL, tP, ost[i].w)
                    for g4 in range(0, 8, 4):
                        q = nb()
                        t = pes([tr(g_ps[q][:, 128 * z:128 * z + 128], ost[i].ap[:, 128 * (g4 + z):128 * (g4 + z) + 128], ident) for z in range(4)], tw, bw[q])
                        fre["os"][i] = [t]
                        t = acp(PwT.v("p (g t) -> p g t", g=8)[:, g4:g4 + 4, 128 * i:128 * i + 128],
                                g_ps[q][:, :].rearrange("p (g t) -> p g t", g=4), t, PwT.w, start)
                        bw[q] = [t]
                        t_pw.append(t)
            PwTv = PwT.v("p (g t) -> p g t", g=8)
            t_gu, t_hh, t_ost = {}, {}, {}

            def gate_up(e):
                q = 4 + e % 2
                cg, cu = chs[e][0], chs[e][1]
                wg = cg.ap.rearrange("p (k n) -> p k n", k=8)
                wu = cu.ap.rearrange("p (k n) -> p k n", k=8)
                fns = []
                for k in range(8):
                    for j in range(4):
                        w = (wg if j < 2 else wu)[:, k, 256 * (j % 2):256 * (j % 2) + 256]
                        fns.append(mm(g_ps[q][32 * j:32 * j + 32, 0:256], xgv[e // 8 % 2][:, k, 32 * (e % 8):32 * (e % 8) + 32], w, k == 0, k == 7))
                t = pes(fns, t_xg[e // 8], cg.tok, cu.tok, bw[q])
                cg.free = cu.free = [t]
                xg_free[e // 8 % 2] = [t]
                i = e % 2
                t1 = act(sgl[i].ap[0:64, :], g_ps[q][0:64, 0:256], ACT.Silu, t, sgl[i].w, fre["sg"][i])
                t2 = tt(hh[i].ap[0:64, :], g_ps[q][64:128, 0:256], sgl[i].ap[0:64, :], MUL, t1, hh[i].w, fre["hh"][i])
                bw[q] = [t2]
                fre["sg"][i] = [t2]
                t_hh[e] = t2

            def down(e):
                i = e % 2
                t = pes([tr(g_ps[6][:, 64 * c:64 * c + 64], hh[i].ap[0:64, 128 * c:128 * c + 128], ident[0:64, 0:64]) for c in range(2)],
                        t_hh[e], bw[6])
                fre["hh"][i] = [t]
                t = acp(hts[i].ap, g_ps[6][:, 0:128], t, hts[i].w, fre["ht"][i])
                bw[6] = [t]
                cd = chs[e][2]
                wd = cd.ap.rearrange("p (k n) -> p k n", k=4)
                fns = []
                for f in range(4):
                    o = 64 * (f % 2) + 32 * (f // 2)
                    for j in range(4):
                        fns.append(mm(g_ps[7][32 * j:32 * j + 32, 0:256], hts[i].ap[:, o:o + 32], wd[:, f, 256 * j:256 * j + 256], f == 0, f == 3))
                t = pes(fns, t, cd.tok, bw[7])
                cd.free = [t]
                fre["ht"][i] = [t]
                g, r = e // 4, 32 * (e % 4)
                o = ost[g % 2]
                tw = []
                for j in range(4):
                    d, s_ = o.ap[r:r + 32, 256 * j:256 * j + 256], g_ps[7][32 * j:32 * j + 32, 0:256]
                    tw.append((acp if j % 2 else vcp)(d, s_, t, o.w, fre["os"][g % 2]))
                bw[7] = tw
                t_ost.setdefault(g, []).extend(tw)

            def combine(g):
                t = pes([mm(g_ps[2 * b_ + h_][:, :], PwTv[:, g, 128 * b_:128 * b_ + 128], ost[g % 2].ap[:, 512 * h_:512 * h_ + 512], g == 0, g == 7)
                         for b_ in range(2) for h_ in range(2)], t_ost[g], t_pw, start)
                fre["os"][g % 2] = [t]
                return t
            gather(0, range(8))
            gate_up(0)
            for e in range(NE):
                if e + 1 < NE:
                    gate_up(e + 1)
                if e == 0:
                    weights()
                if e < 24 and e % 8 in (2, 3, 4, 5):
                    gather(e // 8 + 1, range(2 * (e % 8) - 4, 2 * (e % 8) - 2))
                if e % 4 == 1 and e > 4:
                    combine(e // 4 - 1)
                down(e)
            t = combine(7)
            for h_ in range(2):
                for b_ in range(2):
                    v = x[:, b_, 512 * h_:512 * h_ + 512]
                    t1 = tt(gt.ap, g_ps[2 * b_ + h_][:, :], g2b.ap[:, 512 * h_:512 * h_ + 512], MUL, t, gt.w, cur["ve"].last())
                    t1 = tt(v, v, gt.ap, ADD, t1)
            return t1
        t_x = moe_round(ch_e, [*now(), t_rk], True)
        main_end = now()
        LP = {"pe": Lane(sem("l_pe")), "ve": Lane(sem("l_ve")), "sc": Lane(sem("l_sc")), "gp": Lane(sem("l_gp"))}
        ring2 = Ring([ringt[:, i, :] for i in range(NS)], [sem(f"l_ring{i}") for i in range(NS)])
        cur.update(LP)
        for bf in (Pb, PwT, *xg, *sgl, *hh, *hts, *ost, gt):
            bf.w = []
        ch_e2 = [load_expert(ring2, e) for e in range(NE)]
        moe_round(ch_e2, [], False)
        FN = {"pe": Lane(sem("f_pe")), "ve": Lane(sem("f_ve")), "sc": Lane(sem("f_sc")), "gp": Lane(sem("f_gp"))}
        cur.update(FN)
        s, r = sml(2), sml(2)
        for i in range(2):
            t1 = act(xg[0].ap[:, 1024 * i:1024 * i + 1024], x[:, i, :], ACT.Square, accum=s[:, i:i + 1])
        t2 = ts(r, s, 1.0 / 1024, MUL, 1e-6, ADD, t1)
        t3 = ve(lambda e: e.reciprocal(s, r), t2)
        t3 = act(r, s, ACT.Sqrt, t3)
        for i in range(2):
            t_fin = stt(x[:, i, :], x[:, i, :], r[:, i:i + 1], Pb.ap[:, 0:1024], MUL, MUL, t3, (s_fg, 16))
        block = ctx.enter_context(nc.Block())


        def rounds(eng, body, me):
            n = eng.value_load(cnti[0:1, 0:1].bitcast(mybir.dt.int32), min_val=0, max_val=256)
            with eng.If(n > NSLOT):
                with eng.Fori(NSLOT, n, NSLOT):
                    body(eng)
                    if me is None:
                        for k in ("pe", "ve", "sc"):
                            eng.wait_ge(*LP[k].last())
                        eng.wait_ge(s_done2, 3)
                        for k in ("pe", "ve", "sc"):
                            eng.sem_clear(LP[k].sem)
                        for q in ring2.sems:
                            eng.sem_clear(q)
                        eng.sem_clear(s_done2)
                        for q in s_go[0:3]:
                            eng.sem_inc(q, 1)
                    else:
                        eng.sem_inc(s_done2, 1)
                        eng.wait_ge(s_go[me], 1)
                        eng.sem_clear(s_go[me])

        @block.sync
        def _(e):
            ring.play(e)
            for w in main_end:
                e.wait_ge(*w)
            rounds(e, ring2.play, None)
            e.dma_start(Pb.ap[:, 0:1024], A["final_g_2"].rearrange("(a d) -> a d", a=1).to_broadcast([128, 1024])).then_inc(s_fg, 16)
            e.wait_ge(*t_fin)
            e.dma_start(out.rearrange("a (b p) d -> p (a b) d", p=128), x).then_inc(s_out, 16)
            e.wait_ge(s_out, 16)

        def compute(e, lane, k, me):
            lane.play(e)
            for w in main_end:
                e.wait_ge(*w)
            rounds(e, LP[k].play, me)
            FN[k].play(e)

        @block.scalar
        def _(e):
            load_first(e)
            compute(e, SC, "sc", 0)

        @block.vector
        def _(e):
            compute(e, VE, "ve", 1)

        @block.gpsimd
        def _(e):
            pdma(e, plist2, s_par2)
            GP.play(e)

        @block.tensor
        def _(e):
            compute(e, PE, "pe", 2)


_INS = ["x", "mem", "rel_bias", "mix_norm_g", "w_in", "attn_q_norm", "attn_k_norm", "attn_sinks", "rwkv_mu", "rwkv_w0",
        "rwkv_w2", "rwkv_a0", "rwkv_a2", "rwkv_g2", "rwkv_k_k", "rwkv_k_a", "rwkv_r_k", "rwkv_ln_w", "rwkv_ln_b",
        "mem_norm_g", "w_mem_kv", "mem_q_norm", "mem_k_norm", "w_out", "ffn_norm_g", "w_up", "conv_w", "conv_b", "w_down",
        "c_2", "w_ada_2", "b_ada_2", "norm1_g_2", "w_in_2", "lambda_q1_2", "lambda_k1_2", "lambda_q2_2", "lambda_k2_2",
        "diff_subln_g_2", "w_proj_moba_2", "w_proj_diff_2", "w_out_2", "norm2_g_2", "w_group_2", "b_group_2", "w_expert_2",
        "b_expert_2", "w_gate_2", "w_up_2", "w_down_2", "final_g_2"]


def kernel(**inputs):
    import concourse.bacc as bacc
    from concourse.bass_utils import run_bass_kernel_spmd

    nc = bacc.Bacc("TRN2", target_bir_lowering=False, num_devices=1)
    arrays, aps = {}, {}
    named = [(n, np.ascontiguousarray(inputs[n])) for n in _INS] + [("consts", const_table())]
    for name, a in named:
        arrays[f"in_{name}"] = a
        aps[name] = nc.dram_tensor(f"in_{name}", a.shape, mybir.dt.from_np(a.dtype), kind="ExternalInput").ap()
    out = nc.dram_tensor("out_0", (1, T, D), mybir.dt.float32, kind="ExternalOutput").ap()
    block_kernel(nc, aps, out)
    r = run_bass_kernel_spmd(nc, [arrays], core_ids=[0])
    return r.results[0]["out_0"]
```

```python
import math

import numpy as np

import concourse.bass as bass
from concourse import mybir

T = 256
D = 1024
KT = 8
NEG = -1.0e30
LAM0 = 0.8 - 0.6 * math.exp(-0.3 * 0)
NSLOT = 32
NE = 32


def const_layout():
    names = [("ident", 128), ("ones", 128), ("perm", 128), ("cos", 256), ("sin", 256),
             ("caus", 128), ("SU", 128), ("IU", 128),
             ("iota", 32), ("key4", 4), ("key32", 32), ("hs", 30), ("hs2", 30), ("OHB", 1024),
             ("bo", 128), ("rev", 128), ("LM", 7 * 128), ("LM1T", 128), ("MR", 384)]
    at, off = {}, 0
    for n, w in names:
        at[n] = (off, w)
        off += w
    return at, off


def const_table():
    at, width = const_layout()
    c = np.zeros((128, width), np.float32)

    def put(name, a, rows=128):
        o, w = at[name]
        c[:rows, o:o + w] = a

    p = np.arange(128)
    t, j = p[:, None], p[None, :]
    put("ident", np.eye(128))
    put("rev", np.eye(128)[::-1])
    put("bo", (t // 64 == j // 64))
    put("ones", 1.0)
    pm = np.zeros((128, 128), np.float32)
    for o in range(128):
        if o % 64 < 32:
            pm[o + 32, o] = -1.0
        else:
            pm[o - 32, o] = 1.0
    put("perm", pm)
    inv = (1.0 / (np.float32(10000.0) ** (np.arange(0, 64, 2, dtype=np.float32) / np.float32(64)))).astype(np.float32)
    ang = (np.arange(T, dtype=np.float32)[:, None] * inv[None, :]).astype(np.float32)
    put("cos", np.cos(ang).astype(np.float32).T[p % 32])
    put("sin", np.sin(ang).astype(np.float32).T[p % 32])
    put("caus", np.where(j > t, NEG, 0.0))
    put("SU", t < j)
    put("IU", t <= j)
    lm = [((t // (2 * s) == j // (2 * s)) & (t % (2 * s) >= s) & (j % (2 * s) < s)) for s in (1, 2, 4, 8, 16, 32, 64)]
    put("LM", np.concatenate(lm, 1))
    put("LM1T", lm[0].T)
    put("iota", np.arange(32)[None, :])
    put("key4", 8 - np.arange(4)[None, :])
    put("key32", 64 - np.arange(32)[None, :])
    hs = np.zeros((128, 30), np.float32)
    hs[:64, 14] = 1
    hs[64:, 15] = 1
    put("hs", hs)
    h2 = np.zeros((128, 30), np.float32)
    h2[:, 14:16] = 1
    put("hs2", h2)
    m = np.arange(384)
    dist = 255 - m
    ok = (dist >= 0) & (dist < 128)
    d = np.maximum(dist, 1).astype(np.float32)
    large = 16 + (np.log(d / np.float32(16)) / np.float32(math.log(8)) * np.float32(16)).astype(np.int32)
    bucket = np.where(dist < 16, np.maximum(dist, 0), np.minimum(large, 31))
    ob = np.zeros((128, 1024), np.float32)
    ob[64:96, 0:384] = (np.arange(32)[:, None] == bucket[None, :]) & ok[None, :]
    ob[0:16] = np.arange(16)[:, None] == np.arange(1024)[None, :] // 64
    put("OHB", ob)
    put("MR", np.where(ok, 0.0, NEG)[None, :].repeat(6, 0), 6)
    return c


PARAMS = [("mix_norm_g", 8), ("mem_norm_g", 8), ("ffn_norm_g", 8), ("norm1_g_2", 8), ("norm2_g_2", 8), ("c_2", 8),
          ("rwkv_mu", 10), ("rwkv_w0", 3), ("rwkv_a0", 3), ("rwkv_k_k", 3), ("rwkv_k_a", 3), ("rwkv_r_k", 3),
          ("rwkv_ln_w", 3), ("rwkv_ln_b", 3), ("diff_subln_g_2", 1),
          ("attn_q_norm", 1), ("attn_k_norm", 1), ("mem_q_norm", 1), ("mem_k_norm", 1),
          ("", 44), ("b_ada_2", 48), ("conv_b", 44), ("conv_w", 132)]


class Lane:

    def __init__(self, sem):
        self.sem, self.n, self.items = sem, 0, []

    def op(self, fn, *waits):
        self.n += 1
        self.items.append((fn, waits))
        return (self.sem, self.n)

    def job(self, fn, *waits):
        self.items.append((fn, waits))

    def last(self):
        return (self.sem, self.n)

    def play(self, eng):
        seen = {}

        def wait(w):
            if w is None:
                return
            if isinstance(w, list):
                for x in w:
                    wait(x)
                return
            sem, v = w
            if v > 0 and seen.get(id(sem), 0) < v:
                eng.wait_ge(sem, v)
                seen[id(sem)] = v

        for fn, waits in self.items:
            for w in waits:
                wait(w)
            r = fn(eng)
            if r is not None:
                r.then_inc(self.sem, 1)


class Bank:
    def __init__(self, ap):
        self.ap, self.w = ap, []


class Banks:

    def __init__(self, banks):
        self.all = banks
        self.pool = Pool(banks)

    def take(self):
        return self.pool.take()


class Pool:
    def __init__(self, banks):
        self.banks, self.i = list(banks), 0

    def take(self):
        self.i += 1
        return self.banks[(self.i - 1) % len(self.banks)]


def interleave(ps, lead, others):
    lead_gen, lead_banks = lead
    pools = [(g, Pool([ps.all[i] for i in b]), n) for g, b, n in others]
    lead_pool = Pool([ps.all[i] for i in lead_banks])

    def step(g, pool):
        ps.pool = pool
        try:
            next(g)
            return True
        except StopIteration:
            return False
    alive = True
    credit = [0.0] * len(pools)
    while alive or pools:
        if alive:
            alive = step(lead_gen, lead_pool)
        for q, (_, _, n) in enumerate(pools):
            credit[q] += n if alive else 1.0
        keep, kc = [], []
        for q, (g, pool, n) in enumerate(pools):
            ok = True
            while ok and credit[q] >= 1.0:
                credit[q] -= 1.0
                ok = step(g, pool)
            if ok:
                keep.append((g, pool, n))
                kc.append(credit[q])
            else:
                lead_pool.banks += pool.banks
        pools, credit = keep, kc
    ps.pool = Pool(ps.all)


class Chunk:
    def __init__(self, ring, slot, parts, sem, value, before):
        self.ring, self.slot, self.parts, self.sem, self.tok, self.before, self.free = ring, slot, parts, sem, (sem, value), before, None

    @property
    def ap(self):
        return self.ring.aps[self.slot]


class Ring:

    def __init__(self, aps, sems):
        self.aps, self.sems, self.counts, self.chunks = aps, sems, [0] * len(aps), []
        self.order, self.at, self.lent = list(range(len(aps))), 0, {}
        self.holder = [None] * len(aps)

    def use(self, slots):
        self.order, self.at = slots, 0

    def load(self, *parts):
        s = self.order[self.at % len(self.order)]
        self.at += 1
        before = self.holder[s]
        self.counts[s] += 16 * len(parts)
        c = Chunk(self, s, parts, self.sems[s], self.counts[s], before)
        self.chunks.append(c)
        self.holder[s] = c
        return c

    def play(self, eng):
        for c in self.chunks:
            if c.before is not None:
                if c.before.free is None:
                    break
                for w in c.before.free:
                    eng.wait_ge(*w)
            else:
                for w in self.lent.get(c.slot, []):
                    eng.wait_ge(*w)
            for dst, src in c.parts:
                eng.dma_start(dst(c.ap), src).then_inc(c.sem, 16)


class Arena:

    def __init__(self, ap, width):
        self.ap, self.regions, self.top = ap, [[0, width, []]], 0

    def get(self, n, high=False):
        if high:
            for r in reversed(self.regions):
                if r[1] >= n:
                    r[1] -= n
                    b = Buf(self.ap[:, r[0] + r[1]:r[0] + r[1] + n], r[0] + r[1], n, list(r[2]))
                    if r[1] == 0:
                        self.regions.remove(r)
                    return b
        best = None
        for r in self.regions:
            if r[1] >= n and (best is None or r[1] < best[1]):
                best = r
        if best is None:
            raise ValueError(f"arena full: {n} of {self.regions}")
        b = Buf(self.ap[:, best[0]:best[0] + n], best[0], n, list(best[2]))
        best[0] += n
        best[1] -= n
        self.top = max(self.top, b.off + n)
        if best[1] == 0:
            self.regions.remove(best)
        return b

    def free(self, tokens, *bufs):
        for b in bufs:
            self.regions.append([b.off, b.n, list(tokens)])
        self.regions.sort(key=lambda r: r[0])
        out = []
        for r in self.regions:
            if out and out[-1][0] + out[-1][1] == r[0]:
                out[-1][1] += r[1]
                top = {}
                for s, v in out[-1][2] + r[2]:
                    top[id(s)] = (s, max(v, top.get(id(s), (s, 0))[1]))
                out[-1][2] = list(top.values())
            else:
                out.append([r[0], r[1], list(r[2])])
        self.regions = out


class Buf:
    def __init__(self, ap, off, n, w):
        self.ap, self.off, self.n, self.w, self.home = ap, off, n, w, None

    def v(self, pat, **k):
        return self.ap.rearrange(pat, **k)


def block_kernel(nc, A, out):
    from contextlib import ExitStack
    F = mybir.dt.float32
    I32 = mybir.dt.int32
    ALU = mybir.AluOpType
    ACT = mybir.ActivationFunctionType
    AX = mybir.AxisListType
    MUL, ADD, SUB, MAX, EQ = ALU.mult, ALU.add, ALU.subtract, ALU.max, ALU.is_equal
    NS = 6
    CL, CW = const_layout()
    NSEG = 28632

    ctx = ExitStack()
    with ctx:
        def sb(name, shape, dt=F):
            return ctx.enter_context(nc.sbuf_tensor(name, shape, dt))

        def sem(name):
            return ctx.enter_context(nc.semaphore(name))

        ring_a = sb("ring_a", [128, 3, 4096])
        with nc.sbuf_tensor("ring_r", [128, 3, 4096], mybir.dt.float32r) as ring_r:
            pass
        ring_b = sb("ring_b", [128, 3, 4096])
        with nc.sbuf_tensor("arena_r", [128, NSEG], mybir.dt.float32r) as arena_r:
            pass
        arena_t = sb("arena", [128, NSEG])
        slots = [r[:, i, :] for r in (ring_a, ring_b) for i in range(3)]
        psum = [ctx.enter_context(nc.psum_tensor(f"ps{i}", [128, 512], F)) for i in range(8)]
        scratch = nc.dram_tensor("bias_scratch", [6, 384], F, kind="Internal")

        ar = Arena(arena_t, NSEG)
        ar2 = Arena(ring_b[:, :, :].rearrange("p a n -> p (a n)"), 3 * 4096)

        def as_r(b):
            return arena_r[:, b.off:b.off + b.n]

        def rbuf(n):
            for a in (ar2, ar):
                if any(r[1] >= n for r in a.regions):
                    b = a.get(n)
                    b.home = a
                    return b
            return ar.get(n)

        def rfree(*bufs):
            for b in bufs:
                b.home.free(now(), b)
        PE, VE, SC, GP = Lane(sem("s_pe")), Lane(sem("s_ve")), Lane(sem("s_sc")), Lane(sem("s_gp"))
        ring = Ring(slots + [None], [sem(f"s_ring{i}") for i in range(NS + 1)])
        s_par = sem("s_par")
        s_par2 = sem("s_par2")
        s_x, s_mem = sem("s_x"), sem("s_mem")
        s_cst, s_cst2 = sem("s_cst"), sem("s_cst2")
        s_bias = sem("s_bias")
        s_out = sem("s_out")
        s_gb = sem("s_gb")
        s_rt = sem("s_rt")
        s_fg = sem("s_fg")
        s_x2 = sem("s_x2")
        s_done, s_done2 = sem("s_done"), sem("s_done2")
        s_go = [sem(f"s_go{i}") for i in range(4)]

        def later(waits, parts, sm):
            def run(e):
                for d, s_ in parts:
                    e.dma_start(d, s_).then_inc(sm, 16)
                return None
            GP.job(run, waits)
        ps = Banks([Bank(p[:, :]) for p in psum])
        cur = {"pe": PE, "ve": VE, "sc": SC, "gp": GP}

        def pe(fn, *w):
            return cur["pe"].op(fn, *w)

        def ve(fn, *w):
            return cur["ve"].op(fn, *w)

        def sc(fn, *w):
            return cur["sc"].op(fn, *w)

        def gp(fn, *w):
            return cur["gp"].op(fn, *w)

        def now():
            return [PE.last(), VE.last(), SC.last(), GP.last()]

        def tt(o, a, b, op, *w):
            return ve(lambda e: e.tensor_tensor(o, a, b, op), *w)

        def ts(o, a, s1, op0, s2, op1, *w):
            if s2 is None:
                return ve(lambda e: e.tensor_scalar(o, a, s1, None, op0), *w)
            return ve(lambda e: e.tensor_scalar(o, a, s1, s2, op0, op1), *w)

        def stt(o, a, s, b, op0, op1, *w):
            return ve(lambda e: e.scalar_tensor_tensor(out=o, in0=a, scalar=s, in1=b, op0=op0, op1=op1), *w)

        def vcp(o, a, *w):
            return ve(lambda e: e.tensor_copy(o, a), *w)

        def act(o, a, f, *w, bias=0.0, scale=1.0, accum=None):
            if accum is None:
                return sc(lambda e: e.activation(o, a, f, bias=bias, scale=scale), *w)
            return sc(lambda e: e.activation(o, a, f, bias=bias, scale=scale, accum_out=accum), *w)

        def acp(o, a, *w):
            return sc(lambda e: e.activation(o, a, ACT.Copy), *w)

        def mm(o, l, r, start, stop):
            return lambda e: e.matmul(o, l, r, start=start, stop=stop, skip_group_check=True)

        def tr(o, i, ident):
            return lambda e: e.transpose(o, i, ident)

        def pes(fns, *w):
            def run(e):
                for f in fns:
                    last = f(e)
                return last
            return pe(run, *w)

        def bc(ap, shape):
            return ap.to_broadcast(shape)

        CA = CL["bo"][0]
        cst = ar.get(CA)
        C = {n: cst.ap[:, o:o + w] for n, (o, w) in CL.items() if o < CA}
        par = ar.get(384)
        X = ar.get(2048)
        x = X.v("p (b d) -> p b d", b=2)
        small = ar.get(160)
        sm_at = [0]

        def sml(n):
            o = sm_at[0]
            sm_at[0] += n
            if sm_at[0] > 160:
                raise ValueError("small")
            return small.ap[:, o:o + n]

        cst2 = ar.get(CW - CA)
        C.update({n: cst2.ap[:, o - CA:o - CA + w] for n, (o, w) in CL.items() if o >= CA})
        rows = ar.get(384)
        Xm = ar.get(2048)
        xm = Xm.v("p (b d) -> p b d", b=2)
        swb = ar.get(1536)
        L2 = ar.get(384)
        relb = ar.get(8)
        sink = ar.get(8)
        lamv = ar.get(256)
        gpos, n_par = {}, 0
        for name, cnt in PARAMS:
            gpos[name] = n_par
            n_par += cnt

        def col(name, i=0, n=1):
            return par.ap[:, gpos[name] + i:gpos[name] + i + n]

        x_in = x

        def load_first(eng):
            pdma(eng, plist, s_par)
            eng.dma_start(xm, A["mem"].rearrange("a (b p) d -> p (a b) d", p=128)).then_inc(s_mem, 16)
            eng.dma_start(cst2.ap, A["consts"][:, CA:CW]).then_inc(s_cst2, 16)

        def load_x(eng):
            eng.dma_start(x_in, A["x"].rearrange("a (b p) d -> p (a b) d", p=128)).then_inc(s_x, 16)
            eng.dma_start(cst.ap, A["consts"][:, 0:CA]).then_inc(s_cst, 16)

        def pdma(eng, lst, sm):
            for d, s in lst:
                eng.dma_start(d, s).then_inc(sm, 16)

        plist, plist2 = [], []
        for name, cnt in PARAMS:
            if not name:
                continue
            r0 = gpos[name]
            if name in ("attn_q_norm", "attn_k_norm", "mem_q_norm", "mem_k_norm"):
                src = A[name]
                for h in range(2):
                    plist.append((rows.ap[r0 % 128:r0 % 128 + 1, 128 * (r0 // 128) + 64 * h:128 * (r0 // 128) + 64 * h + 64], src))
                continue
            flat = A[name]
            if name == "conv_w":
                flat = flat.rearrange("a i (t p) -> (a i t) p", p=128)
            elif name == "rwkv_r_k":
                flat = flat.rearrange("a (t h) d -> (a t) (h d)", h=2)
            else:
                flat = flat.rearrange("a (t p) -> (a t) p", p=128)
            i = 0
            while i < cnt:
                r = r0 + i
                m = min(cnt - i, 128 - r % 128)
                (plist2 if r >= 128 else plist).append((rows.ap[r % 128:r % 128 + m, 128 * (r // 128):128 * (r // 128) + 128], flat[i:i + m, :]))
                i += m
        plist2.append((L2.ap[0:32, :], A["rwkv_w2"][0, :, :]))
        plist2.append((L2.ap[32:64, :], A["rwkv_a2"][0, :, :]))
        plist2.append((L2.ap[64:128, :], A["rwkv_g2"][0, :, :]))
        plist2.append((relb.ap[64:96, 0:6], A["rel_bias"]))
        plist2.append((sink.ap[:, 0:6], bc(A["attn_sinks"], [128, 6])))
        for i, name in enumerate(("lambda_q1_2", "lambda_k1_2", "lambda_q2_2", "lambda_k2_2")):
            plist2.append((lamv.ap[:, 64 * i:64 * i + 64], bc(A[name], [128, 64])))
        par1_tok = (s_par, 16 * len(plist))
        par_tok = [(s_par2, 16 * len(plist2)), (s_cst2, 16)]
        x_tok, mem_tok = (s_x, 16), (s_mem, 16)
        cst_tok = (s_cst, 16)
        ident = C["ident"]
        ones = C["ones"]

        def wcols(ap, c0, n, at=0):
            k = ap.shape[0] // 128

            def dst(s, k=k, n=n, at=at):
                return s[:, at:at + k * n].rearrange("p (k n) -> p k n", k=k)
            return dst, ap[:, c0:c0 + n].rearrange("(k p) n -> p k n", p=128)

        w_in = A["w_in"][0, :, :]
        ring.use([0, 1, 2])
        ch_in = [ring.load(wcols(w_in, 640, 512)), ring.load(wcols(w_in, 1152, 512)),
                 ring.load(wcols(w_in, 1664, 512)), ring.load(wcols(w_in, 0, 512)),
                 ring.load(wcols(w_in, 512, 128))]
        ch_mem = ring.load(wcols(A["w_mem_kv"][0, :, :], 0, 512))
        w_ada = A["w_ada_2"][0, :, :]
        ch_ada = [ring.load(wcols(w_ada, 512 * i, 512)) for i in range(12)]
        w_o = A["w_out"][0, :, :]
        ch_o = [ring.load(wcols(w_o, 512 * i, 512)) for i in range(2)]
        ring.use([3, 0, 1, 2])
        w_up = A["w_up"][0, :, :]
        ch_up = [ring.load(wcols(w_up, 256 * i, 256), wcols(w_up, 2816 + 256 * i, 256, 2048)) for i in range(11)]
        w_dn = A["w_down"][0, :, :]
        ch_dn = [ring.load(wcols(w_dn[512 * i:min(512 * i + 512, 2816), :], 0, 1024)) for i in range(6)]
        w_in2 = A["w_in_2"][0, :, :]
        ch_i2 = [ring.load(wcols(w_in2, 512 * i, 512)) for i in range(10)]
        ch_pm = ring.load(wcols(A["w_proj_moba_2"][0, :, :], 0, 1024))
        ch_pd = ring.load(wcols(A["w_proj_diff_2"][0, :, :], 0, 1024))
        ch_o2 = [ring.load(wcols(A["w_out_2"][0, :, :], 512 * i, 512)) for i in range(2)]

        def load_expert(rg, e):
            return [rg.load(wcols(A["w_gate_2"][0, e, :, :], 0, 512)), rg.load(wcols(A["w_up_2"][0, e, :, :], 0, 512)),
                    rg.load(wcols(A["w_down_2"][0, e, :, :], 0, 1024))]
        ring.use([2, 3, 0, 1, 6, 4, 5])
        ch_e = [load_expert(ring, e) for e in range(NE)]

        n_first = gpos[""]

        def par_cols(i, n, tok):
            b = ps.take()
            t = pe(tr(b.ap[:, 0:n], rows.ap[0:n, 128 * i:128 * i + 128], ident[0:n, 0:n]), tok, cst_tok, b.w)
            t = vcp(par.ap[:, 128 * i:128 * i + n], b.ap[:, 0:n], t)
            b.w = [t]
            return t
        t_par = par_cols(0, n_first, par1_tok)
        junk = ar.get(1024)

        def norm_half(src, h, tok, dst):
            s, r = sml(1), sml(1)
            t = act(junk.ap, src[:, h, :], ACT.Square, tok, SC.last(), junk.w, accum=s)
            t = ts(r, s, 1.0 / 1024, MUL, 1e-6, ADD, t)
            t = ve(lambda e: e.reciprocal(s, r), t)
            t = act(r, s, ACT.Sqrt, t)
            return ts(dst.v("p (b d) -> p b d", b=2)[:, h, :], src[:, h, :], r, MUL, None, None, t, dst.w)

        def features(src, toks, tmp, dst, gcol, shift=None, dtok=None, parts=None, between=None):
            sv = tmp.v("p (b d) -> p b d", b=2)
            dv = dst.v("p (k t) -> p k t", k=8)
            out = []
            tn = [norm_half(src, h, toks[h], tmp) for h in range(2)]
            if between is not None:
                between()
            for h in range(2):
                for k in range(0, 8, 4):
                    b = ps.take()
                    t = pes([tr(b.ap[:, 128 * i:128 * i + 128], sv[:, h, 128 * (k + i):128 * (k + i) + 128], ident) for i in range(4)],
                            tn[h], b.w, cst_tok)
                    pv = b.ap.rearrange("p (k t) -> p k t", k=4)
                    o = dv[:, k:k + 4, 128 * h:128 * h + 128]
                    if shift is None:
                        t2 = [tt(o, pv, bc(gcol[:, k:k + 4].unsqueeze(2), [128, 4, 128]), MUL, t, dst.w, t_par, dtok)]
                    else:
                        t2 = []
                        for i in range(4):
                            if k:
                                t2.append(act(o[:, i, :], pv[:, i, :], ACT.Identity, t, dst.w, dtok, scale=gcol[:, k + i:k + i + 1], bias=shift[:, k + i:k + i + 1]))
                            else:
                                t2.append(ts(o[:, i, :], pv[:, i, :], gcol[:, k + i:k + i + 1], MUL, shift[:, k + i:k + i + 1], ADD, t, dst.w, dtok))
                    b.w = t2
                    if parts is not None:
                        p1, p2, first, w = parts
                        sl = (slice(None), slice(k, k + 4), slice(128 * h, 128 * h + 128))
                        t2 = [split_act(o, [p1[sl], p2[sl]], first[sl], t2, w)]
                    out += t2
            return out

        Xn = ar.get(2048)
        hT = ar.get(2048)
        t_h = features(x, [x_tok, x_tok], Xn, hT, col("mix_norm_g", 0, 8))
        ar.free(now(), Xn)
        Mn = ar.get(2048)
        mT = ar.get(2048)
        t_m = features(xm, [mem_tok, mem_tok], Mn, mT, col("mem_norm_g", 0, 8))
        ar.free(now(), Mn, Xm, X)
        hv = hT.v("p (k t) -> p k t", k=8)
        mv_ = mT.v("p (k t) -> p k t", k=8)

        def proj_fm(b, half, chunk, cols, c0, act_v, k_n=8, base=0):
            w = chunk.ap[:, base:base + k_n * cols].rearrange("p (k n) -> p k n", k=k_n)
            return [mm(b.ap[:, 256 * half:256 * half + 256], w[:, k, c0:c0 + 128], act_v[:, k, :], k == 0, k == k_n - 1)
                    for k in range(k_n)]

        pz = rbuf(10 * 257)
        sh = rbuf(2560)
        shv = sh.v("p (n t) -> p n t", n=10)
        pzv = pz.v("p (n t) -> p n t", n=10)
        t_z = gp(lambda e: e.memset(pzv[:, :, 0:1], 0.0), pz.w)
        evac = []
        for i in range(0, 10, 2):
            b = ps.take()
            for h in range(2):
                n = i + h
                ch = ch_in[n // 4]
                t = pes(proj_fm(b, h, ch, 512, 128 * (n % 4), hv), t_h, ch.tok, b.w)
            t2 = acp(pzv[:, i:i + 2, 1:257], b.ap.rearrange("p (n t) -> p n t", n=2), t, pz.w)
            b.w = [t2]
            if i == 2:
                ch_in[0].free = [t]
            if i == 6:
                ch_in[1].free = [t]
        t_pz = t2
        par_cols(1, 128, par_tok)
        t_par = par_cols(2, n_par - 256, par_tok)
        t = tt(shv, pzv[:, :, 0:256], pzv[:, :, 1:257], SUB, t_pz, t_z, sh.w)
        t = tt(shv, shv, bc(col("rwkv_mu", 0, 10).unsqueeze(2), [128, 10, 256]), MUL, t)
        t_sh = tt(shv, shv, pzv[:, :, 1:257], ADD, t)
        rfree(pz)
        b = ps.take()
        t = pe(mm(b.ap[0:6, 0:384], relb.ap[64:96, 0:6], C["OHB"][64:96, 0:384], True, True), b.w)
        Eb = ar.get(384)
        t_eb = tt(Eb.ap[0:6, :], b.ap[0:6, 0:384], C["MR"][0:6, :], ADD, t, Eb.w)
        b.w = [t_eb]
        bias_v = swb.v("p (h k) -> p h k", h=6)
        toep = bass.AP(scratch, 0, [[1, 128], [384, 6], [1, 256]])
        swr = ar.get(1536)
        swr_v = swr.v("p (h k) -> p h k", h=6)
        bias_tok = (s_bias, 32)

        def bias_dma(e):
            e.dma_start(scratch.ap(), Eb.ap[0:6, :]).then_inc(s_bias, 16)
            e.wait_ge(s_bias, 16)
            e.dma_start(swr_v, toep).then_inc(s_bias, 16)
            return None
        GP.job(bias_dma, t_eb, swr.w)

        qk = ar.get(8 * 256)
        qkv = qk.v("p (n t) -> p n t", n=8)
        plan = [(ch_in[2], 256, hv, t_h), (ch_in[2], 384, hv, t_h), (ch_in[3], 0, hv, t_h), (ch_in[3], 128, hv, t_h),
                (ch_in[3], 256, hv, t_h), (ch_in[3], 384, hv, t_h), (ch_mem, 0, mv_, t_m), (ch_mem, 128, mv_, t_m)]
        lam = sml(6)
        lv_ = lamv.v("p (a k) -> p a k", a=4)
        lt2 = ar.get(128)
        t = tt(lt2.v("p (a k) -> p a k", a=2), lamv.v("p (a z k) -> p a z k", a=2, z=2)[:, :, 0, :],
               lamv.v("p (a z k) -> p a z k", a=2, z=2)[:, :, 1, :], MUL, par_tok, lt2.w)
        t = ve(lambda e: e.tensor_reduce(lam[:, 0:2], lt2.v("p (a k) -> p a k", a=2), AX.X, ADD), t)
        t = act(lam[:, 2:4], lam[:, 0:2], ACT.Exp, t)
        t = tt(lam[:, 4:5], lam[:, 3:4], lam[:, 2:3], SUB, t)
        t_lam = ts(lam[:, 4:5], lam[:, 4:5], -LAM0, ADD, None, None, t)
        ar.free(now(), lt2, lamv)
        va = ar.get(256)
        vm = ar.get(512)
        for i in range(0, 8, 2):
            b = ps.take()
            for h in range(2):
                ch, c0, av, tk = plan[i + h]
                t = pes(proj_fm(b, h, ch, 512, c0, av), tk, ch.tok, b.w)
            t_qk = acp(qkv[:, i:i + 2, :], b.ap.rearrange("p (n t) -> p n t", n=2), t, qk.w)
            b.w = [t_qk]
            if i == 0:
                ch_in[2].free = [t]
            if i == 4:
                ch_in[3].free = [t]
        b = ps.take()
        w = ch_in[4].ap[:, 0:1024].rearrange("p (k n) -> p k n", k=8)
        for h in range(2):
            t = pes([mm(b.ap[:, 128 * h:128 * h + 128], hv[:, k, 128 * h:128 * h + 128], w[:, k, :], k == 0, k == 7)
                     for k in range(8)], ch_in[4].tok, b.w)
        ch_in[4].free = [t]
        t_va = acp(va.ap, b.ap[:, 0:256], t, va.w)
        b.w = [t_va]
        b = ps.take()
        w = ch_mem.ap.rearrange("p (k n) -> p k n", k=8)
        for h in range(2):
            t = pes([mm(b.ap[:, 256 * h:256 * h + 256], mv_[:, k, 128 * h:128 * h + 128], w[:, k, 256:512], k == 0, k == 7)
                     for k in range(8)], b.w)
        ch_mem.free = [t]
        t_vm = acp(vm.ap, b.ap, t, vm.w)
        b.w = [t_vm]
        ar.free(now(), hT, mT, rows, junk)

        def head_rstd(tiles, tok, n, eps, dst, nh, floor=None, sel="hs"):
            b = ps.take()
            fns = [mm(b.ap[0:16, 0:256], C[sel][:, 14 - 2 * i:30 - 2 * i], s, i == 0, i == len(tiles) - 1)
                   for i, s in enumerate(tiles)]
            t = pes(fns, tok, b.w)
            if floor is None:
                t = ts(dst[0:16, 0:256], b.ap[0:16, 0:256], 1.0 / n, MUL, eps, ADD, t)
            else:
                t = ts(dst[0:16, 0:256], b.ap[0:16, 0:256], floor, MAX, None, None, t)
            b.w = [t]
            t = ve(lambda e: e.reciprocal(dst[0:16, 256:512], dst[0:16, 0:256]), t)
            return act(dst[0:16, 0:256], dst[0:16, 256:512], ACT.Sqrt, t)

        def head_bcast(b, half, i, dst):
            return mm(b.ap[:, 256 * half:256 * half + 256], C["OHB"][0:16, 128 * i:128 * i + 128],
                      dst[0:16, 0:256], True, True)

        sq = ar.get(2048)
        rs = ar.get(512)
        t = tt(sq.ap, qk.ap, qk.ap, MUL, t_qk, sq.w)
        sqv = sq.v("p (n t) -> p n t", n=8)
        t_rs = head_rstd([sqv[:, i, :] for i in range(8)], [t, *rs.w], 64.0, 1e-6, rs.ap, 16)
        gains = ["mem_q_norm", "mem_q_norm", "attn_q_norm", "attn_q_norm", "attn_q_norm", "attn_k_norm", "mem_k_norm", "mem_k_norm"]
        for i in range(0, 8, 2):
            b = ps.take()
            t = pes([head_bcast(b, 0, i, rs.ap), head_bcast(b, 1, i + 1, rs.ap)], t_rs, b.w)
            for h in range(2):
                t_qn = stt(qkv[:, i + h, :], qkv[:, i + h, :], col(gains[i + h]), b.ap[:, 256 * h:256 * h + 256], MUL, MUL, t)
            b.w = [t_qn]
        ar.free(now(), sq, rs)
        kb = ar.get(256)
        t_kb = act(kb.ap[0:64, :], qkv[64:128, 5, :], ACT.Copy, t_qn, kb.w)
        t_kb = act(kb.ap[64:128, :], qkv[0:64, 5, :], ACT.Copy, t_qn)

        for i in range(3):
            b = ps.take()
            t = pe(mm(b.ap, C["rev"], swr.ap[:, 512 * i:512 * i + 512], True, True), bias_tok, b.w)
            t_sw = acp(swb.ap[:, 512 * i:512 * i + 512], b.ap, t, swb.w)
            b.w = [t_sw]
        ar.free(now(), swr)
        cat = ar.get(2048)
        catv = cat.v("p (k t) -> p k t", k=8)

        cpad = ar.get(256)
        cpv = cpad.v("p (k m) -> p k m", k=8)
        modc = ar.get(32, True)
        g1b, g2b = ar.get(1024, True), ar.get(1024, True)
        msb = [ar.get(512), ar.get(512)]
        ms_free = [[], []]
        t_cp = ve(lambda e: e.memset(cpad.ap, 0.0), cpad.w)
        t_cp = act(cpv[:, :, 0:1].rearrange("p k o -> p (k o)"), col("c_2", 0, 8), ACT.Silu, t_cp, t_par)
        ada_tok = []

        def ada_step(i):
            b, m = ps.take(), msb[i % 2]
            w = ch_ada[i].ap.rearrange("p (k n) -> p k n", k=8)
            t = pes([mm(b.ap[32 * j:32 * j + 32, :], cpv[:, 2 * j + q, :], w[:, 2 * j + q, :], q == 0, q == 1)
                     for q in range(2) for j in range(4)], ch_ada[i].tok, t_cp, b.w)
            ch_ada[i].free = [t]
            t2 = acp(m.ap, b.ap, t, ms_free[i % 2], m.w)
            b.w = [t2]
            yield
            b = ps.take()
            part = i // 2
            if part in (2, 5):
                t = pe(mm(b.ap, ones, m.ap, True, True), t2, b.w)
                gb = (g1b if part == 2 else g2b).ap[:, 512 * (i % 2):512 * (i % 2) + 512]
                t3 = tt(gb, b.ap, gb, ADD, t, (s_gb, 32))
            else:
                t = pes([mm(b.ap[:, q:q + 1], m.ap[:, 128 * q:128 * q + 128], ones[:, 0:1], True, True) for q in range(4)], t2, b.w)
                o = {0: 0, 1: 8, 3: 16, 4: 24}[part] + 4 * (i % 2)
                t3 = tt(modc.ap[:, o:o + 4], b.ap[:, 0:4], col("b_ada_2", 4 * i, 4), ADD, t, modc.w)
            b.w = [t3]
            ms_free[i % 2] = [t]
            ada_tok.append(t3)

        def ada_chain():
            for i in range(12):
                yield from ada_step(i)
                yield
        later(g1b.w, [(g1b.ap, bc(A["b_ada_2"][:, 2048:3072], [128, 1024]))], s_gb)
        later(g2b.w, [(g2b.ap, bc(A["b_ada_2"][:, 5120:6144], [128, 1024]))], s_gb)

        NB_A = 2
        S_ = [ar.get(512) for _ in range(NB_A)]
        P_ = [ar.get(512) for _ in range(NB_A)]
        PT_ = [ar.get(512) for _ in range(NB_A)]
        st_ = [sml(12) for _ in range(NB_A)]
        a_free = [[[], []] for _ in range(NB_A)]

        def attn_scores(i, q2, k2, blk, nk, masks, tok, sink_c=None, combine=None):
            S, P, PT, st = S_[i], P_[i], PT_[i], st_[i]
            bb = [ps.take(), ps.take()]
            w = nk * 128
            t = pes([mm(bb[h].ap[:, 0:w], q2[h][:, 128 * blk:128 * blk + 128], k2[h][:, 0:w], True, True)
                     for h in range(2)], tok, bb[0].w, bb[1].w)
            sv = S.ap[:, 0:2 * w].rearrange("p (h k) -> p h k", h=2)
            prev = a_free[i][0]
            for h in range(2):
                t1 = masks(h, sv[:, h, :], bb[h].ap[:, 0:w], [t, *prev, *S.w])
                bb[h].w = [t1]
            mx, nm, ssum, rc = st[:, 0:2], st[:, 2:4], st[:, 4:6], st[:, 6:8]
            t2 = ve(lambda e: e.tensor_reduce(mx, sv, AX.X, MAX), t1, prev)
            if sink_c is not None:
                t2 = tt(mx, mx, sink_c, MAX, t2)
            t3 = ts(nm, mx, -1.0, MUL, None, None, t2)
            pv = P.ap[:, 0:2 * w].rearrange("p (h k) -> p h k", h=2)
            for h in range(2):
                t4 = act(pv[:, h, :], sv[:, h, :], ACT.Exp, t3, prev, P.w, bias=nm[:, h:h + 1], accum=ssum[:, h:h + 1])
            if sink_c is not None:
                t5 = tt(st[:, 8:10], sink_c, nm, ADD, t3)
                t5 = act(st[:, 10:12], st[:, 8:10], ACT.Exp, t5)
                t4 = tt(ssum, ssum, st[:, 10:12], ADD, t4, t5)
            t5 = ve(lambda e: e.reciprocal(rc, ssum), t4)
            return i, pv, rc, t5, w

        def attn_out(i, pv, rc, t5, w, nk, v2, dst, vtok, dtok, done):
            P, PT = P_[i], PT_[i]
            t6 = tt(pv, pv, bc(rc.unsqueeze(2), [128, 2, w]), MUL, t5)
            b = ps.take()
            t7 = pes([tr(b.ap[:, 128 * (nk * h + j):128 * (nk * h + j) + 128], pv[:, h, 128 * j:128 * j + 128], ident)
                      for h in range(2) for j in range(nk)], t6, b.w)
            t8 = acp(PT.ap[:, 0:2 * w], b.ap[:, 0:2 * w], t7, a_free[i][1], PT.w)
            b.w = [t8]
            yield
            b = ps.take()
            t9 = pes([mm(b.ap[64 * h:64 * h + 64, 0:128], v2[h](j), PT.ap[:, 128 * (nk * h + j):128 * (nk * h + j) + 128], j == 0, j == nk - 1)
                      for h in range(2) for j in range(nk)], t8, vtok, b.w)
            if isinstance(dst, list):
                t10 = split_act(b.ap[:, 0:128], dst[0:2], dst[2], t9, dtok)
            else:
                t10 = acp(dst, b.ap[:, 0:128], t9, dtok)
            b.w = [t10]
            a_free[i] = [[t7, t6], [t9]]
            done.append(t10)

        def plain(h, sv, bv, w):
            return ts(sv, bv, 0.125, MUL, None, None, *w)

        def causal(nk):
            def f(h, sv, bv, w):
                if nk == 2:
                    ts(sv[:, 0:128], bv[:, 0:128], 0.125, MUL, None, None, *w)
                l = 128 * (nk - 1)
                return stt(sv[:, l:l + 128], bv[:, l:l + 128], 0.125, C["caus"], MUL, ADD, *w)
            return f

        def windowed(pair, nk):
            def f(h, sv, bv, w):
                return stt(sv, bv, 0.125, bias_v[:, 2 * pair + h, 256 - 128 * nk:256], MUL, ADD, t_sw, *w)
            return f

        def hrow(ap, h):
            return ap[64 * (h % 2):64 * (h % 2) + 64, :]

        vmv = vm.v("p (b d) -> p b d", b=2)
        vav = va.v("p (b d) -> p b d", b=2)
        cat_done = []

        def mem_unit(i, pr, blk):
            r = attn_scores(i, [hrow(qkv[:, pr, :], h) for h in range(2)], [hrow(qkv[:, 6 + pr, :], h) for h in range(2)],
                            blk, 2, plain, t_qn)
            yield
            yield from attn_out(*r, 2, [(lambda j, h=2 * pr + h: vmv[:, j, 64 * h:64 * h + 64]) for h in range(2)],
                                catv[:, 6 + pr, 128 * blk:128 * blk + 128], t_vm, cat.w, cat_done)

        def win_unit(i, pr, blk):
            nk = 1 + blk
            ks = []
            for h in range(2):
                kvh = (2 * pr + h) // 3
                ks.append(hrow(qkv[:, 5, :] if kvh == h else kb.ap, h))
            r = attn_scores(i, [hrow(qkv[:, 2 + pr, :], h) for h in range(2)], ks, blk, nk, windowed(pr, nk), [t_qn, t_kb],
                            sink_c=sink.ap[:, 2 * pr:2 * pr + 2])
            yield
            yield from attn_out(*r, nk, [(lambda j, n=(2 * pr + h) // 3: vav[:, j, 64 * n:64 * n + 64]) for h in range(2)],
                                catv[:, pr, 128 * blk:128 * blk + 128], t_va, cat.w, cat_done)

        def unit_chain(i, units):
            for f, pr, blk in units:
                yield from f(i, pr, blk)
                yield
        units = [(mem_unit, pr, blk) for pr in range(2) for blk in range(2)] + [(win_unit, pr, blk) for pr in range(3) for blk in range(2)]

        def v3(b):
            return b.v("p (n t) -> p n t", n=3)

        def c3(name):
            return bc(col(name, 0, 3).unsqueeze(2), [128, 3, 256])
        rT, kT_, vT = shv[:, 0:3, :], shv[:, 3:6, :], shv[:, 6:9, :]
        cat2_done = []

        def rwkv_chain():
            lt = rbuf(256)
            t1 = act(lt.ap[0:32, :], shv[0:32, 9, :], ACT.Tanh, t_sh, lt.w)
            t1 = act(lt.ap[32:64, :], shv[32:64, 9, :], ACT.Copy, t_sh, lt.w)
            t_lt = act(lt.ap[64:128, :], shv[64:128, 9, :], ACT.Sigmoid, t_sh, lt.w)
            sg, av, gg = rbuf(768), rbuf(768), rbuf(768)
            for p0, k_, dstb, f, bn in ((0, 32, sg, ACT.Sigmoid, "rwkv_w0"), (32, 32, av, ACT.Sigmoid, "rwkv_a0"), (64, 64, gg, ACT.Copy, None)):
                for i in range(3):
                    b = ps.take()
                    t = pe(mm(b.ap[:, 0:256], L2.ap[p0:p0 + k_, 128 * i:128 * i + 128], lt.ap[p0:p0 + k_, :], True, True), t_lt, par_tok, b.w)
                    if bn:
                        t_w = act(v3(dstb)[:, i, :], b.ap[:, 0:256], f, t, dstb.w, bias=col(bn, i))
                    else:
                        t_w = acp(v3(dstb)[:, i, :], b.ap[:, 0:256], t, dstb.w)
                    b.w = [t_w]
            yield
            kk, tmp, rs = rbuf(768), rbuf(768), rbuf(512)
            t = tt(v3(kk), kT_, c3("rwkv_k_k"), MUL, t_sh, t_par, kk.w)
            t = tt(v3(tmp), v3(kk), v3(kk), MUL, t, tmp.w)
            t_rs = head_rstd([v3(tmp)[:, i, :] for i in range(3)], [t, *rs.w], 1.0, 0.0, rs.ap, 16, floor=1e-24)
            for i in range(3):
                b = ps.take()
                t = pe(head_bcast(b, 0, i, rs.ap), t_rs, b.w)
                t_kk = tt(v3(kk)[:, i, :], v3(kk)[:, i, :], b.ap[:, 0:256], MUL, t)
                b.w = [t_kk]
            yield
            t = ts(v3(tmp), v3(av), -1.0, ADD, None, None, t_w, VE.last(), PE.last())
            t = tt(v3(tmp), v3(tmp), c3("rwkv_k_a"), MUL, t)
            kp = rbuf(768)
            t_kp = stt(kp.ap, tmp.ap, 1.0, sh.ap[:, 768:1536], ADD, MUL, t, kp.w)
            t_b = tt(av.ap, kk.ap, av.ap, MUL, t_kk, t_kp)
            yield
            Lz = rbuf(6 * 129)
            Lv = Lz.v("p (n c t) -> p n c t", n=3, c=2)
            t_l0 = gp(lambda e: e.memset(Lv[:, :, :, 0:1], 0.0), Lz.w)
            t = ts(sg.ap, sg.ap, -math.exp(-0.5), MUL, None, None, t_w)
            for i in range(3):
                for c in range(2):
                    t_L = ve(lambda e, i=i, c=c: e.tensor_tensor_scan(out=Lv[:, i, c, 1:129], data0=ones, data1=v3(sg)[:, i, 128 * c:128 * c + 128],
                                                                     initial=0.0, op0=MUL, op1=ADD), t, Lz.w)
            yield
            Lm = sml(12)
            t_lm = vcp(Lm[:, 0:6], Lv[:, :, :, 64:65].rearrange("p n c o -> p (n c o)"), t_L)
            t_nl = ts(Lm[:, 6:12], Lm[:, 0:6], -1.0, MUL, None, None, t_lm)
            E1, E2 = rbuf(6 * 129), rbuf(768)
            E1v, E2v = E1.v("p (n c t) -> p n c t", n=3, c=2), E2.v("p (n c t) -> p n c t", n=3, c=2)
            for i in range(3):
                for c in range(2):
                    q = 2 * i + c
                    act(E1v[:, i, c, :], Lv[:, i, c, :], ACT.Exp, t_L, t_nl, t_l0, E1.w, bias=Lm[:, 6 + q:7 + q])
                    t_E = act(E2v[:, i, c, :], Lv[:, i, c, 1:129], ACT.Exp, E2.w, bias=Lm[:, q:q + 1], scale=-1.0)
            yield
            eM = sml(6)
            t_eM = act(eM, Lm[:, 0:6], ACT.Exp, t_lm)
            AR = rbuf(1536)
            ARv = AR.v("p (n c z t) -> p n c z t", n=3, c=2, z=2)

            def v4(ap):
                return ap.rearrange("p (n c t) -> p n c t", n=3, c=2)
            BK = [rbuf(768), rbuf(768)]
            for i in range(3):
                stt(ARv[:, i, :, 0, :], v4(kk.ap)[:, i, :, :], -1.0, E1v[:, i, :, 0:128], MUL, MUL, t_E, t_kk, AR.w)
                t_AR = tt(ARv[:, i, :, 1, :], v4(sh.ap[:, 0:768])[:, i, :, :], E1v[:, i, :, 1:129], MUL, AR.w)
            t_B = tt(BK[0].ap, av.ap, E2.ap, MUL, t_b, BK[0].w)
            t_K = tt(BK[1].ap, kp.ap, E2.ap, MUL, BK[1].w)
            yield
            bs = tmp
            t = tt(bs.ap, sh.ap[:, 0:768], kp.ap, MUL, t_kp, VE.last())
            t = tt(v3(bs), v3(bs), c3("rwkv_r_k"), MUL, t)
            for i in range(3):
                b = ps.take()
                t2 = pe(mm(b.ap[:, 0:256], C["bo"], v3(bs)[:, i, :], True, True), t, b.w)
                t_bon = tt(v3(bs)[:, i, :], b.ap[:, 0:256], vT[:, i, :], MUL, t2)
                b.w = [t_bon]
            yield
            VT, BT, KT_ = rbuf(768), rbuf(384), rbuf(384)
            VTv = VT.v("p (c n k) -> p c n k", c=2, n=3)
            for c in range(2):
                b = ps.take()
                t = pes([tr(b.ap[:, 128 * i:128 * i + 128], vT[:, i, 128 * c:128 * c + 128], ident) for i in range(3)], t_sh, b.w)
                t_VT = acp(VT.ap[:, 384 * c:384 * c + 384], b.ap[:, 0:384], t, VT.w)
                b.w = [t_VT]
            for src, dst, tk in ((BK[0], BT, t_B), (BK[1], KT_, t_K)):
                b = ps.take()
                t = pes([tr(b.ap[:, 128 * i:128 * i + 128], v4(src.ap)[:, i, 0, :], ident) for i in range(3)], tk, b.w)
                t_BT = acp(dst.ap, b.ap[:, 0:384], t, dst.w)
                b.w = [t_BT]
            rfree(kk, E2, Lz, sg, kp, av, lt)

            yield
            yT = rbuf(768)
            rhs_b, sa_b = rbuf(384), rbuf(384)
            st_b = rbuf(192)
            MB, MK, XZ, T1 = rbuf(1536), rbuf(1536), rbuf(1536), rbuf(768)
            t_z1 = gp(lambda e: e.memset(MB.ap, 0.0), MB.w)
            t_z2 = gp(lambda e: e.memset(MK.ap, 0.0), MK.w)
            i32 = lambda a: a.bitcast(I32)
            su_iu = cst.ap[:, CL["SU"][0]:CL["SU"][0] + 256]
            done_prev = []
            XZv = XZ.v("p (h z t) -> p h z t", h=6, z=2)
            T1v = T1.v("p (h t) -> p h t", h=6)

            def at(h):
                return 3 * (h % 2) + h // 2

            def Mab(k):
                h = 2 * (k % 3) + k // 3
                return MB.ap[:, 256 * h:256 * h + 128]
            for c in range(2):
                t_unit = [[] for _ in range(6)]
                for h in range(6):
                    i, o = h // 2, 64 * (h % 2)
                    b = ps.take()
                    ARh = ARv[o:o + 64, i, c, :, :].rearrange("p z t -> p (z t)")
                    Bh, Kh = v4(BK[0].ap)[o:o + 64, i, c, :], v4(BK[1].ap)[o:o + 64, i, c, :]
                    t = pes([mm(b.ap[:, 0:256], Bh, ARh, True, True), mm(b.ap[:, 256:512], Kh, ARh, True, True)], t_AR, t_B, t_K, b.w)
                    ve(lambda e, h=h, b=b: e.copy_predicated(MB.ap[:, 256 * h:256 * h + 256], i32(su_iu), b.ap[:, 0:256]), t, t_z1, done_prev)
                    t2 = ve(lambda e, h=h, b=b: e.copy_predicated(MK.ap[:, 256 * h:256 * h + 256], i32(su_iu), b.ap[:, 256:512]), t_z2)
                    b.w = [t2]
                    t_unit[at(h)].append(t2)
                    yield
                for z in range(2):
                    b = ps.take()
                    t = pes([mm(b.ap[:, 128 * i:128 * i + 128], ARv[64 * z:64 * z + 64, i, c, 0, :], v4(BK[0].ap)[64 * z:64 * z + 64, i, c, :], True, True)
                             for i in range(3)], b.w)
                    X3, Z3 = XZv[:, 3 * z:3 * z + 3, 0, :], XZv[:, 3 * z:3 * z + 3, 1, :]
                    t3 = tt(X3, b.ap[:, 0:384].rearrange("p (n t) -> p n t", n=3), bc(C["LM"][:, 0:128].unsqueeze(1), [128, 3, 128]), MUL, t, XZ.w, done_prev)
                    b.w = [t3]
                    M3 = MB.ap.rearrange("p (i o x) -> p i o x", i=3, o=2)[:, :, z, 0:128]
                    t5 = tt(Z3, M3, bc(C["LM1T"].unsqueeze(1), [128, 3, 128]), MUL, t_unit[3 * z:3 * z + 3], XZ.w)
                    for i in range(3):
                        t5 = tt(XZv[:, 3 * z + i, :, :], XZv[:, 3 * z + i, :, :], bc(ident.unsqueeze(1), [128, 2, 128]), ADD, t3, t5)
                        t_unit[3 * z + i] = [t5]
                    yield
                for lv in range(1, 7):
                    lm = bc(C["LM"][:, 128 * lv:128 * lv + 128].unsqueeze(1), [128, 2, 128])
                    t_T = []
                    for q in range(3):
                        b = ps.take()
                        t = pes([mm(b.ap[:, 128 * y:128 * y + 128], Mab(2 * q + y), XZv[:, 2 * q + y, 0, :], True, True) for y in range(2)],
                                t_unit[2 * q], t_unit[2 * q + 1], b.w)
                        t = tt(T1v[:, 2 * q:2 * q + 2, :], b.ap[:, 0:256].rearrange("p (y t) -> p y t", y=2), lm, MUL, t, T1.w)
                        b.w = [t]
                        t_T.append(t)
                    yield
                    for q in range(3):
                        b = ps.take()
                        fns = []
                        for y in range(2):
                            Th, Zh = T1v[:, 2 * q + y, :], XZv[:, 2 * q + y, 1, :]
                            if lv < 6:
                                fns.append(mm(b.ap[:, 256 * y:256 * y + 128], Zh, Th, True, True))
                            fns.append(mm(b.ap[:, 256 * y + 128:256 * y + 256], Th, Zh, True, True))
                        t = pes(fns, t_T[q], b.w)
                        b4 = b.ap.rearrange("p (y z t) -> p y z t", y=2, z=2)
                        if lv < 6:
                            t2 = tt(XZ.ap[:, 512 * q:512 * q + 512], XZ.ap[:, 512 * q:512 * q + 512], b.ap, ADD, t)
                        else:
                            t2 = tt(XZv[:, 2 * q:2 * q + 2, 1, :], XZv[:, 2 * q:2 * q + 2, 1, :], b4[:, :, 1, :], ADD, t)
                        b.w = [t2]
                        t_unit[2 * q] = t_unit[2 * q + 1] = [t2]
                    yield
                yield
                rbs = [ps.take(), ps.take()]
                fns = []
                for h in range(6):
                    i, o = h // 2, 64 * (h % 2)
                    oc = rbs[h % 2].ap[:, 64 * i:64 * i + 64]
                    if c == 1:
                        fns.append(mm(oc, ARv[o:o + 64, i, c, 0, :], st_b.ap[o:o + 64, 64 * i:64 * i + 64], True, False))
                    fns.append(mm(oc, MK.ap[:, 256 * h:256 * h + 128], VTv[:, c, i, o:o + 64], c == 0, True))
                t0 = pes(fns, [x for u in t_unit for x in u], rbs[0].w, rbs[1].w, t_VT, done_prev)
                for o in range(2):
                    t = acp(rhs_b.ap.rearrange("p (n o k) -> p n o k", n=3, o=2)[:, :, o, :],
                            rbs[o].ap[:, 0:192].rearrange("p (n k) -> p n k", n=3), t0, rhs_b.w, done_prev)
                    rbs[o].w = [t]
                yield
                rb = ps.take()
                t = pes([mm(rb.ap[:, 64 * h:64 * h + 64], XZv[:, at(h), 1, :], rhs_b.ap[:, 64 * h:64 * h + 64], True, True) for h in range(6)], t, rb.w)
                t_sa = acp(sa_b.ap, rb.ap[:, 0:384], t, sa_b.w, done_prev)
                rb.w = [t_sa]
                yield
                yb = ps.take()
                fns = []
                for h in range(6):
                    i, o = h // 2, 64 * (h % 2)
                    oc = yb.ap[o:o + 64, 128 * i:128 * i + 128]
                    if c == 1:
                        fns.append(mm(oc, st_b.ap[o:o + 64, 64 * i:64 * i + 64], ARv[o:o + 64, i, c, 1, :], True, False))
                    fns.append(mm(oc, sa_b.ap[:, 64 * h:64 * h + 64], MB.ap[:, 256 * h + 128:256 * h + 256], c == 0, False))
                    fns.append(mm(oc, VTv[:, c, i, o:o + 64], MK.ap[:, 256 * h + 128:256 * h + 256], False, True))
                t_y = pes(fns, t_sa, yb.w)
                t_yT = vcp(v4(yT.ap)[:, :, c, :], yb.ap[:, 0:384].rearrange("p (n t) -> p n t", n=3), t_y, yT.w)
                yb.w = [t_yT]
                yield
                if c == 0:
                    sbk = ps.take()
                    fns = []
                    for h in range(6):
                        i, o = h // 2, 64 * (h % 2)
                        oc = sbk.ap[o:o + 64, 64 * i:64 * i + 64]
                        fns.append(mm(oc, BT.ap[:, 128 * i + o:128 * i + o + 64], sa_b.ap[:, 64 * h:64 * h + 64], True, False))
                        fns.append(mm(oc, KT_.ap[:, 128 * i + o:128 * i + o + 64], VTv[:, 0, i, o:o + 64], False, True))
                    t = pes(fns, t_sa, t_BT, sbk.w)
                    for i in range(3):
                        t = ts(st_b.ap[:, 64 * i:64 * i + 64], sbk.ap[:, 64 * i:64 * i + 64], E1v[:, i, 0, 128:129], MUL,
                               eM[:, 2 * i + 1:2 * i + 2], MUL, t, t_eM, st_b.w)
                    sbk.w = [t]
                    t_st = t
                    done_prev = [t_st, t_y, t_yT]
            yield
            rfree(MB, MK, XZ, T1, rhs_b, sa_b, st_b, E1, AR, *BK, BT, KT_, VT)
            ysq = rbuf(768)
            for i in range(3):
                b = ps.take()
                t = pe(mm(b.ap[:, 0:256], C["bo"], v3(yT)[:, i, :], True, True), t_yT, b.w)
                t_c = stt(v3(yT)[:, i, :], b.ap[:, 0:256], -1.0 / 64, v3(yT)[:, i, :], MUL, ADD, t)
                b.w = [t_c]
            yield
            t = tt(ysq.ap, yT.ap, yT.ap, MUL, t_c, ysq.w)
            t_rs = head_rstd([v3(ysq)[:, i, :] for i in range(3)], [t, VE.last(), PE.last()], 64.0, 64e-5, rs.ap, 16)
            for i in range(3):
                b = ps.take()
                t = pe(head_bcast(b, 0, i, rs.ap), t_rs, b.w)
                t = tt(v3(yT)[:, i, :], v3(yT)[:, i, :], b.ap[:, 0:256], MUL, t)
                b.w = [t]
                t = ts(v3(yT)[:, i, :], v3(yT)[:, i, :], col("rwkv_ln_w", i), MUL, col("rwkv_ln_b", i), ADD, t)
            t = tt(yT.ap, yT.ap, bs.ap, ADD, t)
            t_cat2 = tt(cat.ap[:, 768:1536], yT.ap, gg.ap, MUL, t, cat.w)
            rfree(ysq, yT, rs, tmp, gg, sh)
            ring.lent[3] = now()
            cat2_done.append(t_cat2)

        interleave(ps, (rwkv_chain(), [4, 5, 6]), [(unit_chain(0, units[0::2]), [0, 1], 0.35), (unit_chain(1, units[1::2]), [2, 3], 0.35),
                                                   (ada_chain(), [7], 0.35)])
        t_cat, t_cat2 = cat_done, cat2_done
        ar.free(now(), *S_, *P_, *PT_, qk, kb, va, vm, Eb, swb, *msb, cpad, L2, cst2)

        X = ar.get(2048, True)
        x = X.v("p (b d) -> p b d", b=2)
        later(X.w, [(x, A["x"].rearrange("a (b p) d -> p (a b) d", p=128))], s_x2)
        x2_tok = (s_x2, 16)

        def token_out(chunks, act_v, use, tok, k_n=8):
            tu = [None, None]
            for c, ch in enumerate(chunks):
                w = ch.ap.rearrange("p (k n) -> p k n", k=8)
                for h in range(2):
                    b = ps.take()
                    t = pes([mm(b.ap, act_v[:, k, 128 * h:128 * h + 128], w[:, k, :], k == 0, k == k_n - 1)
                             for k in range(k_n)], tok, ch.tok, b.w)
                    t2 = use(c, h, b.ap, t)
                    b.w = [t2]
                    tu[h] = t2
                ch.free = [t]
            return tu

        def add_x(c, h, bank, t):
            v = x[:, h, 512 * c:512 * c + 512]
            return tt(v, bank, v, ADD, t, x2_tok)

        t_xh = token_out(ch_o, catv, add_x, [t_cat, t_cat2])
        ar.free(now(), cat)

        class Half:
            pass

        halves, ready, taken = [], [], [0]
        sp_r = [[ring_r[:, 1 + i, 2048 * z:2048 * z + 2048] for z in range(2)] for i in range(2)]
        sp_f = [[v.bitcast(F) for v in vs] for vs in sp_r]
        sp_free = [ring.lent[3], ring.lent[3]]
        for c in range(11):
            for z in range(2):
                halves.append((ch_up[c], ch_up[c].ap[:, 2048 * z:2048 * z + 2048].rearrange("p (k n) -> p k n", k=8), z))
        for c in range(6):
            for z in range(2):
                k = 4 if c < 5 else 2
                halves.append((ch_dn[c], ch_dn[c].ap[:, 0:1024 * k].rearrange("p (k n) -> p k n", k=k)[:, :, 512 * z:512 * z + 512], z))
        for ch, k in [(ch, 8) for ch in ch_i2] + [(ch_pm, 4), (ch_pd, 4)] + [(ch, 8) for ch in ch_o2]:
            for z in range(2):
                n = 4096 // k
                halves.append((ch, ch.ap.rearrange("p (k n) -> p k n", k=k)[:, :, n // 2 * z:n // 2 * z + n // 2], z))

        def split_next():
            if taken[0] == len(halves):
                return
            i = taken[0] % 2
            ch, src, z = halves[taken[0]]
            taken[0] += 1
            k, n = src.shape[1], src.shape[2]
            h = Half()
            h.i = i
            h.w = [v[:, 0:k * n].rearrange("p (k n) -> p k n", k=k) for v in sp_r[i]]
            first = sp_f[i][0][:, 0:k * n].rearrange("p (k n) -> p k n", k=k)
            ts_ = [acp(h.w[0][:, ks, :], src[:, ks, :], ch.tok, sp_free[i]) for ks in (slice(0, k // 2), slice(k // 2, k))]
            for ks, t in zip((slice(0, k // 2), slice(k // 2, k)), ts_):
                h.tok = tt(h.w[1][:, ks, :], src[:, ks, :], first[:, ks, :], SUB, t)
            if z == 1:
                ch.free = [h.tok]
            ready.append(h)

        split_next()
        split_next()

        def take_half():
            return ready.pop(0)

        def done_half(h, tok):
            sp_free[h.i] = [tok]
            split_next()

        def mm3(o, l, r, start, stop):
            f = [mm(o, l[0], r[0], start, False), mm(o, l[0], r[1], False, False), mm(o, l[1], r[0], False, stop)]

            def run(e):
                f[0](e)
                f[1](e)
                return f[2](e)
            return run

        def pair(n):
            b = [ar.get(n), ar.get(n)]
            return b, [as_r(v) for v in b], as_r(b[0]).bitcast(F)

        def split_act(src, parts, first, *w):
            t = acp(parts[0], src, *w)
            return tt(parts[1], src, first, SUB, t)

        def proj3(o, w, c0, act_p, k_n):
            return [mm3(o, [v[:, k, c0:c0 + 128] for v in w], [a[:, k, :] for a in act_p], k == 0, k == k_n - 1) for k in range(k_n)]

        def tokens3(outs, hw, act_p, h0=0):
            return [mm3(o, [a[:, k, 128 * h:128 * h + 128] for a in act_p], [v[:, k, :] for v in hw.w], k == 0, k == 7)
                    for h, o in enumerate(outs, h0) for k in range(8)]

        def features_pair(src, toks, gcol, tmp=None, **kw):
            tmp, hT = tmp or ar.get(2048), ar.get(2048)
            bufs, r, f0 = pair(2048)
            r = [v.rearrange("p (k t) -> p k t", k=8) for v in r]
            t = features(src, toks, tmp, hT, gcol, parts=(*r, f0.rearrange("p (k t) -> p k t", k=8), [*bufs[0].w, *bufs[1].w]), **kw)
            ar.free(now(), tmp, hT)
            return bufs, r, t

        junk = ar.get(1024)
        hbufs, hp, t_h = features_pair(x, t_xh, col("ffn_norm_g", 0, 8))
        ar.free(now(), junk)
        abufs, ap_, af = pair(22 * 256)
        ap_ = [v.rearrange("p (k t) -> p k t", k=22) for v in ap_]
        afv = af.rearrange("p (k t) -> p k t", k=22)
        Uz = [ar.get(4 * 258) for _ in range(2)]
        Ub = [ar.get(1024) for _ in range(2)]
        u_free = [[], []]
        tz = []
        for u in Uz:
            tz.append(gp(lambda e, u=u: e.memset(u.v("p (n t) -> p n t", n=4)[:, :, 0:2], 0.0), u.w))
        t_as = []
        for i in range(11):
            U, Uc = Uz[i % 2].v("p (n t) -> p n t", n=4), Ub[i % 2].v("p (n t) -> p n t", n=4)
            te = []
            for z in range(2):
                b = ps.take()
                hw = take_half()
                for h in range(2):
                    t = pes(proj3(b.ap[:, 256 * h:256 * h + 256], hw.w, 128 * h, hp, 8), t_h, hw.tok, b.w)
                done_half(hw, t)
                t2 = acp(U[:, 2 * z:2 * z + 2, 2:258], b.ap.rearrange("p (n t) -> p n t", n=2), t, u_free[i % 2], Uz[i % 2].w, tz)
                b.w = [t2]
                te.append(t2)
            tiles = [2 * i, 2 * i + 1, 22 + 2 * i, 23 + 2 * i]
            for n, g_ in enumerate(tiles):
                t2 = act(Uc[:, n, :], U[:, n, 2:258], ACT.Identity, te[n // 2], u_free[i % 2], Ub[i % 2].w,
                         scale=col("conv_w", 88 + g_), bias=col("conv_b", g_))
                t2 = stt(Uc[:, n, :], U[:, n, 1:257], col("conv_w", 44 + g_), Uc[:, n, :], MUL, ADD, t2)
                t2 = stt(Uc[:, n, :], U[:, n, 0:256], col("conv_w", g_), Uc[:, n, :], MUL, ADD, t2)
                if n == 1:
                    tg = t2
            t3 = act(Uc[:, 0:2, :], Uc[:, 0:2, :], ACT.Silu, tg)
            t3 = tt(Uc[:, 0:2, :], Uc[:, 0:2, :], Uc[:, 2:4, :], MUL, t3, t2)
            ks = slice(2 * i, 2 * i + 2)
            t_a = split_act(Uc[:, 0:2, :], [v[:, ks, :] for v in ap_], afv[:, ks, :], t3, abufs[0].w, abufs[1].w)
            u_free[i % 2] = [t_a]
            t_as.append(t_a)
        ar.free(now(), *Uz, *Ub)
        junk, tmp2 = ar.get(1024), ar.get(2048)
        bb = [ps.take() for _ in range(4)]
        for c in range(6):
            hws = [ready[0], ready[1]]

            def down_fns(h, q):
                return [mm3(bb[2 * h + q].ap, [v[:, 4 * c + k, 128 * h:128 * h + 128] for v in ap_], [v[:, k, :] for v in hws[q].w],
                            4 * c + k == 0, 4 * c + k == 21) for k in range(4 if c < 5 else 2)]
            if c < 5:
                for q in range(2):
                    hw = take_half()
                    t = pes(down_fns(0, q) + down_fns(1, q), t_as[2 * c + 1], hw.tok, [b.w for b in bb])
                    done_half(hw, t)
            else:
                take_half()
                take_half()
                t_xh = [None, None]
                for h in range(2):
                    for q in range(2):
                        t = pes(down_fns(h, q), t_as[10], hws[q].tok)
                        bb[2 * h + q].w = [t_xh[h]] = [add_x(q, h, bb[2 * h + q].ap, t)]
        last_halves, t_last = hws, t
        ar.free(now(), *abufs, *hbufs)
        mods = ar.get(32, True)
        t_md = stt(mods.ap[:, 0:8], modc.ap[:, 8:16], 1.0, col("norm1_g_2", 0, 8), ADD, MUL, ada_tok, mods.w)
        t_md = stt(mods.ap[:, 8:16], modc.ap[:, 24:32], 1.0, col("norm2_g_2", 0, 8), ADD, MUL)
        hbufs, hp, t_h = features_pair(x, t_xh, mods.ap[:, 0:8], tmp=tmp2, between=lambda: [done_half(q, t_last) for q in last_halves], shift=modc.ap[:, 0:8], dtok=t_md)
        ar.free(now(), junk)
        Q = [ar.get(1024) for _ in range(6)]
        rt = ar.get(512)
        rt_free = []
        t_q = [None] * 6
        cosb = bc(C["cos"].unsqueeze(1), [128, 2, 256])
        sinb = bc(C["sin"].unsqueeze(1), [128, 2, 256])
        GM = ar.get(4096)
        GMv = GM.v("p (k t) -> p k t", k=16)
        rtv = rt.v("p (n t) -> p n t", n=2)
        late = []

        def rope(c, z, qv, t1):
            b = ps.take()
            t2 = pe(mm(b.ap, C["perm"], Q[c].ap[:, 512 * z:512 * z + 512], True, True), t1, b.w)
            t3 = tt(rtv, b.ap.rearrange("p (n t) -> p n t", n=2), sinb, MUL, t2, rt.w, VE.last())
            b.w = [t3]
            t4 = tt(qv, qv, cosb, MUL, t3)
            t_q[c] = tt(qv, qv, rtv, ADD, t4)

        def proj_chain(chunks):
            for c in chunks:
                if c in (2, 5):
                    for z in range(2):
                        b = ps.take()
                        hw = take_half()
                        t = pes(tokens3([b.ap[:, 0:256], b.ap[:, 256:512]], hw, hp), t_h, hw.tok, b.w)
                        tv = acp(Q[c].v("p (h n) -> p h n", h=2)[:, :, 256 * z:256 * z + 256], b.ap.rearrange("p (h n) -> p h n", h=2), t, Q[c].w)
                        b.w = [tv]
                        done_half(hw, t)
                        while late:
                            rope(*late.pop())
                        if z == 1:
                            t_q[c] = tv
                        yield
                    continue
                for z in range(2):
                    b = ps.take()
                    hw = take_half()
                    for h in range(2):
                        t = pes(proj3(b.ap[:, 256 * h:256 * h + 256], hw.w, 128 * h, hp, 8), t_h, hw.tok, b.w)
                        if h == 0 and c > 2:
                            yield
                    bv = b.ap.rearrange("p (n t) -> p n t", n=2)
                    if c < 6:
                        qv = Q[c].v("p (n t) -> p n t", n=4)[:, 2 * z:2 * z + 2, :]
                        t1 = acp(qv, bv, t, Q[c].w)
                    else:
                        t1 = acp(GMv[:, 4 * (c - 6) + 2 * z:4 * (c - 6) + 2 * z + 2, :], bv, t, GM.w)
                    b.w = [t1]
                    done_half(hw, t)
                    while late:
                        rope(*late.pop())
                    if c < 6:
                        late.append((c, z, qv, t1))
                    yield
        for _ in proj_chain([0, 1, 2]):
            pass
        S_[:] = [ar.get(512) for _ in range(3)]
        P_[:] = S_
        PT_[:] = [ar.get(512) for _ in range(3)]
        a_free[:] = [[[], []] for _ in range(3)]
        st_.append(sml(12))
        ombufs, om_p, om_f = pair(1024)
        om_p = [v.rearrange("p (n t) -> p n t", n=4) for v in om_p]
        om_fv = om_f.rearrange("p (n t) -> p n t", n=4)
        OD = ar.get(1024)
        ODv = OD.v("p (n t) -> p n t", n=4)
        Qv = [q.v("p (n t) -> p n t", n=4) for q in Q]
        VMv, VDv = Q[2].v("p (b d) -> p b d", b=2), Q[5].v("p (b d) -> p b d", b=2)
        om_done, od_done = [], []

        def moba_unit(i, pr, blk):
            nk = 1 + blk
            r = attn_scores(i, [hrow(Qv[0][:, pr, :], h) for h in range(2)], [hrow(Qv[1][:, pr, :], h) for h in range(2)],
                            blk, nk, causal(nk), [t_q[0], t_q[1]])
            yield
            yield
            yield from attn_out(*r, nk, [(lambda j, h=2 * pr + h: VMv[:, j, 64 * h:64 * h + 64]) for h in range(2)],
                                [v[:, pr, 128 * blk:128 * blk + 128] for v in (*om_p, om_fv)], t_q[2], [ombufs[0].w, ombufs[1].w], om_done)

        def diff_unit(i, pr, blk):
            nk = 1 + blk
            while t_q[5] is None:
                yield
            _, pv, rc, t5, w = attn_scores(i, [hrow(Qv[3][:, pr, :], h) for h in range(2)], [hrow(Qv[4][:, pr, :], h) for h in range(2)],
                                           blk, nk, causal(nk), [t_q[3], t_q[4]])
            yield
            yield
            PT = PT_[i]
            t6 = ts(pv[:, 1, :], pv[:, 1, :], rc[:, 1:2], MUL, lam[:, 4:5], MUL, t5, t_lam)
            t6 = stt(pv[:, 0, :], pv[:, 0, :], rc[:, 0:1], pv[:, 1, :], MUL, ADD, t6)
            b = ps.take()
            t7 = pes([tr(b.ap[:, 128 * j:128 * j + 128], pv[:, 0, 128 * j:128 * j + 128], ident) for j in range(nk)], t6, b.w)
            t8 = acp(PT.ap[:, 0:w], b.ap[:, 0:w], t7, a_free[i][1], PT.w)
            b.w = [t8]
            yield
            b = ps.take()
            t9 = pes([mm(b.ap[:, 0:128], VDv[:, j, 128 * pr:128 * pr + 128], PT.ap[:, 128 * j:128 * j + 128], j == 0, j == nk - 1)
                      for j in range(nk)], t8, t_q[5], b.w)
            t10 = acp(ODv[:, pr, 128 * blk:128 * blk + 128], b.ap[:, 0:128], t9, OD.w)
            b.w = [t10]
            a_free[i] = [[t7, t6], [t9]]
            od_done.append(t10)
        units = [(f, pr, blk) for f in (moba_unit, diff_unit) for pr in range(4) for blk in range(2)]
        interleave(ps, (proj_chain([3, 4, 5, 6, 7, 8, 9]), [6, 7]), [(unit_chain(i, units[i::3]), [2 * i, 2 * i + 1], 0.9) for i in range(3)])
        t_od = od_done
        ar.free(now(), rt)
        ar.free(now(), *hbufs, *S_, *PT_, *Q)
        odbufs, od_p, od_f = pair(1024)
        od_p = [v.rearrange("p (n t) -> p n t", n=4) for v in od_p]
        od_fv = od_f.rearrange("p (n t) -> p n t", n=4)
        sq, rs = ar.get(1024), ar.get(512)
        g8 = sml(1)
        t8 = ts(g8, col("diff_subln_g_2"), 1.0 - LAM0, MUL, None, None, t_par)
        t = tt(sq.ap, OD.ap, OD.ap, MUL, t_od, sq.w)
        t_rs = head_rstd([sq.ap[:, 256 * i:256 * i + 256] for i in range(4)], [t, *rs.w], 128.0, 1e-6, rs.ap, 16, sel="hs2")
        t_g = [act(GM.ap[:, 1024 * i:1024 * i + 1024], GM.ap[:, 1024 * i:1024 * i + 1024], ACT.Sigmoid, SC.last()) for i in range(4)]
        mg = ar.get(2048)
        mgv = mg.v("p (k t) -> p k t", k=8)
        mgbufs, mg_p, mg_f = pair(2048)

        def merge(src, z, tk):
            for n in range(0, 8, 2):
                b = ps.take()
                if n % 4 == 0:
                    hw = take_half()
                for h in range(2):
                    t = pes(proj3(b.ap[:, 256 * h:256 * h + 256], hw.w, 128 * (n % 4 + h), src, 4), tk, hw.tok, b.w)
                bv = b.ap.rearrange("p (n t) -> p n t", n=2)
                gv = GMv[:, z + n:z + n + 2, :]
                if z == 0:
                    t_mg = tt(mgv[:, n:n + 2, :], bv, gv, MUL, t, t_g[n // 4], mg.w)
                    b.w = [t_mg]
                else:
                    t2 = tt(gv, bv, gv, MUL, t, t_g[2 + n // 4])
                    b.w = [t2]
                    t2 = tt(mgv[:, n:n + 2, :], mgv[:, n:n + 2, :], gv, ADD, t2)
                    cs = slice(256 * n, 256 * n + 512)
                    t_mg = split_act(mg.ap[:, cs], [v[:, cs] for v in mg_p], mg_f[:, cs], t2, mgbufs[0].w, mgbufs[1].w)
                if n % 4 == 2:
                    done_half(hw, t)
            return t_mg
        merge(om_p, 0, om_done)
        od_n = []
        for i in range(4):
            b = ps.take()
            t = pe(head_bcast(b, 0, i, rs.ap), t_rs, b.w)
            t = stt(ODv[:, i, :], ODv[:, i, :], g8, b.ap[:, 0:256], MUL, MUL, t, t8)
            b.w = [t]
            od_n.append(split_act(ODv[:, i, :], [v[:, i, :] for v in od_p], od_fv[:, i, :], t, odbufs[0].w, odbufs[1].w))
        t_mg = merge(od_p, 8, od_n)

        ar.free(now(), GM, OD, *ombufs, *odbufs, mg, sq, rs)
        slot7 = ar.get(4096)
        ring.aps[6], ring.lent[6] = slot7.ap, slot7.w
        gt = ar.get(512, True)

        def add_gated(gb):
            def f(c, h, bank, t):
                v = x[:, h, 512 * c:512 * c + 512]
                t = tt(gt.ap, bank, gb.ap[:, 512 * c:512 * c + 512], MUL, t, gt.w, VE.last() if cur["ve"] is VE else None)
                tt(v, v, gt.ap, ADD, t)
                return cur["ve"].last()
            return f
        junk, X2 = ar.get(1024), ar.get(2048, True)
        mg_p = [v.rearrange("p (k t) -> p k t", k=8) for v in mg_p]
        add_g = add_gated(g1b)
        t_xh = [None, None]
        bb = [ps.take(), ps.take()]
        for z in range(2):
            hw = take_half()
            t = pes(tokens3([b.ap[:, 256 * z:256 * z + 256] for b in bb], hw, mg_p), t_mg, hw.tok, bb[0].w, bb[1].w)
            done_half(hw, t)
        for h in range(2):
            bb[h].w = [add_g(0, h, bb[h].ap, t)]
        for c in (1,):
            hws = [take_half(), take_half()]
            for h in range(2):
                b = ps.take()
                t = pes([f for z in range(2) for f in tokens3([b.ap[:, 256 * z:256 * z + 256]], hws[z], mg_p, h)], t_mg, hws[0].tok, hws[1].tok, b.w)
                t_xh[h] = add_g(c, h, b.ap, t)
                b.w = [t_xh[h]]
            for hw in hws:
                done_half(hw, t)
        ring.lent[4] = ring.lent[5] = [t]
        ar.free(now(), *mgbufs, g1b)
        w36, b36 = ar.get(288), ar.get(36)
        w36v = w36.v("p (k n) -> p k n", k=8)
        later([*w36.w, *b36.w], [
            (w36v[:, :, 0:4], A["w_group_2"][0, :, :].rearrange("(k p) n -> p k n", p=128)),
            (w36v[:, :, 4:36], A["w_expert_2"][0, :, :].rearrange("(k p) n -> p k n", p=128)),
            (b36.ap[:, 0:4], bc(A["b_group_2"], [128, 4])), (b36.ap[:, 4:36], bc(A["b_expert_2"], [128, 32]))], s_rt)
        hT = ar.get(2048)
        t_h = features(x, t_xh, X2, hT, mods.ap[:, 8:16], shift=modc.ap[:, 16:24], dtok=t_md)
        hv = hT.v("p (k t) -> p k t", k=8)
        b = ps.take()
        t = pes([mm(b.ap[:, 36 * h:36 * h + 36], hv[:, k, 128 * h:128 * h + 128], w36v[:, k, :], k == 0, k == 7)
                 for h in range(2) for k in range(8)], t_h, (s_rt, 64), b.w)
        lg = ar.get(72)
        lgv = lg.v("p (b n) -> p b n", b=2)
        t_lg = tt(lgv, b.ap[:, 0:72].rearrange("p (b n) -> p b n", b=2), bc(b36.ap[:, 0:36].unsqueeze(1), [128, 2, 36]), ADD, t, lg.w)
        b.w = [t_lg]
        R = ar.get(640)
        ro = [0]

        def rget(n, pat="p (b n) -> p b n"):
            o = ro[0]
            ro[0] += 2 * n
            return R.ap[:, o:o + 2 * n].rearrange(pat, b=2)

        def chain(f, *w):
            return ve(f, VE.last(), *w)

        def first_max(src, n, key, dst, mx):
            kt_ = rget(n)
            chain(lambda e: e.tensor_reduce(mx, src, AX.X, MAX), t_lg, R.w)
            chain(lambda e: e.tensor_tensor(kt_, src, bc(mx, [128, 2, n]), EQ))
            chain(lambda e: e.tensor_tensor(kt_, kt_, bc(key.unsqueeze(1), [128, 2, n]), MUL))
            km = rget(1)
            chain(lambda e: e.tensor_reduce(km, kt_, AX.X, MAX))
            return chain(lambda e: e.tensor_tensor(dst, kt_, bc(km, [128, 2, n]), EQ))

        def softmax_parts(src, mx, n):
            nm, ee, zz = rget(1), rget(n), rget(1)
            t = chain(lambda e: e.tensor_scalar(nm, mx, -1.0, None, MUL))
            for i in range(2):
                t = act(ee[:, i, :], src[:, i, :], ACT.Exp, t, SC.last(), bias=nm[:, i, :], accum=zz[:, i, :])
            chain(lambda e: e.reciprocal(zz, zz), t)
            return ee, zz
        mxg, ohg = rget(1), rget(4)
        first_max(lgv[:, :, 0:4], 4, C["key4"], ohg, mxg)
        _, gw = softmax_parts(lgv[:, :, 0:4], mxg, 4)
        em = rget(32)
        of = rget(4)
        chain(lambda e: e.tensor_scalar(of, ohg, -1.0, -NEG, ADD, MUL))
        for i in range(2):
            v8 = em[:, i, :].rearrange("p (g n) -> p g n", g=4)
            chain(lambda e, i=i, v8=v8: e.tensor_tensor(v8, lgv[:, i, 4:36].rearrange("p (g n) -> p g n", g=4), bc(ohg[:, i, :].unsqueeze(2), [128, 4, 8]), MUL))
            chain(lambda e, i=i, v8=v8: e.tensor_tensor(v8, v8, bc(of[:, i, :].unsqueeze(2), [128, 4, 8]), ADD))
        mx1, oh1 = rget(1), rget(32)
        first_max(em, 32, C["key32"], oh1, mx1)
        ee, zz = softmax_parts(em, mx1, 32)
        chain(lambda e: e.tensor_tensor(ee, ee, bc(zz, [128, 2, 32]), MUL))
        chain(lambda e: e.scalar_tensor_tensor(out=em, in0=oh1, scalar=NEG, in1=em, op0=MUL, op1=ADD))
        mx2, oh2 = rget(1), rget(32)
        first_max(em, 32, C["key32"], oh2, mx2)
        RK = ar.get(192, True)
        Aa, Ww, rk = (RK.ap[:, 64 * i:64 * i + 64].rearrange("p (b n) -> p b n", b=2) for i in range(3))
        chain(lambda e: e.tensor_tensor(Aa, oh1, oh2, ADD), RK.w)
        chain(lambda e: e.tensor_tensor(Ww, Aa, ee, MUL))
        tot = rget(1)
        chain(lambda e: e.tensor_reduce(tot, Ww, AX.X, ADD))
        chain(lambda e: e.reciprocal(tot, tot))
        chain(lambda e: e.tensor_tensor(tot, tot, gw, MUL))
        t_ww = chain(lambda e: e.tensor_tensor(Ww, Ww, bc(tot, [128, 2, 32]), MUL))
        b = ps.take()
        t = pes([mm(b.ap[:, 0:32], C["SU"], Aa[:, 0, :], True, True), mm(b.ap[:, 32:64], ones, Aa[:, 0, :], True, False),
                 mm(b.ap[:, 32:64], C["SU"], Aa[:, 1, :], False, True), mm(b.ap[:, 64:96], ones, Aa[:, 0, :], True, False),
                 mm(b.ap[:, 64:96], ones, Aa[:, 1, :], False, True)], t_ww, b.w)
        cntf, cnti = sml(1), sml(1)
        chain(lambda e, b=b: e.tensor_reduce(cntf, b.ap[:, 64:96], AX.X, MAX), t)
        t_cnt = chain(lambda e: e.tensor_copy(cnti.bitcast(I32), cntf))
        chain(lambda e, b=b: e.scalar_tensor_tensor(out=rk, in0=b.ap[:, 0:64].rearrange("p (b n) -> p b n", b=2), scalar=1.0, in1=Aa, op0=ADD, op1=MUL))
        t_rk = chain(lambda e: e.tensor_scalar(rk, rk, -1.0, None, ADD))
        b.w = [t_rk]
        ar.free(now(), hT, w36, b36, lg, R, junk)
        xg = [ar.get(2048), ar.get(2048)]
        Pb, PwT = ar.get(2048), ar.get(2048)
        sgl, hh, hts, ost = ([ar.get(n) for _ in range(2)] for n in (256, 256, 128, 1024))
        g_ps = psum

        def moe_round(chs, start, first):
            Pv = Pb.v("p (b e s) -> p b e s", b=2, e=32)
            xgv = [g.v("p (k s) -> p k s", k=8) for g in xg]
            X2v = X2.v("p (b d) -> p b d", b=2)
            bw = {i: [] for i in range(8)}
            tk = start
            if not first:
                tk = ts(rk, rk, -float(NSLOT), ADD, None, None, tk)
            for i in range(2):
                tP = tt(Pv[:, i, :, :], bc(rk[:, i, :].unsqueeze(2), [128, 32, 32]), bc(C["iota"].unsqueeze(1), [128, 32, 32]), EQ,
                        tk, start, Pb.w)
            bi = [0]

            def nb():
                r = 4 + bi[0] % 4
                bi[0] += 1
                return r
            t_xg = [[] for _ in range(4)]
            xg_free = [[], []]

            def gather(qu, ks):
                for k in ks:
                    q = nb()
                    t = pes([mm(g_ps[q][:, 0:256], X2v[:, i, 128 * k:128 * k + 128], Pv[:, i, 8 * qu:8 * qu + 8, :].rearrange("p e s -> p (e s)"),
                                i == 0, i == 1) for i in range(2)], tP, start, bw[q])
                    o = xgv[qu % 2][:, k, :]
                    if k % 2:
                        t = ts(o, g_ps[q][:, 0:256], mods.ap[:, 8 + k:9 + k], MUL, modc.ap[:, 16 + k:17 + k], ADD, t, start, xg[qu % 2].w, xg_free[qu % 2])
                    else:
                        t = act(o, g_ps[q][:, 0:256], ACT.Identity, t, start, xg[qu % 2].w, xg_free[qu % 2],
                                scale=mods.ap[:, 8 + k:9 + k], bias=modc.ap[:, 16 + k:17 + k])
                    bw[q] = [t]
                    t_xg[qu].append(t)
            t_pw = []
            fre = {"sg": [[], []], "hh": [[], []], "ht": [[], []], "os": [[], []]}

            def weights():
                for i in range(2):
                    tw = tt(ost[i].v("p (e s) -> p e s", e=32), Pv[:, i, :, :], bc(Ww[:, i, :].unsqueeze(2), [128, 32, 32]), MUL, tP, ost[i].w)
                    for g4 in range(0, 8, 4):
                        q = nb()
                        t = pes([tr(g_ps[q][:, 128 * z:128 * z + 128], ost[i].ap[:, 128 * (g4 + z):128 * (g4 + z) + 128], ident) for z in range(4)], tw, bw[q])
                        fre["os"][i] = [t]
                        t = acp(PwT.v("p (g t) -> p g t", g=8)[:, g4:g4 + 4, 128 * i:128 * i + 128],
                                g_ps[q][:, :].rearrange("p (g t) -> p g t", g=4), t, PwT.w, start)
                        bw[q] = [t]
                        t_pw.append(t)
            PwTv = PwT.v("p (g t) -> p g t", g=8)
            t_gu, t_hh, t_ost = {}, {}, {}

            def gate_up(e):
                q = 4 + e % 2
                cg, cu = chs[e][0], chs[e][1]
                wg = cg.ap.rearrange("p (k n) -> p k n", k=8)
                wu = cu.ap.rearrange("p (k n) -> p k n", k=8)
                fns = []
                for k in range(8):
                    for j in range(4):
                        w = (wg if j < 2 else wu)[:, k, 256 * (j % 2):256 * (j % 2) + 256]
                        fns.append(mm(g_ps[q][32 * j:32 * j + 32, 0:256], xgv[e // 8 % 2][:, k, 32 * (e % 8):32 * (e % 8) + 32], w, k == 0, k == 7))
                t = pes(fns, t_xg[e // 8], cg.tok, cu.tok, bw[q])
                cg.free = cu.free = [t]
                xg_free[e // 8 % 2] = [t]
                i = e % 2
                t1 = act(sgl[i].ap[0:64, :], g_ps[q][0:64, 0:256], ACT.Silu, t, sgl[i].w, fre["sg"][i])
                t2 = tt(hh[i].ap[0:64, :], g_ps[q][64:128, 0:256], sgl[i].ap[0:64, :], MUL, t1, hh[i].w, fre["hh"][i])
                bw[q] = [t2]
                fre["sg"][i] = [t2]
                t_hh[e] = t2

            def down(e):
                i = e % 2
                t = pes([tr(g_ps[6][:, 64 * c:64 * c + 64], hh[i].ap[0:64, 128 * c:128 * c + 128], ident[0:64, 0:64]) for c in range(2)],
                        t_hh[e], bw[6])
                fre["hh"][i] = [t]
                t = acp(hts[i].ap, g_ps[6][:, 0:128], t, hts[i].w, fre["ht"][i])
                bw[6] = [t]
                cd = chs[e][2]
                wd = cd.ap.rearrange("p (k n) -> p k n", k=4)
                fns = []
                for f in range(4):
                    o = 64 * (f % 2) + 32 * (f // 2)
                    for j in range(4):
                        fns.append(mm(g_ps[7][32 * j:32 * j + 32, 0:256], hts[i].ap[:, o:o + 32], wd[:, f, 256 * j:256 * j + 256], f == 0, f == 3))
                t = pes(fns, t, cd.tok, bw[7])
                cd.free = [t]
                fre["ht"][i] = [t]
                g, r = e // 4, 32 * (e % 4)
                o = ost[g % 2]
                tw = []
                for j in range(4):
                    d, s_ = o.ap[r:r + 32, 256 * j:256 * j + 256], g_ps[7][32 * j:32 * j + 32, 0:256]
                    tw.append((acp if j % 2 else vcp)(d, s_, t, o.w, fre["os"][g % 2]))
                bw[7] = tw
                t_ost.setdefault(g, []).extend(tw)

            def combine(g):
                t = pes([mm(g_ps[2 * b_ + h_][:, :], PwTv[:, g, 128 * b_:128 * b_ + 128], ost[g % 2].ap[:, 512 * h_:512 * h_ + 512], g == 0, g == 7)
                         for b_ in range(2) for h_ in range(2)], t_ost[g], t_pw, start)
                fre["os"][g % 2] = [t]
                return t
            gather(0, range(8))
            gate_up(0)
            for e in range(NE):
                if e + 1 < NE:
                    gate_up(e + 1)
                if e == 0:
                    weights()
                if e < 24 and e % 8 in (2, 3, 4, 5):
                    gather(e // 8 + 1, range(2 * (e % 8) - 4, 2 * (e % 8) - 2))
                if e % 4 == 1 and e > 4:
                    combine(e // 4 - 1)
                down(e)
            t = combine(7)
            for h_ in range(2):
                for b_ in range(2):
                    v = x[:, b_, 512 * h_:512 * h_ + 512]
                    t1 = tt(gt.ap, g_ps[2 * b_ + h_][:, :], g2b.ap[:, 512 * h_:512 * h_ + 512], MUL, t, gt.w, cur["ve"].last())
                    t1 = tt(v, v, gt.ap, ADD, t1)
            return t1
        t_x = moe_round(ch_e, [*now(), t_rk], True)
        main_end = now()
        LP = {"pe": Lane(sem("l_pe")), "ve": Lane(sem("l_ve")), "sc": Lane(sem("l_sc")), "gp": Lane(sem("l_gp"))}
        ring2 = Ring(slots, [sem(f"l_ring{i}") for i in range(NS)])
        cur.update(LP)
        for bf in (Pb, PwT, *xg, *sgl, *hh, *hts, *ost, gt):
            bf.w = []
        ch_e2 = [load_expert(ring2, e) for e in range(NE)]
        moe_round(ch_e2, [], False)
        FN = {"pe": Lane(sem("f_pe")), "ve": Lane(sem("f_ve")), "sc": Lane(sem("f_sc")), "gp": Lane(sem("f_gp"))}
        cur.update(FN)
        s, r = sml(2), sml(2)
        for i in range(2):
            t1 = act(xg[0].ap[:, 1024 * i:1024 * i + 1024], x[:, i, :], ACT.Square, accum=s[:, i:i + 1])
        t2 = ts(r, s, 1.0 / 1024, MUL, 1e-6, ADD, t1)
        t3 = ve(lambda e: e.reciprocal(s, r), t2)
        t3 = act(r, s, ACT.Sqrt, t3)
        for i in range(2):
            t_fin = stt(x[:, i, :], x[:, i, :], r[:, i:i + 1], Pb.ap[:, 0:1024], MUL, MUL, t3, (s_fg, 16))
        block = ctx.enter_context(nc.Block())


        def rounds(eng, body, me):
            n = eng.value_load(cnti[0:1, 0:1].bitcast(mybir.dt.int32), min_val=0, max_val=256)
            with eng.If(n > NSLOT):
                with eng.Fori(NSLOT, n, NSLOT):
                    body(eng)
                    if me is None:
                        for k in ("pe", "ve", "sc"):
                            eng.wait_ge(*LP[k].last())
                        eng.wait_ge(s_done2, 3)
                        for k in ("pe", "ve", "sc"):
                            eng.sem_clear(LP[k].sem)
                        for q in ring2.sems:
                            eng.sem_clear(q)
                        eng.sem_clear(s_done2)
                        for q in s_go[0:3]:
                            eng.sem_inc(q, 1)
                    else:
                        eng.sem_inc(s_done2, 1)
                        eng.wait_ge(s_go[me], 1)
                        eng.sem_clear(s_go[me])

        @block.sync
        def _(e):
            load_x(e)
            e.wait_ge(*par1_tok)
            ring.play(e)
            for w in main_end:
                e.wait_ge(*w)
            rounds(e, ring2.play, None)
            e.dma_start(Pb.ap[:, 0:1024], A["final_g_2"].rearrange("(a d) -> a d", a=1).to_broadcast([128, 1024])).then_inc(s_fg, 16)
            e.wait_ge(*t_fin)
            e.dma_start(out.rearrange("a (b p) d -> p (a b) d", p=128), x).then_inc(s_out, 16)
            e.wait_ge(s_out, 16)

        def compute(e, lane, k, me):
            lane.play(e)
            for w in main_end:
                e.wait_ge(*w)
            rounds(e, LP[k].play, me)
            FN[k].play(e)

        @block.scalar
        def _(e):
            load_first(e)
            compute(e, SC, "sc", 0)

        @block.vector
        def _(e):
            compute(e, VE, "ve", 1)

        @block.gpsimd
        def _(e):
            pdma(e, plist2, s_par2)
            GP.play(e)

        @block.tensor
        def _(e):
            compute(e, PE, "pe", 2)


_INS = ["x", "mem", "rel_bias", "mix_norm_g", "w_in", "attn_q_norm", "attn_k_norm", "attn_sinks", "rwkv_mu", "rwkv_w0",
        "rwkv_w2", "rwkv_a0", "rwkv_a2", "rwkv_g2", "rwkv_k_k", "rwkv_k_a", "rwkv_r_k", "rwkv_ln_w", "rwkv_ln_b",
        "mem_norm_g", "w_mem_kv", "mem_q_norm", "mem_k_norm", "w_out", "ffn_norm_g", "w_up", "conv_w", "conv_b", "w_down",
        "c_2", "w_ada_2", "b_ada_2", "norm1_g_2", "w_in_2", "lambda_q1_2", "lambda_k1_2", "lambda_q2_2", "lambda_k2_2",
        "diff_subln_g_2", "w_proj_moba_2", "w_proj_diff_2", "w_out_2", "norm2_g_2", "w_group_2", "b_group_2", "w_expert_2",
        "b_expert_2", "w_gate_2", "w_up_2", "w_down_2", "final_g_2"]


def kernel(**inputs):
    import concourse.bacc as bacc
    from concourse.bass_utils import run_bass_kernel_spmd

    nc = bacc.Bacc("TRN2", target_bir_lowering=False, num_devices=1)
    arrays, aps = {}, {}
    named = [(n, np.ascontiguousarray(inputs[n])) for n in _INS] + [("consts", const_table())]
    for name, a in named:
        arrays[f"in_{name}"] = a
        aps[name] = nc.dram_tensor(f"in_{name}", a.shape, mybir.dt.from_np(a.dtype), kind="ExternalInput").ap()
    out = nc.dram_tensor("out_0", (1, T, D), mybir.dt.float32, kind="ExternalOutput").ap()
    block_kernel(nc, aps, out)
    r = run_bass_kernel_spmd(nc, [arrays], core_ids=[0])
    return r.results[0]["out_0"]
```
